# Optimizing a Trainium2 kernel written in Bass

```python
import math
import jax, jax.numpy as jnp
from jax import lax
import numpy as np

D_MODEL = 1024
BATCH = 1
SEQ = 256
DEPTH = 1

HEAD_DIM = 64
BLOCK_Q = 128
N_SB_HEADS = 4
DIL_PATTERNS = ((128, 1), (512, 4), (2048, 16))
N_DIL_GROUPS = len(DIL_PATTERNS)
N_DIL_HEADS = 4
N_FOX_HEADS = 4
N_DIFF_HEADS = 4
DIFF_QK_DIM = HEAD_DIM // 2
N_BRANCH = 4
BRANCH_WIDTH = 4 * HEAD_DIM
D_FF = 4 * D_MODEL
RMS_EPS = 1e-6
N_ALIBI = N_DIL_GROUPS * N_DIL_HEADS + N_DIFF_HEADS

SB_W = N_SB_HEADS * HEAD_DIM
DIL_W = N_DIL_GROUPS * N_DIL_HEADS * HEAD_DIM
FOX_W = N_FOX_HEADS * HEAD_DIM
DIFF_QK_W = N_DIFF_HEADS * 2 * DIFF_QK_DIM
DIFF_V_W = N_DIFF_HEADS * HEAD_DIM
GATE_W = N_BRANCH * D_MODEL
SPLIT_SIZES = (SB_W,) * 3 + (DIL_W,) * 3 + (FOX_W,) * 3 + (N_FOX_HEADS,) + (DIFF_QK_W, DIFF_QK_W, DIFF_V_W) + (GATE_W,)
D_IN = sum(SPLIT_SIZES)
SPLIT_OFFSETS = tuple(sum(SPLIT_SIZES[:i + 1]) for i in range(len(SPLIT_SIZES) - 1))


def rms_norm(x, g):
    xf = x.astype(jnp.float32)
    y = xf * lax.rsqrt(jnp.mean(xf * xf, axis=-1, keepdims=True) + RMS_EPS)
    return (y * g.astype(jnp.float32)).astype(x.dtype)

def alibi_slopes():
    return jnp.asarray(2.0 ** (-8.0 * np.arange(1, N_ALIBI + 1) / N_ALIBI), dtype=jnp.float32)

def _stick_breaking(q_blk, k, v, dist):
    z = jnp.einsum('bqhd,bshd->bhqs', q_blk, k).astype(jnp.float32) * (HEAD_DIM ** -0.5)
    strict = dist > 0
    log_keep = jnp.where(strict, jax.nn.log_sigmoid(-z), 0.0)
    log_between = lax.cumsum(log_keep, axis=3, reverse=True) - log_keep
    a = jnp.where(strict, jnp.exp(jax.nn.log_sigmoid(z) + log_between), 0.0)
    return jnp.einsum('bhqs,bshd->bqhd', a.astype(v.dtype), v)

def _dilated(q_blk, k, v, t_idx, slopes):
    outs, lses = [], []
    for g, (window, dil) in enumerate(DIL_PATTERNS):
        dists = dil * jnp.arange(window // dil + 1)
        idx = t_idx[:, None] - dists[None, :]
        valid = idx >= 0
        idx = jnp.maximum(idx, 0)
        kg = jnp.take(k[:, :, g], idx, axis=1)
        vg = jnp.take(v[:, :, g], idx, axis=1)
        s = jnp.einsum('bqhd,bqnhd->bhqn', q_blk[:, :, g], kg).astype(jnp.float32) * (HEAD_DIM ** -0.5)
        s = s - slopes[g][:, None, None] * dists.astype(jnp.float32)
        s = jnp.where(valid, s, -jnp.inf)
        lse = jax.nn.logsumexp(s, axis=-1)
        p = jnp.exp(s - lse[..., None])
        outs.append(jnp.einsum('bhqn,bqnhd->bqhd', p.astype(v.dtype), vg))
        lses.append(lse)
    alpha = jax.nn.softmax(jnp.stack(lses, axis=0), axis=0)
    alpha = jnp.transpose(alpha, (0, 1, 3, 2))[..., None]
    return jnp.sum(alpha.astype(v.dtype) * jnp.stack(outs, axis=0), axis=0)

def _forgetting(q_blk, k, v, cum_blk, cum, dist):
    s = jnp.einsum('bqhd,bshd->bhqs', q_blk, k).astype(jnp.float32) * (HEAD_DIM ** -0.5)
    s = s + jnp.transpose(cum_blk, (0, 2, 1))[..., None] - jnp.transpose(cum, (0, 2, 1))[:, :, None, :]
    p = jax.nn.softmax(jnp.where(dist >= 0, s, -jnp.inf), axis=-1)
    return jnp.einsum('bhqs,bshd->bqhd', p.astype(v.dtype), v)

def _differential(q_blk, k, v, dist, slopes, lam):
    s = jnp.einsum('bqhcd,bshcd->bchqs', q_blk, k).astype(jnp.float32) * (DIFF_QK_DIM ** -0.5)
    s = s - slopes[:, None, None] * dist.astype(jnp.float32)
    p = jax.nn.softmax(jnp.where(dist >= 0, s, -jnp.inf), axis=-1)
    w = p[:, 0] - lam * p[:, 1]
    return jnp.einsum('bhqs,bshd->bqhd', w.astype(v.dtype), v)

def _token_mixers(h, w_in, b_forget, lam, diff_g, diff_out_scale, slopes_dil, slopes_diff):
    bsz, seq, _ = h.shape
    proj = h @ w_in
    (qa, ka, va, qb, kb, vb, qc, kc, vc, f_logit, qd, kd, vd, gate_logit) = jnp.split(proj, SPLIT_OFFSETS, axis=-1)
    qa, ka, va = (a.reshape(bsz, seq, N_SB_HEADS, HEAD_DIM) for a in (qa, ka, va))
    qb, kb, vb = (a.reshape(bsz, seq, N_DIL_GROUPS, N_DIL_HEADS, HEAD_DIM) for a in (qb, kb, vb))
    qc, kc, vc = (a.reshape(bsz, seq, N_FOX_HEADS, HEAD_DIM) for a in (qc, kc, vc))
    qd, kd = (a.reshape(bsz, seq, N_DIFF_HEADS, 2, DIFF_QK_DIM) for a in (qd, kd))
    vd = vd.reshape(bsz, seq, N_DIFF_HEADS, HEAD_DIM)
    log_f = jax.nn.log_sigmoid(f_logit.astype(jnp.float32) + b_forget.astype(jnp.float32))
    cum = jnp.cumsum(log_f, axis=1)
    s_idx = jnp.arange(seq)

    def block(q0):
        t_idx = q0 + jnp.arange(BLOCK_Q)
        dist = t_idx[:, None] - s_idx[None, :]
        sl = lambda a: lax.dynamic_slice_in_dim(a, q0, BLOCK_Q, axis=1)
        return (_stick_breaking(sl(qa), ka, va, dist),
                _dilated(sl(qb), kb, vb, t_idx, slopes_dil),
                _forgetting(sl(qc), kc, vc, sl(cum), cum, dist),
                _differential(sl(qd), kd, vd, dist, slopes_diff, lam))

    o_a, o_b, o_c, o_d = lax.map(block, jnp.arange(seq // BLOCK_Q) * BLOCK_Q)
    unblock = lambda o: jnp.moveaxis(o, 0, 1).reshape(bsz, seq, o.shape[3], o.shape[4])
    o_d = rms_norm(unblock(o_d), diff_g) * diff_out_scale
    ys = jnp.stack([unblock(o_a), unblock(o_b), unblock(o_c), o_d], axis=2)
    return ys.reshape(bsz, seq, N_BRANCH, BRANCH_WIDTH), gate_logit

def first_inputs(seed: int = 0) -> dict:
    key = jax.random.key(seed)
    ks = jax.random.split(key, 16)
    nrm = lambda k, shape, scale: jax.random.normal(k, shape, jnp.float32) * scale
    return {
        'x': nrm(ks[0], (BATCH, SEQ, D_MODEL), 1.0),
        'mix_norm_g': 1.0 + nrm(ks[1], (DEPTH, D_MODEL), 0.05),
        'w_in': nrm(ks[2], (DEPTH, D_MODEL, D_IN), D_MODEL ** -0.5),
        'b_forget': jax.random.uniform(ks[3], (DEPTH, N_FOX_HEADS), jnp.float32, 1.0, 4.0),
        'lambda_q1': nrm(ks[4], (DEPTH, DIFF_QK_DIM), 0.1),
        'lambda_k1': nrm(ks[5], (DEPTH, DIFF_QK_DIM), 0.1),
        'lambda_q2': nrm(ks[6], (DEPTH, DIFF_QK_DIM), 0.1),
        'lambda_k2': nrm(ks[7], (DEPTH, DIFF_QK_DIM), 0.1),
        'diff_norm_g': 1.0 + nrm(ks[8], (DEPTH, HEAD_DIM), 0.05),
        'w_branch': nrm(ks[9], (DEPTH, N_BRANCH, BRANCH_WIDTH, D_MODEL), BRANCH_WIDTH ** -0.5),
        'w_out': nrm(ks[10], (DEPTH, D_MODEL, D_MODEL), D_MODEL ** -0.5),
        'mlp_norm_g': 1.0 + nrm(ks[11], (DEPTH, D_MODEL), 0.05),
        'w_up': nrm(ks[12], (DEPTH, D_MODEL, D_FF), D_MODEL ** -0.5),
        'w_down': nrm(ks[13], (DEPTH, D_FF, D_MODEL), D_FF ** -0.5),
        'final_norm_g': 1.0 + nrm(ks[14], (D_MODEL,), 0.05),
    }

def first_block(x, mix_norm_g, w_in, b_forget, lambda_q1, lambda_k1, lambda_q2, lambda_k2, diff_norm_g, w_branch, w_out, mlp_norm_g, w_up, w_down, final_norm_g):
    bsz, seq, _ = x.shape
    slopes = alibi_slopes()
    n0, n1 = N_DIL_HEADS, N_DIL_HEADS + N_DIFF_HEADS
    slopes_dil = jnp.stack([slopes[:n0], slopes[n1:n1 + N_DIL_HEADS], slopes[n1 + N_DIL_HEADS:]], axis=0)
    slopes_diff = slopes[n0:n1]
    for l in range(DEPTH):
        lambda_init = 0.8 - 0.6 * math.exp(-0.3 * l)
        lam = (jnp.exp(jnp.sum(lambda_q1[l].astype(jnp.float32) * lambda_k1[l].astype(jnp.float32)))
               - jnp.exp(jnp.sum(lambda_q2[l].astype(jnp.float32) * lambda_k2[l].astype(jnp.float32))) + lambda_init)
        h = rms_norm(x, mix_norm_g[l])
        ys, gate_logit = _token_mixers(h, w_in[l], b_forget[l], lam, diff_norm_g[l], 1.0 - lambda_init, slopes_dil, slopes_diff)
        branch = jnp.einsum('bsnc,ncd->bsnd', ys, w_branch[l])
        gates = jax.nn.sigmoid(gate_logit.reshape(bsz, seq, N_BRANCH, D_MODEL))
        x = x + jnp.sum(gates * branch, axis=2) @ w_out[l]
        h = rms_norm(x, mlp_norm_g[l])
        x = x + jnp.square(jax.nn.relu(h @ w_up[l])) @ w_down[l]
    return rms_norm(x, final_norm_g)


D_MIX = D_MODEL
ATTN_WIDTH = D_MIX // 2
CONV_WIDTH = D_MIX - ATTN_WIDTH
N_HEADS = 8
HEAD_DIM_2 = ATTN_WIDTH // N_HEADS
CONV_KERNEL = 31
MOBA_BLOCK = 256
MOBA_TOPK = 3
Q_CHUNK = 64
ROPE_THETA = 10000.0
D_FF_2 = -(-8 * D_MODEL // (3 * 256)) * 256
EPS = 1e-6
D_IN_2 = 3 * ATTN_WIDTH + 2 * CONV_WIDTH


def rms_norm_2(x, g):
    xf = x.astype(jnp.float32)
    y = xf * lax.rsqrt(jnp.mean(xf * xf, axis=-1, keepdims=True) + EPS)
    return (y * g.astype(jnp.float32)).astype(x.dtype)

def layer_norm(x, g, b):
    xf = x.astype(jnp.float32)
    mu = jnp.mean(xf, axis=-1, keepdims=True)
    var = jnp.mean(jnp.square(xf - mu), axis=-1, keepdims=True)
    y = (xf - mu) * lax.rsqrt(var + EPS)
    return (y * g.astype(jnp.float32) + b.astype(jnp.float32)).astype(x.dtype)

def rope_tables(seq_len):
    pos = jnp.arange(seq_len, dtype=jnp.float32)
    inv_freq = ROPE_THETA ** (-jnp.arange(0, HEAD_DIM_2, 2, dtype=jnp.float32) / HEAD_DIM_2)
    ang = pos[:, None] * inv_freq[None, :]
    ang = jnp.concatenate([ang, ang], axis=-1)
    return jnp.cos(ang)[:, None, :], jnp.sin(ang)[:, None, :]

def apply_rope(x, cos, sin):
    xf = x.astype(jnp.float32)
    x1, x2 = jnp.split(xf, 2, axis=-1)
    rot = jnp.concatenate([-x2, x1], axis=-1)
    return (xf * cos + rot * sin).astype(x.dtype)

def moba_attention(q, k, v):
    B, H, S, Dh = q.shape
    n_blocks = -(-S // MOBA_BLOCK)
    pad = n_blocks * MOBA_BLOCK - S
    kp = jnp.pad(k, ((0, 0), (0, 0), (0, pad), (0, 0)))
    vp = jnp.pad(v, ((0, 0), (0, 0), (0, pad), (0, 0)))
    kb = kp.reshape(B, H, n_blocks, MOBA_BLOCK, Dh)
    vb = vp.reshape(B, H, n_blocks, MOBA_BLOCK, Dh)
    k_mean = jnp.mean(kb.astype(jnp.float32), axis=3)
    topk = min(MOBA_TOPK, n_blocks)
    scale = HEAD_DIM_2 ** -0.5
    b_idx = jnp.arange(B)[:, None, None, None]
    h_idx = jnp.arange(H)[None, :, None, None]
    key_off = jnp.arange(MOBA_BLOCK)
    block_ids = jnp.arange(n_blocks)
    n_chunks = S // Q_CHUNK

    def chunk_fn(c):
        start = c * Q_CHUNK
        qc = lax.dynamic_slice_in_dim(q, start, Q_CHUNK, axis=2)
        q_pos = start + jnp.arange(Q_CHUNK)
        own = start // MOBA_BLOCK
        gate = jnp.einsum('bhqd,bhnd->bhqn', qc.astype(jnp.float32), k_mean)
        gate = jnp.where((block_ids < own)[None, None, None, :], gate, -jnp.inf)
        _, top_idx = lax.top_k(gate, topk)
        sel_valid = top_idx < own
        k_sel = kb[b_idx, h_idx, top_idx]
        v_sel = vb[b_idx, h_idx, top_idx]
        s_sel = jnp.einsum('bhqd,bhqnkd->bhqnk', qc, k_sel).astype(jnp.float32) * scale
        s_sel = jnp.where(sel_valid[..., None], s_sel, -jnp.inf)
        s_sel = s_sel.reshape(B, H, Q_CHUNK, topk * MOBA_BLOCK)
        k_own = lax.dynamic_slice_in_dim(kp, own * MOBA_BLOCK, MOBA_BLOCK, axis=2)
        v_own = lax.dynamic_slice_in_dim(vp, own * MOBA_BLOCK, MOBA_BLOCK, axis=2)
        s_own = jnp.einsum('bhqd,bhkd->bhqk', qc, k_own).astype(jnp.float32) * scale
        own_pos = own * MOBA_BLOCK + key_off
        s_own = jnp.where((own_pos[None, :] <= q_pos[:, None])[None, None], s_own, -jnp.inf)
        p = jax.nn.softmax(jnp.concatenate([s_own, s_sel], axis=-1), axis=-1)
        p_own = p[..., :MOBA_BLOCK].astype(v.dtype)
        p_sel = p[..., MOBA_BLOCK:].reshape(B, H, Q_CHUNK, topk, MOBA_BLOCK).astype(v.dtype)
        out = (jnp.einsum('bhqk,bhkd->bhqd', p_own, v_own)
               + jnp.einsum('bhqnk,bhqnkd->bhqd', p_sel, v_sel))
        return out

    outs = lax.map(chunk_fn, jnp.arange(n_chunks))
    return outs.transpose(1, 2, 0, 3, 4).reshape(B, H, S, Dh)

def conformer_conv(u, glu_b, dw_w, dw_b, ln_g, ln_b):
    u = u + glu_b.astype(u.dtype)
    a, g = jnp.split(u, 2, axis=-1)
    h = a * jax.nn.sigmoid(g)
    h = jnp.pad(h, ((0, 0), (CONV_KERNEL - 1, 0), (0, 0)))
    h = lax.conv_general_dilated(
        h, dw_w[:, None, :].astype(h.dtype), window_strides=(1,), padding='VALID',
        dimension_numbers=('NWC', 'WIO', 'NWC'), feature_group_count=CONV_WIDTH)
    h = h + dw_b.astype(h.dtype)
    h = layer_norm(h, ln_g, ln_b)
    return jax.nn.silu(h)

def second_inputs(seed: int = 0) -> dict:
    key = jax.random.key(seed)
    ks = jax.random.split(key, 16)
    f32 = jnp.float32
    L = DEPTH

    def nrm(k, shape, scale):
        return jax.random.normal(k, shape, f32) * scale

    return {
        "x": jax.random.normal(ks[0], (BATCH, SEQ, D_MODEL), f32),
        "norm1_g": 1.0 + nrm(ks[1], (L, D_MODEL), 0.02),
        "w_in": nrm(ks[2], (L, D_MODEL, D_IN_2), D_MODEL ** -0.5),
        "glu_b": nrm(ks[3], (L, 2 * CONV_WIDTH), 0.02),
        "q_norm_g": 1.0 + nrm(ks[4], (L, HEAD_DIM_2), 0.02),
        "k_norm_g": 1.0 + nrm(ks[5], (L, HEAD_DIM_2), 0.02),
        "dw_w": nrm(ks[6], (L, CONV_KERNEL, CONV_WIDTH), CONV_KERNEL ** -0.5),
        "dw_b": nrm(ks[7], (L, CONV_WIDTH), 0.02),
        "conv_ln_g": 1.0 + nrm(ks[8], (L, CONV_WIDTH), 0.02),
        "conv_ln_b": nrm(ks[9], (L, CONV_WIDTH), 0.02),
        "w_out": nrm(ks[10], (L, D_MIX, D_MODEL), D_MIX ** -0.5),
        "norm2_g": 1.0 + nrm(ks[11], (L, D_MODEL), 0.02),
        "w_gate": nrm(ks[12], (L, D_MODEL, D_FF_2), D_MODEL ** -0.5),
        "w_up": nrm(ks[13], (L, D_MODEL, D_FF_2), D_MODEL ** -0.5),
        "w_down": nrm(ks[14], (L, D_FF_2, D_MODEL), D_FF_2 ** -0.5),
    }

def second_block(x, norm1_g, w_in, glu_b, q_norm_g, k_norm_g, dw_w, dw_b, conv_ln_g,
              conv_ln_b, w_out, norm2_g, w_gate, w_up, w_down):
    B, S, _ = x.shape
    cos, sin = rope_tables(S)
    for l in range(DEPTH):
        h = rms_norm_2(x, norm1_g[l])
        proj = h @ w_in[l]
        q, k, v, u = jnp.split(proj, [ATTN_WIDTH, 2 * ATTN_WIDTH, 3 * ATTN_WIDTH], axis=-1)
        q = q.reshape(B, S, N_HEADS, HEAD_DIM_2)
        k = k.reshape(B, S, N_HEADS, HEAD_DIM_2)
        v = v.reshape(B, S, N_HEADS, HEAD_DIM_2)
        q = apply_rope(rms_norm_2(q, q_norm_g[l]), cos, sin)
        k = apply_rope(rms_norm_2(k, k_norm_g[l]), cos, sin)
        attn = moba_attention(q.transpose(0, 2, 1, 3), k.transpose(0, 2, 1, 3),
                              v.transpose(0, 2, 1, 3))
        attn = attn.transpose(0, 2, 1, 3).reshape(B, S, ATTN_WIDTH)
        conv = conformer_conv(u, glu_b[l], dw_w[l], dw_b[l], conv_ln_g[l], conv_ln_b[l])
        x = x + jnp.concatenate([attn, conv], axis=-1) @ w_out[l]
        h = rms_norm_2(x, norm2_g[l])
        x = x + (jax.nn.silu(h @ w_gate[l]) * (h @ w_up[l])) @ w_down[l]
    return x


def setup_inputs(seed=0):
    out = dict(first_inputs(seed))
    for name, value in second_inputs(seed + 1).items():
        if name != "x":
            out[name + "_2"] = value
    return out


def reference(
    x, mix_norm_g, w_in, b_forget, lambda_q1, lambda_k1, lambda_q2, lambda_k2, diff_norm_g,
    w_branch, w_out, mlp_norm_g, w_up, w_down, final_norm_g, norm1_g_2, w_in_2, glu_b_2,
    q_norm_g_2, k_norm_g_2, dw_w_2, dw_b_2, conv_ln_g_2, conv_ln_b_2, w_out_2, norm2_g_2,
    w_gate_2, w_up_2, w_down_2,
):
    x = first_block(
        x, mix_norm_g, w_in, b_forget, lambda_q1, lambda_k1, lambda_q2, lambda_k2, diff_norm_g,
        w_branch, w_out, mlp_norm_g, w_up, w_down, final_norm_g,
    )
    return second_block(
        x, norm1_g_2, w_in_2, glu_b_2, q_norm_g_2, k_norm_g_2, dw_w_2, dw_b_2, conv_ln_g_2,
        conv_ln_b_2, w_out_2, norm2_g_2, w_gate_2, w_up_2, w_down_2,
    )


_drawn_inputs = setup_inputs


def setup_inputs(seed=0):
    import zlib

    import numpy as np

    out = dict(_drawn_inputs(seed))
    spreads = {}
    factors = {'lambda_k1': 2.991,
     'lambda_q2': 5.798,
     'lambda_k2': 5.549,
     'norm1_g_2': 5.032,
     'glu_b_2': 5.659,
     'q_norm_g_2': 8.0,
     'k_norm_g_2': 8.0,
     'dw_b_2': 10.284,
     'conv_ln_g_2': 18.052,
     'conv_ln_b_2': 20.333,
     'norm2_g_2': 3.906}
    for name, (base, spread) in spreads.items():
        noise = np.random.default_rng([zlib.crc32(name.encode()), seed]).standard_normal(out[name].shape)
        drawn = base * np.exp(spread * noise) if base else spread * noise
        out[name] = __import__('jax').numpy.asarray(drawn.astype(out[name].dtype))
    for name, factor in factors.items():
        out[name] = (out[name] * factor).astype(out[name].dtype)
    return out
```

```python
import concourse.bass as bass
from concourse import mybir
from contextlib import ExitStack

F32 = mybir.dt.float32
F32R = mybir.dt.float32r
ALU = mybir.AluOpType
ACT = mybir.ActivationFunctionType
AX = mybir.AxisListType

D = 1024
S = 256
EPS = 1e-6
DFF1 = 4096
DFF2 = 2816
NRAW = 4
NSPL = 3
LEAD = 2
NEG = -1e30

SLOPES = [2.0 ** (-8.0 * i / 16) for i in range(1, 17)]
SL_DIL = [SLOPES[0:4], SLOPES[8:12], SLOPES[12:16]]
SL_DIFF = SLOPES[4:8]

PAR = {}
CST = {}


def _layout():
    n = 0
    for name, w in (("g_mix", 8), ("g_mlp", 8), ("g_fin", 8), ("g_n1", 8), ("g_n2", 8), ("glu_b", 8),
                    ("dw_w", 124), ("dw_b", 4), ("ln_g", 4), ("ln_b", 4), ("b_f", 4), ("lam", 128),
                    ("g_diff", 64)):
        PAR[name] = (n, w)
        n += w
    PAR["_n"] = n
    n = 0
    for name, w in (("ident", 128), ("maskF", 256)):
        CST[name] = (n, w)
        n += w
    CST["_n0"] = n
    n = 0
    for name, w in (("DD", 1536), ("MB", 384), ("UO", 256), ("LG", 128)):
        CST[name] = (n, w)
        n += w
    CST["_n1"] = n
    return


_layout()


class Queue:

    def __init__(self, sem):
        self.sem = sem
        self.n = 0
        self.items = []

    def put(self, fn, *waits, sig=True):
        flat = []
        todo = list(waits)
        while todo:
            w = todo.pop(0)
            if isinstance(w, list):
                todo = w + todo
            elif w is not None:
                flat.append(w)
        if sig:
            self.n += 1
        self.items.append((fn, flat, sig))
        return (self.sem, self.n)

    def play(self, eng):
        seen = {}
        for fn, waits, sig in self.items:
            for sem, v in waits:
                if seen.get(sem, 0) < v:
                    eng.wait_ge(sem, v)
                    seen[sem] = v
            ins = fn(eng)
            if sig:
                ins.then_inc(self.sem, 1)


def program(nc, x_d, w_in, w_br, w_out, w_up, w_dn, w_in2, w_out2, w_g2, w_u2, w_d2, par_d, par2_d, cst_d, out_d):
    with ExitStack() as ctx:
        build(nc, ctx, x_d, w_in, w_br, w_out, w_up, w_dn, w_in2, w_out2, w_g2, w_u2, w_d2, par_d, par2_d,
              cst_d, out_d)


def build(nc, ctx, x_d, w_in, w_br, w_out, w_up, w_dn, w_in2, w_out2, w_g2, w_u2, w_d2, par_d, par2_d, cst_d, out_d):
    def sem(name):
        return ctx.enter_context(nc.semaphore(name))

    def sb(name, shape, dt=F32, c=ctx):
        return c.enter_context(nc.sbuf_tensor(name, shape, dt))

    NPAR = PAR["_n"]
    N0, N1 = CST["_n0"], CST["_n1"]
    raw = sb("raw", [128, NRAW, 2048])
    whi = sb("whi", [128, NSPL, 2048], F32R)
    wlo = sb("wlo", [128, NSPL, 2048], F32R)
    xr = sb("xr", [128, 2, D])
    Ahi = sb("Ahi", [128, 8, S], F32R)
    Alo = sb("Alo", [128, 8, S], F32R)
    ys = sb("ys", [128, 2, D])
    par = sb("par", [128, NPAR])
    cst = sb("cst", [128, N0])
    st = sb("st", [128, 384])
    with ExitStack() as r1:
        qkA = sb("qkA", [128, 16, S], c=r1)
    with ExitStack() as r2:
        Bhi = sb("Bhi", [128, 8, S], F32R, c=r2)
        Blo = sb("Blo", [128, 8, S], F32R, c=r2)
        gap = ExitStack()
        gates = sb("gates", [128, 2, 4096], c=gap)
        r1 = ExitStack()
        qkB = sb("qkB", [128, 8, S], c=r1)
        V = sb("V", [128, 2, 1536], c=r1)
        Sb = sb("Sb", [128, 2, 768], c=r1)
        PT = sb("PT", [128, 2, 768], c=r1)
        cs1 = sb("cs1", [128, N1], c=r1)
        nlf = sb("nlf", [128, 2, 128], c=r1)
        r1.close()
        r3 = ExitStack()
        hhi = sb("hhi", [128, 2, 4, S], F32R, c=r3)
        hlo = sb("hlo", [128, 2, 4, S], F32R, c=r3)
        ust = sb("ust", [128, 2, 2, 512], c=r3)
        V2 = sb("V2", [128, 2, 512], c=r3)
        tg = sb("tg", [128, 2, 512], c=r3)
        r3.close()
        gap.close()
        g2 = ExitStack()
        qk2T = sb("qk2T", [128, 8, S], c=g2)
        par2 = sb("par2", [128, 1024 + 128 + 256], c=g2)
        ch = sb("ch", [128, 4, 288], c=g2)
        ca = sb("ca", [128, 4, S], c=g2)
        PT2 = sb("PT2", [128, 2, 768], c=g2)
        S2 = sb("S2", [128, 2, 256], c=g2)
        g2.close()

    b = [ctx.enter_context(nc.psum_tensor(f"b{i}", [128, 512], F32)) for i in range(3)]
    SS = ctx.enter_context(nc.psum_tensor("SS", [128, 1024], F32))
    TT = ctx.enter_context(nc.psum_tensor("TT", [128, 1024], F32))
    OO = ctx.enter_context(nc.psum_tensor("OO", [128, 512], F32))
    bank = {0: b[0][:], 1: b[1][:], 2: b[2][:], 3: SS[:, 0:512], 4: SS[:, 512:1024],
            5: TT[:, 0:512], 6: TT[:, 512:1024], 7: OO[:]}
    free = {i: [] for i in range(8)}

    PE = Queue(sem("s_pe"))
    AC = Queue(sem("s_act"))
    VE = Queue(sem("s_dve"))
    GP = Queue(sem("s_pool"))
    SP = Queue(sem("s_sp"))
    d_raw = [sem(f"d_raw{i}") for i in range(NRAW)]
    d_x = sem("d_x")
    d_par = sem("d_par")
    d_cst = sem("d_cst")
    d_cs1 = sem("d_cs1")
    d_par2 = sem("d_par2")
    d_out = sem("d_out")

    def dma(dst, src, s, *waits):
        def fn(e):
            e.dma_start(dst, src).then_inc(s, 16)
        SP.put(fn, *waits, sig=False)

    def pcol(name, i=0, n=1):
        o, w = PAR[name]
        return par[:, o + i:o + i + n]

    ident = cst[:, 0:128]
    maskF = cst[:, 128:384]

    def c1(name, a=0, n=None):
        o, w = CST[name]
        return cs1[:, o + a:o + a + (w - a if n is None else n)]

    _st = [0]

    def stat(n=1):
        a = _st[0]
        _st[0] += n
        assert _st[0] <= 384
        return st[:, a:a + n]

    units = []

    def add_unit(src, k0, kn, c0, n):
        v = src[k0 * 128:(k0 + kn) * 128, c0:c0 + n].rearrange("(k p) n -> p k n", p=128)
        units.append((v, kn, n))
        return len(units) - 1

    CH1 = [(0, 512), (512, 512), (1024, 512), (1536, 512), (2048, 512), (2560, 512), (3072, 512),
           (3584, 260), (3844, 512), (4356, 256)] + [(4612 + 512 * i, 512) for i in range(8)]
    u_p1 = [[add_unit(w_in, 0, 4, c, n), add_unit(w_in, 4, 4, c, n)] for c, n in CH1]
    u_br = [[add_unit(w_br, 4 * p, 4, 512 * h, 512) for p in range(2)] for h in range(2)]
    u_wo = [[add_unit(w_out, 4 * k, 4, 512 * n, 512) for n in range(2)] for k in range(2)]
    u_up, u_dn = {}, {}

    def plan_down(tab, w, j, kn):
        if kn == 4:
            tab[j] = [add_unit(w, 4 * j, 4, 512 * n, 512) for n in range(2)]
        else:
            tab[j] = [add_unit(w, 4 * j, kn, 0, 1024)]

    for j in range(8):
        u_up[j] = [add_unit(w_up, 4 * k, 4, 512 * j, 512) for k in range(2)]
        if j:
            plan_down(u_dn, w_dn, j - 1, 4)
    plan_down(u_dn, w_dn, 7, 4)
    CH2 = [(1536, 512), (2048, 512), (0, 512), (512, 512), (1024, 512)]
    u_p2 = [[add_unit(w_in2, 4 * k, 4, c, n) for k in range(2)] for c, n in CH2]
    u_wo2 = [[add_unit(w_out2, 4 * k, 4, 512 * n, 512) for n in range(2)] for k in range(2)]
    u_g2, u_u2, u_d2 = {}, {}, {}
    HC2 = [4, 4, 4, 4, 4, 2]
    for j in range(6):
        n = HC2[j] * 128
        u_g2[j] = [add_unit(w_g2, 4 * k, 4, 512 * j, n) for k in range(2)]
        u_u2[j] = [add_unit(w_u2, 4 * k, 4, 512 * j, n) for k in range(2)]
        if j:
            plan_down(u_d2, w_d2, j - 1, HC2[j - 1])
    plan_down(u_d2, w_d2, 5, 2)

    nu = len(units)
    hi_t, lo_t, pe_t = [None] * nu, [None] * nu, [None] * nu
    nxt = {"dma": 0, "split": 0}

    def load(i):
        v, kn, n = units[i]
        s = i % NRAW
        w = [hi_t[i - NRAW], lo_t[i - NRAW]] if i >= NRAW else []
        dma(raw[:, s, 0:kn * n].rearrange("p (k n) -> p k n", k=kn), v, d_raw[s], w)

    def split_hi(i):
        v, kn, n = units[i]
        s, r = i % NSPL, i % NRAW
        m = kn * n
        landed = (d_raw[r], 16 * (i // NRAW + 1))
        old = pe_t[i - NSPL] if i >= NSPL else None
        hi_t[i] = AC.put(lambda e: e.copy(whi[:, s, 0:m], raw[:, r, 0:m]), landed, old)

    def split_lo(i):
        v, kn, n = units[i]
        s, r = i % NSPL, i % NRAW
        m = kn * n
        landed = (d_raw[r], 16 * (i // NRAW + 1))
        lo_t[i] = VE.put(lambda e: e.tensor_tensor(wlo[:, s, 0:m], raw[:, r, 0:m], whi[:, s, 0:m].bitcast(F32),
                                                   ALU.subtract), landed, hi_t[i])
        if nxt["dma"] < nu:
            load(nxt["dma"])
            nxt["dma"] += 1

    def prefetch(i):
        lows()
        while nxt["split"] < min(nu, i + LEAD):
            split_hi(nxt["split"])
            lo_due.append(nxt["split"])
            nxt["split"] += 1

    lo_due = []

    def lows():
        while lo_due:
            split_lo(lo_due.pop(0))

    def mm_unit(i, hi, lo, k0, t, out_of, first, last, waits, done, kr=None):
        lows()
        v, kn, n = units[i]
        s = i % NSPL
        H = whi[:, s, 0:kn * n].rearrange("p (k n) -> p k n", k=kn)
        L = wlo[:, s, 0:kn * n].rearrange("p (k n) -> p k n", k=kn)
        ws = [hi_t[i], lo_t[i]] + list(waits)
        krs = list(range(kn)) if kr is None else list(kr)
        tok = None
        for c0 in range(0, n, 512):
            c1_ = min(n, c0 + 512)
            for kc in krs:
                dst = out_of(kc, c0)
                xh = hi[:, k0 + kc, t * 128:(t + 1) * 128]
                xl = lo[:, k0 + kc, t * 128:(t + 1) * 128]
                f = first(kc)
                for q, (a, w) in enumerate(((xh, H), (xh, L), (xl, H))):
                    tok = PE.put(_mm(dst, a, w[:, kc, c0:c1_], f and q == 0, last(kc) and q == 2), ws,
                                 sig=(kc == krs[-1] and q == 2 and c1_ == n))
                    ws = []
        if done:
            pe_t[i] = tok
        return tok

    def _mm(dst, a, w, start, stop):
        return lambda e: e.matmul(dst, a, w, start=start, stop=stop)

    def mm(dst, lhsT, rhs, start, stop, *waits, sig=True):
        return PE.put(_mm(dst, lhsT, rhs, start, stop), *waits, sig=sig)

    def tr(dst, src, *waits, sig=True):
        return PE.put(lambda e: e.transpose(dst, src, ident), *waits, sig=sig)

    active, pending = [], []
    cnt = {"O": 0, "S": 0, "P": 0, "B": 0, "T": 0}
    tg_free = [None, None]
    tgbuf = [PT]

    freed = []

    def rel(tab, k, toks):
        freed.append((tab, k, toks))

    def bg(start=1):
        for g in list(active):
            if next(g, "end") == "end":
                active.remove(g)
        for _ in range(start):
            if pending:
                g = pending.pop(0)
                if next(g, "end") != "end":
                    active.append(g)
        while freed:
            tab, k, toks = freed.pop(0)
            tab[k] = toks

    def bg_all():
        late()
        while active or pending:
            bg()

    def take(*bks):
        while any(free[k] is None for k in bks):
            yield
        w = [free[k] for k in bks]
        for k in bks:
            free[k] = None
        return w

    def take_one(*bks):
        while all(free[k] is None for k in bks):
            yield
        k = next(k for k in bks if free[k] is not None)
        w = free[k]
        free[k] = None
        return k, w

    def slot(frees):
        while all(f is None for f in frees):
            yield
        i = next(i for i, f in enumerate(frees) if f is not None)
        w = frees[i]
        frees[i] = None
        return i, w

    dma(xr[:], x_d.rearrange("(t p) d -> p t d", p=128), d_x)
    dma(cst[:], cst_d[:, 0:N0], d_cst)
    dma(par[:], par_d, d_par)
    for i in range(NRAW):
        load(i)
        nxt["dma"] += 1
    dma(cs1[:], cst_d[:, N0:N0 + N1], d_cs1)
    T_X, T_PAR, T_CST, T_CS1 = (d_x, 16), (d_par, 16), (d_cst, 16), (d_cs1, 16)

    mhalf = stat(16)
    t_mh = GP.put(lambda e: e.memset(mhalf, -0.5))

    def rsqrt(src, n, count, t_src):
        v = stat(n)
        r = stat(n)
        a = VE.put(lambda e: e.tensor_scalar(v, src, 1.0 / count, EPS, ALU.mult, ALU.add), t_src)
        c = GP.put(lambda e: e.tensor_tensor(r, v, mhalf[:, 0:n], ALU.pow), a, t_mh)
        return r, c

    def sumsq(src, t_src, junk):
        o = stat(1)
        t = AC.put(lambda e: e.activation(junk, src, ACT.Square, accum_out=o), t_src)
        return o, t

    def turn_split(src, t_src, hi, lo, kc0, t, bk, gain=None, nk=4, post=None):
        w = [t_src, T_CST] + free[bk]
        for k in range(nk):
            tk = tr(bank[bk][:, 128 * k:128 * k + 128], src[:, 128 * k:128 * k + 128], w, sig=(k == nk - 1))
            w = []
        ph = hi[:, kc0:kc0 + nk, t * 128:(t + 1) * 128]
        pl = lo[:, kc0:kc0 + nk, t * 128:(t + 1) * 128]
        ps = bank[bk][:, 0:128 * nk].rearrange("p (k q) -> p k q", k=nk)
        if gain is None:
            a = AC.put(lambda e: e.copy(ph, ps), tk)
            v = VE.put(lambda e: e.tensor_tensor(pl, ps, ph.bitcast(F32), ALU.subtract), a)
        else:
            i = cnt["T"] % 2
            cnt["T"] += 1
            w = tgbuf[0][:, i, 0:128 * nk].rearrange("p (k q) -> p k q", k=nk)
            m = VE.put(lambda e: e.tensor_tensor(w, ps, gain(kc0).unsqueeze(2).broadcast_to([128, nk, 128]), ALU.mult),
                       tk, T_PAR, tg_free[i])
            a = AC.put(lambda e: e.copy(ph, w), m)
            v = VE.put(lambda e: e.tensor_tensor(pl, w, ph.bitcast(F32), ALU.subtract), a)
            tg_free[i] = v
            free[bk] = [m]
            return [a, v]
        free[bk] = [a, v]
        return [a, v]

    prefetch(0)
    A_t = {}
    for t in range(2):
        for h in range(2):
            A_t[t, h] = turn_split(xr[:, t, 512 * h:512 * h + 512], T_X, Ahi, Alo, 4 * h, t, 5 + h,
                                   gain=lambda k: pcol("g_mix", k, 4))
    ss1 = stat(2)
    tq = None
    for t in range(2):
        tq = AC.put(lambda e, t=t: e.activation(ys[:, t, :], xr[:, t, :], ACT.Square, accum_out=ss1[:, t:t + 1]), T_X)
    r1_, t_r1 = rsqrt(ss1, 2, D, tq)

    lamt = stat(2)
    lame = stat(2)
    lam = stat(1)
    nlam = stat(1)
    lo_, _ = PAR["lam"]
    lscr = stat(64)
    ta = VE.put(lambda e: e.tensor_tensor(lscr, par[:, lo_:lo_ + 64], par[:, lo_ + 64:lo_ + 128], ALU.mult), T_PAR)
    ta = VE.put(lambda e: e.tensor_reduce(lamt, lscr.rearrange("p (a b) -> p a b", a=2), AX.X, ALU.add), ta)
    ta = AC.put(lambda e: e.activation(lame, lamt, ACT.Exp), ta)
    ta = VE.put(lambda e: e.tensor_tensor(lam, lame[:, 0:1], lame[:, 1:2], ALU.subtract), ta)
    t_nlam = VE.put(lambda e: e.tensor_scalar(nlam, lam, -1.0, -0.2, ALU.mult, ALU.add), ta)

    rot = [0]
    later = []

    def late():
        while later:
            later.pop(0)()

    def chunk(us, hi, lo, src_t, evac, first_of_phase=False, start=1):
        n = units[us[0]][2]
        bks = []
        for t in range(2):
            bks.append(rot[0] % 2)
            rot[0] += 1
        order = [(0, 0), (1, 0), (0, 1), (1, 1)] if first_of_phase else [(0, 0), (0, 1), (1, 0), (1, 1)]
        for ui, t in order:
            bk = bks[t]
            w = list(src_t[t, ui])
            if ui == 0:
                w += free[bk]
                free[bk] = []
            tk = mm_unit(us[ui], hi, lo, 4 * ui, t, lambda kc, c0, bk=bk: bank[bk][:, 0:n],
                         lambda kc, ui=ui: ui == 0 and kc == 0, lambda kc, ui=ui: ui == 1 and kc == 3, w, t == 1)
            if t == 1:
                prefetch(us[ui] + 1)
            late()
            if ui == 1:
                later.append(lambda t=t, bk=bk, tk=tk: evac(t, bk, tk, n))
            bg(start)

    qk_t = {}
    V_t = {}
    PAIRS = {0: [(0, "qk", 0, 0.125), (256, "qk", 2, 1.0)],
             1: [(0, "v", 0, None), (256, "qk", 4, 0.125)],
             2: [(0, "qk", 6, 0.125), (256, "qk", 8, 0.125)],
             3: [(0, "qk", 10, 1.0), (256, "qk", 12, 1.0)],
             4: [(0, "qk", 14, 1.0), (256, "v", 256, None)],
             5: [(0, "v", 512, None), (256, "v", 768, None)],
             6: [(0, "qk", 16, 0.125), (256, "qk", 18, 1.0)],
             7: [(0, "v", 1024, None)],
             8: [(0, "qk", 20, 32 ** -0.5), (256, "qk", 22, 1.0)],
             9: [(0, "v", 1280, None)]}
    f_t = {}
    ff = stat(8)
    stage_free = {5: [], 7: [], 9: []}

    def qk_tile(i):
        return qkA[:, i, :] if i < 16 else qkB[:, i - 16, :]

    def turn_pairs(c, t_stage):
        sg = gates[:, :, 1024 + 512 * (c % 6):1536 + 512 * (c % 6)]
        done = []
        for col, kind, dst, sc in PAIRS[c]:
            if kind != "qk":
                continue
            bk = 5 + (dst // 2) % 2
            w = yield from take(bk)
            w = [t_stage[0], t_stage[1], w]
            for j in range(2):
                for t in range(2):
                    tk = tr(bank[bk][:, 256 * j + 128 * t:256 * j + 128 * t + 128],
                            sg[:, t, col + 128 * j:col + 128 * j + 128], w, sig=(j == 1 and t == 1))
                    w = []
            done.append(tk)
            yield
            q = qkA[:, dst:dst + 2, :] if dst < 16 else qkB[:, dst - 16:dst - 14, :]
            src = bank[bk].rearrange("p (j q) -> p j q", j=2)
            if (dst // 2) % 2 == 0:
                tv = VE.put(lambda e, q=q, src=src, sc=sc: e.tensor_scalar(q, src, sc, None, ALU.mult), tk)
            else:
                tv = AC.put(lambda e, q=q, src=src, sc=sc: e.mul(q, src, sc), tk)
            rel(free, bk, [tv])
            qk_t[dst] = qk_t[dst + 1] = tv
        stage_free[c] = [done[-1]]

    def evac1(c):
        def fn(t, bk, tk, n):
            ts = []
            for col, kind, dst, sc in PAIRS[c]:
                if kind == "v":
                    o = V[:, t, dst:dst + 256]
                    w = []
                else:
                    a = 1024 + 512 * (c % 6) + col
                    o = gates[:, t, a:a + 256]
                    w = stage_free[c - 6] if c >= 6 else []
                tv = AC.put(lambda e, o=o, col=col: e.mul(o, bank[bk][:, col:col + 256], r1_[:, t:t + 1]), tk, t_r1, w)
                if kind == "v":
                    V_t[dst, t] = tv
                else:
                    stg[c, t] = tv
                ts.append(tv)
            if c == 7:
                tv = VE.put(lambda e: e.scalar_tensor_tensor(
                    out=ff[:, 4 * t:4 * t + 4], in0=bank[bk][:, 256:260], scalar=r1_[:, t:t + 1],
                    in1=pcol("b_f", 0, 4), op0=ALU.mult, op1=ALU.add), tk, tv, t_r1, T_PAR)
                f_t[t] = tv
                ts.append(tv)
            free[bk] = ts
            if t == 1 and any(k == "qk" for _, k, _, _ in PAIRS[c]):
                active.insert(0, turn_pairs(c, [stg[c, 0], stg[c, 1]]))
            if t == 1:
                if c == 1:
                    pending.extend(sb_task(h) for h in range(4))
                if c == 5:
                    pending.extend(dil_task(h, qb) for h in range(4) for qb in range(2))
                if c == 7:
                    pending.append(forget_gates())
                    pending.extend(fox_task(h, qb) for h in range(4) for qb in range(2))
                if c == 9:
                    pending.extend(diff_task(h, qb) for h in range(4) for qb in range(2))
        return fn

    stg = {}
    Sb_free = [[], []]
    PT_free = [[tg_free[0]], [tg_free[1]]]
    ys_t = {}

    def sb_task(h):
        qt, kt, p = h // 2, 2 + h // 2, 64 * (h % 2)
        Q, K = qkA[p:p + 64, qt, :], qkA[p:p + 64, kt, :]
        while kt not in qk_t:
            yield
        bk, wb = yield from take_one(3, 4)
        Z = bank[bk]
        mm(Z[:, 0:256], K[:, 0:128], Q[:, 0:256], True, True, qk_t[qt], qk_t[kt], wb, sig=False)
        tz = mm(Z[:, 256:384], K[:, 128:256], Q[:, 128:256], True, True)
        yield
        si, ws = yield from slot(Sb_free)
        zm, L = Sb[:, si, 0:384], Sb[:, si, 384:768]
        t = VE.put(lambda e: e.tensor_tensor(zm, Z[:, 0:384], c1("MB"), ALU.add), tz, T_CS1, ws)
        rel(free, bk, [t])
        a = AC.put(lambda e: e.activation(L, zm, ACT.Abs), t)
        a = AC.put(lambda e: e.activation(L, L, ACT.Exp, scale=-1.0), a)
        a = AC.put(lambda e: e.activation(L, L, ACT.Ln, bias=1.0), a)
        yield
        t = VE.put(lambda e: e.scalar_tensor_tensor(out=L, in0=zm, scalar=0.0, in1=L, op0=ALU.max, op1=ALU.add), a)
        yield
        bk, wb = yield from take_one(5, 6)
        R = bank[bk]
        mm(R[:, 0:384], c1("LG"), L, True, False, t, wb, sig=False)
        tr_ = mm(R[:, 128:256], c1("UO", 128, 128), L[:, 256:384], False, True)
        yield
        t = VE.put(lambda e: e.tensor_tensor(zm, zm, R[:, 0:384], ALU.subtract), tr_)
        rel(free, bk, [t])
        a = AC.put(lambda e: e.activation(zm, zm, ACT.Exp), t)
        yield
        ob, wo = yield from take_one(2, 7)
        o0, o1 = bank[ob][:, 0:64], bank[ob][:, 64:128]
        v = V[:, :, 64 * h:64 * h + 64]
        t0 = mm(o0, zm[:, 0:128], v[:, 0, :], True, True, a, V_t[0, 0], V_t[0, 1], wo)
        mm(o1, zm[:, 128:256], v[:, 0, :], True, False, sig=False)
        t1 = mm(o1, zm[:, 256:384], v[:, 1, :], False, True)
        rel(Sb_free, si, [t1])
        yield
        for qb, o in ((0, o0), (1, o1)):
            ys_t[0, h, qb] = VE.put(
                lambda e, qb=qb, o=o: e.tensor_copy(ys[:, qb, 64 * h:64 * h + 64], o), t1, tq)
        rel(free, ob, [ys_t[0, h, 1]])

    def softmax_tail(P, segs, ptr, kn, vs, vw, l, t_exp, write, si, sfree):
        n = len(vs)
        if n > 4:
            wb = yield from take(5, 6)
            bt, T = 5, TT
        else:
            bt, wb = yield from take_one(5, 6)
            T = bank[bt]
        w = [t_exp, wb]
        for j in range(n):
            tk = tr(T[:, 128 * j:128 * j + 128], P[:, 128 * j:128 * j + 128], w, sig=(j == n - 1))
            w = []
        rel(sfree, si, [tk])
        yield
        m = 128 * n
        pi, wp = yield from slot(PT_free)
        te = AC.put(lambda e: e.copy(ptr[:, pi, 0:m], T[:, 0:m]), tk, wp)
        rel(free, bt, [te])
        if n > 4:
            rel(free, 6, [te])
        rl = stat_l[cnt["P"] % 8]
        cnt["P"] += 1
        trl = VE.put(lambda e: e.reciprocal(rl, l), t_exp)
        yield
        ob, wo = yield from take_one(2, 7)
        o = bank[ob][:, 0:64]
        w = [te, vw, wo]
        for j in range(n):
            tk = mm(o, ptr[:, pi, 128 * j:128 * j + 128], vs[j], j == 0, j == n - 1, w, sig=(j == n - 1))
            w = []
        rel(PT_free, pi, [tk])
        yield
        rel(free, ob, [write(o, rl, [tk, trl])])

    stat_l = [stat(1) for _ in range(8)]
    stat_m = [stat(2) for _ in range(8)]
    stat_s = [stat(2) for _ in range(8)]

    def dil_task(h, qb):
        kn = qb + 1
        m = 128 * kn
        off = 0 if qb == 0 else 128
        while 14 not in qk_t:
            yield
        w = yield from take(3, 4)
        w = [w] + [qk_t[i] for i in (4, 6, 8, 10, 12, 14)]
        p = 64 * (h % 2)
        for g in range(3):
            q, k = 4 + 2 * g + h // 2, 10 + 2 * g + h // 2
            tk = mm(SS[:, m * g:m * g + m], qkA[p:p + 64, q, 128 * qb:128 * qb + 128], qkA[p:p + 64, k, 0:m],
                    True, True, w, sig=(g == 2))
            w = []
        yield
        si, ws = yield from slot(Sb_free)
        P = Sb[:, si, 0:3 * m]
        for g in range(3):
            t = VE.put(lambda e, g=g: e.scalar_tensor_tensor(
                out=P[:, m * g:m * g + m], in0=c1("DD", 384 * g + off, m), scalar=-SL_DIL[g][h],
                in1=SS[:, m * g:m * g + m], op0=ALU.mult, op1=ALU.add), tk, T_CS1, ws)
        rel(free, 3, [t])
        rel(free, 4, [t])
        i = cnt["S"] % 8
        cnt["S"] += 1
        nm, l = stat_m[i][:, 0:1], stat_s[i][:, 0:1]
        t = VE.put(lambda e: e.tensor_reduce(nm, P, AX.X, ALU.max, negate=True), t)
        te = AC.put(lambda e: e.activation(P, P, ACT.Exp, bias=nm, accum_out=l), t)
        yield
        vs = [V[:, kb, 256 + 256 * g + 64 * h:320 + 256 * g + 64 * h] for g in range(3) for kb in range(kn)]
        vw = [V_t[256 * g, t_] for g in (1, 2, 3) for t_ in range(2)]

        def write(o, rl, w):
            ys_t[1, h, qb] = VE.put(lambda e: e.tensor_scalar(ys[:, qb, 256 + 64 * h:320 + 64 * h], o, rl, None,
                                                              ALU.mult), w)
            return ys_t[1, h, qb]

        yield from softmax_tail(P, None, PT, kn, vs, vw, l, te, write, si, Sb_free)

    cumq = stat(8)
    lf = stat(8)
    fox = {}

    def forget_gates():
        e1 = stat(8)
        a = AC.put(lambda e: e.activation(e1, ff, ACT.Abs), f_t[0], f_t[1])
        a = AC.put(lambda e: e.activation(e1, e1, ACT.Exp, scale=-1.0), a)
        a = AC.put(lambda e: e.activation(e1, e1, ACT.Ln, bias=1.0), a)
        yield
        t = VE.put(lambda e: e.scalar_tensor_tensor(out=lf, in0=ff, scalar=0.0, in1=e1, op0=ALU.min,
                                                    op1=ALU.subtract), a)
        fox["lf"] = t
        yield
        ob, wo = yield from take_one(2, 7)
        o0, o1 = bank[ob][:, 0:64], bank[ob][:, 64:128]
        mm(o0[:, 0:4], c1("UO", 0, 128), lf[:, 0:4], True, True, t, T_CS1, wo, sig=False)
        mm(o1[:, 0:4], c1("UO", 128, 128), lf[:, 0:4], True, False, sig=False)
        tk = mm(o1[:, 0:4], c1("UO", 0, 128), lf[:, 4:8], False, True)
        yield
        VE.put(lambda e: e.tensor_copy(cumq[:, 0:4], o0[:, 0:4]), tk)
        fox["cq"] = VE.put(lambda e: e.tensor_copy(cumq[:, 4:8], o1[:, 0:4]), tk)
        rel(free, ob, [fox["cq"]])

    nlf_free = [[]]

    def fox_task(h, qb):
        while "cq" not in fox or (qb == 1 and ("b", h, 1) not in fox):
            yield
        if qb == 0:
            _, wn = yield from slot(nlf_free)
            for t_ in range(2):
                src = lf[:, 4 * t_ + h:4 * t_ + h + 1]
                fox["b", h, t_] = VE.put(lambda e, src=src, t_=t_: e.tensor_scalar(
                    nlf[:, t_, :], c1("UO", 128, 128), src, -1.0, ALU.mult, ALU.mult), fox["lf"], wn, T_CS1)
            yield
        kn = qb + 1
        m = 128 * kn
        while 18 not in qk_t:
            yield
        bk, wb = yield from take_one(3, 4)
        Z = bank[bk]
        p = 64 * (h % 2)
        q, k = h // 2, 2 + h // 2
        mm(Z[:, 0:m], qkB[p:p + 64, q, 128 * qb:128 * qb + 128], qkB[p:p + 64, k, 0:m], True, False,
           wb, qk_t[16], qk_t[18], sig=False)
        tk = mm(Z[:, 0:m], nlf[:, 0, :], c1("UO", 0, m), False, qb == 0, fox["b", h, 0], fox["b", h, 1])
        if qb == 1:
            tk = mm(Z[:, 128:256], nlf[:, 1, :], c1("UO", 0, 128), False, True)
        fox["r", h, qb] = tk
        if ("r", h, 1 - qb) in fox:
            rel(nlf_free, 0, [fox["r", h, 0], fox["r", h, 1]])
        yield
        si, ws = yield from slot(Sb_free)
        P = Sb[:, si, 0:m]
        t = VE.put(lambda e: e.scalar_tensor_tensor(
            out=P, in0=Z[:, 0:m], scalar=cumq[:, 4 * qb + h:4 * qb + h + 1], in1=maskF[:, 256 - m:256],
            op0=ALU.add, op1=ALU.add), tk, ws, fox["cq"])
        rel(free, bk, [t])
        i = cnt["S"] % 8
        cnt["S"] += 1
        nm, l = stat_m[i][:, 0:1], stat_s[i][:, 0:1]
        t = VE.put(lambda e: e.tensor_reduce(nm, P, AX.X, ALU.max, negate=True), t)
        te = AC.put(lambda e: e.activation(P, P, ACT.Exp, bias=nm, accum_out=l), t)
        yield
        vs = [V[:, kb, 1024 + 64 * h:1088 + 64 * h] for kb in range(kn)]

        def write(o, rl, w):
            ys_t[2, h, qb] = VE.put(lambda e: e.tensor_scalar(ys[:, qb, 512 + 64 * h:576 + 64 * h], o, rl, None,
                                                              ALU.mult), w)
            return ys_t[2, h, qb]

        yield from softmax_tail(P, None, PT, kn, vs, [V_t[1024, 0], V_t[1024, 1]], l, te, write, si, Sb_free)

    gd8 = stat(0)
    lc = [stat(1) for _ in range(8)]

    def diff_task(h, qb):
        kn = qb + 1
        m = 128 * kn
        off = 0 if qb == 0 else 128
        while 22 not in qk_t:
            yield
        bk, wb = yield from take_one(3, 4)
        Z = bank[bk]
        w = [wb, qk_t[20], qk_t[22]]
        for c in range(2):
            p = 64 * (h % 2) + 32 * c
            tk = mm(Z[:, m * c:m * c + m], qkB[p:p + 32, 4 + h // 2, 128 * qb:128 * qb + 128],
                    qkB[p:p + 32, 6 + h // 2, 0:m], True, True, w)
            w = [tk]
        yield
        si, ws = yield from slot(Sb_free)
        P = Sb[:, si, 0:2 * m]
        for c in range(2):
            t = VE.put(lambda e, c=c: e.scalar_tensor_tensor(
                out=P[:, m * c:m * c + m], in0=c1("DD", 1152 + off, m), scalar=-SL_DIFF[h],
                in1=Z[:, m * c:m * c + m], op0=ALU.mult, op1=ALU.add), tk, T_CS1, ws)
        rel(free, bk, [t])
        i = cnt["S"] % 8
        cnt["S"] += 1
        nm, l = stat_m[i], stat_s[i]
        t = VE.put(lambda e: e.tensor_reduce(nm, P.rearrange("p (c k) -> p c k", c=2), AX.X, ALU.max, negate=True), t)
        for c in range(2):
            te = AC.put(lambda e, c=c: e.activation(P[:, m * c:m * c + m], P[:, m * c:m * c + m], ACT.Exp,
                                                    bias=nm[:, c:c + 1], accum_out=l[:, c:c + 1]), t)
        yield
        co = lc[i]
        t = VE.put(lambda e: e.reciprocal(co, l[:, 1:2]), te)
        t = VE.put(lambda e: e.scalar_tensor_tensor(out=co, in0=co, scalar=l[:, 0:1], in1=nlam, op0=ALU.mult,
                                                    op1=ALU.mult), t, t_nlam)
        t = VE.put(lambda e: e.scalar_tensor_tensor(out=P[:, 0:m], in0=P[:, m:2 * m], scalar=co, in1=P[:, 0:m],
                                                    op0=ALU.mult, op1=ALU.add), t)
        yield
        vs = [V[:, kb, 1280 + 64 * h:1344 + 64 * h] for kb in range(kn)]

        def write(o, rl, w):
            ys_t[3, h, qb] = VE.put(lambda e: e.tensor_scalar(ys[:, qb, 768 + 64 * h:832 + 64 * h], o, rl, None,
                                                              ALU.mult), w)
            return ys_t[3, h, qb]

        yield from softmax_tail(P, None, PT, kn, vs, [V_t[1280, 0], V_t[1280, 1]], l[:, 0:1], t, write, si, Sb_free)

    prefetch(u_p1[0][0])
    g_t = {}

    def evac_gate(c):
        def fn(t, bk, tk, n):
            o = gates[:, t, 512 * c:512 * c + 512]
            w = [[stage_free[k] for k in range(10)], None]
            free[bk] = [AC.put(lambda e: e.mul(o, bank[bk], r1_[:, t:t + 1]), tk, t_r1, w[0], w[1])]
            g_t[c, t] = free[bk][0]
        return fn

    for c in range(18):
        chunk(u_p1[c], Ahi, Alo, A_t, evac1(c) if c < 10 else evac_gate(c - 10), first_of_phase=(c == 0))
    bg_all()

    tgbuf[0] = tg
    def diff_norm(qb):
        yd = ys[:, qb, 768:1024]
        y3 = yd.rearrange("p (h d) -> p h d", h=4)
        sq = ust[:, 0, qb, 0:256]
        rs4 = stat(4)
        t = VE.put(lambda e: e.tensor_tensor(sq, yd, yd, ALU.mult), [ys_t[3, h, qb] for h in range(4)], PE_last(PE))
        t = VE.put(lambda e: e.tensor_reduce(rs4, sq.rearrange("p (h d) -> p h d", h=4), AX.X, ALU.add), t)
        r, tp = rsqrt(rs4, 4, 64, t)
        t = VE.put(lambda e: e.tensor_tensor(y3, y3, r.unsqueeze(2).broadcast_to([128, 4, 64]), ALU.mult), tp)
        t = VE.put(lambda e: e.scalar_tensor_tensor(
            out=y3, in0=y3, scalar=0.8, in1=pcol("g_diff", 0, 64).unsqueeze(1).broadcast_to([128, 4, 64]),
            op0=ALU.mult, op1=ALU.mult), t)
        ys_t["d", qb] = t

    for qb in range(2):
        diff_norm(qb)

    B_t = {}
    for hf in range(2):
        for t in range(2):
            w = [ys_t[2 * hf, h, t] for h in range(4)] + [ys_t[2 * hf + 1, h, t] for h in range(4)] + [ys_t["d", t]]
            B_t[t, hf] = turn_split(ys[:, t, 512 * hf:512 * hf + 512], w, Bhi, Blo, 4 * hf, t, 5 + t)
    t_ysfree = PE_last(PE)
    mix_t = {}
    M_t = {}
    W_acc = {(0, 0): 3, (1, 0): 4, (0, 1): 7, (1, 1): 0}
    for hf in range(2):
        for n in range(4):
            sg = gates[:, :, 1024 * n + 512 * hf:1024 * n + 512 * hf + 512]
            tsg = AC.put(lambda e, sg=sg: e.activation(sg, sg, ACT.Sigmoid), g_t[2 * n + hf, 0], g_t[2 * n + hf, 1])
            u = u_br[hf][n // 2]
            kr = range(2 * (n % 2), 2 * (n % 2) + 2)
            for t in range(2):
                bk = 1 + rot[0] % 2
                rot[0] += 1
                tk = mm_unit(u, Bhi, Blo, 4 * (n // 2), t, lambda kc, c0, bk=bk: bank[bk],
                             lambda kc, kr=kr: kc == kr[0], lambda kc, kr=kr: kc == kr[-1],
                             B_t[t, n // 2] + free[bk], t == 1 and n % 2 == 1, kr=kr)
                mx = ys[:, t, 512 * hf:512 * hf + 512]
                if n == 0:
                    v = VE.put(lambda e, sg=sg, t=t, bk=bk, mx=mx: e.tensor_tensor(
                        mx, sg[:, t, :], bank[bk], ALU.mult), tk, tsg, t_ysfree)
                    free[bk] = [v]
                else:
                    v = VE.put(lambda e, sg=sg, t=t, bk=bk: e.tensor_tensor(
                        sg[:, t, :], sg[:, t, :], bank[bk], ALU.mult), tk, tsg)
                    free[bk] = [v]
                    v = VE.put(lambda e, sg=sg, t=t, mx=mx: e.tensor_tensor(mx, mx, sg[:, t, :], ALU.add), v,
                               mix_t[t, hf])
                mix_t[t, hf] = v
            if n % 2 == 1:
                prefetch(u + 1)
            if hf == 1 and n in (0, 1):
                t = n
                M_t[t, 0] = turn_split(ys[:, t, 0:512], mix_t[t, 0], Ahi, Alo, 0, t, 5 + t)
    t_gfree = (VE.sem, VE.n)

    def out_proj(us, hi, lo, src_t, mid):
        ts = {}
        for n in range(2):
            for t in range(2):
                bk = W_acc[t, n]
                mm_unit(us[0][n], hi, lo, 0, t, lambda kc, c0, bk=bk: bank[bk],
                        lambda kc: kc == 0, lambda kc: False, src_t[t, 0] + free[bk], t == 1)
                free[bk] = []
            prefetch(us[0][n] + 1)
        mid()
        for t in range(2):
            for n in range(2):
                bk = W_acc[t, n]
                tk = mm_unit(us[1][n], hi, lo, 4, t, lambda kc, c0, bk=bk: bank[bk],
                             lambda kc: False, lambda kc: kc == 3, src_t[t, 1], t == 1)
                if t == 1:
                    prefetch(us[1][n] + 1)
                xs = xr[:, t, 512 * n:512 * n + 512]
                v = VE.put(lambda e, xs=xs, bk=bk: e.tensor_tensor(xs, xs, bank[bk], ALU.add), tk, x_w[t])
                free[bk] = [v]
                ts[t, n] = v
        return ts

    x_w = [[tq], [tq]]

    def mid1():
        for t in range(2):
            M_t[t, 1] = turn_split(ys[:, t, 512:1024], mix_t[t, 1], Ahi, Alo, 4, t, 5 + t)

    x1_t = out_proj(u_wo, Ahi, Alo, M_t, mid1)

    def norm_turn(ts, hi, lo, gname):
        H = {}
        for t in range(2):
            for n in range(2):
                H[t, n] = turn_split(xr[:, t, 512 * n:512 * n + 512], ts[t, n], hi, lo, 4 * n, t, 5 + n,
                                     gain=gname)
        return H

    H_t = norm_turn(x1_t, Bhi, Blo, lambda k: pcol("g_mlp", k, 4))

    def x_stats(ts, junk, jw):
        o = stat(2)
        for t in range(2):
            a = AC.put(lambda e, t=t: e.activation(junk[:, t, :], xr[:, t, :], ACT.Square, accum_out=o[:, t:t + 1]),
                       ts[t, 0], ts[t, 1], jw)
        return rsqrt(o, 2, D, a), a

    (r2_, t_r2), ta2 = x_stats(x1_t, ys, PE_last(PE))

    h_free = [[], []]
    u_free = [[], []]

    def ffn_down(us, j, nj, hid_t, last):
        kn = nj_of(us, j)
        tk_of = {}
        hi, lo = hhi[:, j % 2], hlo[:, j % 2]
        if len(us[j]) == 2:
            seq = [(n, t) for t in range(2) for n in range(2)] if last else [(n, t) for n in range(2) for t in range(2)]
            for n, t in seq:
                bk = W_acc[t, n]
                w = hid_t[t] + (free[bk] if j == 0 else [])
                tk = mm_unit(us[j][n], hi, lo, 0, t, lambda kc, c0, bk=bk: bank[bk],
                             lambda kc: j == 0 and kc == 0, lambda kc: last and kc == 3, w, t == 1)
                if j == 0:
                    free[bk] = []
                if t == 1:
                    prefetch(us[j][n] + 1)
                tk_of[t, n] = tk
                if last:
                    nj(t, n, tk)
        else:
            for t in range(2):
                tk = mm_unit(us[j][0], hi, lo, 0, t, lambda kc, c0, t=t: bank[W_acc[t, c0 // 512]],
                             lambda kc: False, lambda kc: last and kc == kn - 1, hid_t[t], t == 1)
                for n in range(2):
                    nj(t, n, tk)
            prefetch(us[j][0] + 1)
        h_free[j % 2] = [tk]

    def nj_of(us, j):
        return units[us[j][0]][1]

    def residual(ts):
        def fn(t, n, tk):
            bk = W_acc[t, n]
            xs = xr[:, t, 512 * n:512 * n + 512]
            v = VE.put(lambda e: e.tensor_tensor(xs, xs, bank[bk], ALU.add), tk, x_w[t])
            free[bk] = [v]
            ts[t, n] = v
        return fn

    def up_product(us, hi, lo, src_t, order_first, evac):
        n = units[us[0]][2]
        order = [(0, 0), (1, 0), (0, 1), (1, 1)] if order_first else [(0, 0), (0, 1), (1, 0), (1, 1)]
        for ui, t in order:
            bk = 1 + t
            w = list(src_t[t, ui])
            if ui == 0:
                w += free[bk]
                free[bk] = []
            tk = mm_unit(us[ui], hi, lo, 4 * ui, t, lambda kc, c0, bk=bk: bank[bk][:, 0:n],
                         lambda kc, ui=ui: ui == 0 and kc == 0, lambda kc, ui=ui: ui == 1 and kc == 3, w, t == 1)
            if t == 1:
                prefetch(us[ui] + 1)
            if ui == 1:
                evac(t, bk, tk, n)

    x_w = [[ta2], [ta2]]
    x2_t = {}
    hid_t = {}
    for j in range(8):
        up_t = {}

        def ev(t, bk, tk, n, j=j):
            o = ust[:, j % 2, t, :]
            a = AC.put(lambda e: e.activation(o, bank[bk], ACT.Relu, scale=r2_[:, t:t + 1]), tk, t_r2, u_free[j % 2])
            free[bk] = [a]
            up_t[t] = AC.put(lambda e: e.activation(o, o, ACT.Square), a)

        up_product(u_up[j], Bhi, Blo, H_t, j == 0, ev)
        if j:
            ffn_down(u_dn, j - 1, None, hid_t[j - 1], False)
        hid_t[j] = {}
        for t in range(2):
            free[5 + t] = free[5 + t] + h_free[j % 2]
            hid_t[j][t] = turn_split(ust[:, j % 2, t, :], up_t[t], hhi[:, j % 2], hlo[:, j % 2], 0, t, 5 + t)
        u_free[j % 2] = [PE_last(PE)]
    ffn_down(u_dn, 7, residual(x2_t), hid_t[7], True)

    gg = stat(8)
    t_gg = VE.put(lambda e: e.tensor_tensor(gg, pcol("g_fin", 0, 8), pcol("g_n1", 0, 8), ALU.mult), T_PAR)
    t_dve0 = t_gg
    dma(par2[:], par2_d, d_par2, t_gfree)
    T_P2 = (d_par2, 16)
    for t in range(2):
        for n in range(2):
            x2_t[t, n] = [x2_t[t, n], t_gg]
    H2_t = norm_turn(x2_t, Ahi, Alo, lambda k: gg[:, k:k + 4])
    (r3_, t_r3), ta3 = x_stats(x2_t, ys, PE_last(PE))
    ss4 = stat(2)
    x0_t = {}
    t_xturn = PE_last(PE)
    for t in range(2):
        v = VE.put(lambda e, t=t: e.scalar_tensor_tensor(out=xr[:, t, :], in0=xr[:, t, :], scalar=r3_[:, t:t + 1],
                                                         in1=par2[:, 0:1024], op0=ALU.mult, op1=ALU.mult),
                   t_r3, T_P2, ta3, t_xturn)
        a = AC.put(lambda e, t=t: e.activation(ys[:, t, :], xr[:, t, :], ACT.Square, accum_out=ss4[:, t:t + 1]), v)
        x0_t[t] = v
    r4a, t_r4a = rsqrt(ss4, 2, D, a)
    r4_ = stat(2)
    t_r4 = VE.put(lambda e: e.tensor_tensor(r4_, r3_, r4a, ALU.mult), t_r4a)
    x_w = [[a], [a]]

    RT = ust[:, 1, 0, :]
    RT2 = ust[:, 1, 1, :]
    for qk in range(2):
        g = par2[:, 1024 + 64 * qk:1088 + 64 * qk]
        for t in range(2):
            o = (qk * 2 + t) * 64
            VE.put(lambda e, o=o, g=g, t=t: e.tensor_tensor(RT[:, o:o + 64], par2[:, 1152 + 64 * t:1216 + 64 * t], g,
                                                            ALU.mult), T_P2, u_free[1])
            VE.put(lambda e, o=o, g=g, t=t: e.tensor_tensor(
                RT2[:, o:o + 32], par2[:, 1280 + 64 * t:1312 + 64 * t], g[:, 32:64], ALU.mult))
            t_rt = VE.put(lambda e, o=o, g=g, t=t: e.tensor_tensor(
                RT2[:, o + 32:o + 64], par2[:, 1312 + 64 * t:1344 + 64 * t], g[:, 0:32], ALU.mult))

    t_pad = GP.put(lambda e: e.memset(ch[:, :, 0:30], 0.0), t_gfree)
    glu_t = {}
    c_t = {}

    def evac_u(c):
        def fn(t, bk, tk, n):
            o = (ys[:, t, 0:512], ys[:, t, 512:1024])[c]
            v = AC.put(lambda e: e.mul(o, bank[bk], r4_[:, t:t + 1]), tk, t_r4)
            free[bk] = [v]
            glu_t[c, t] = v
            if c == 1 and t == 1:
                pending.append(conv_task())
        return fn

    def conv_task():
        for t in range(2):
            for c, bk in ((1, 6), (0, 5)):
                w = yield from take(bk)
                w = [glu_t[c, t], w]
                for k in range(4):
                    tk = tr(bank[bk][:, 128 * k:128 * k + 128], ys[:, t, 512 * c + 128 * k:512 * c + 128 * k + 128], w,
                            sig=(k == 3))
                    w = []
                if c == 1:
                    yield
                    sg = ca[:, :, 128 * t:128 * t + 128]
                    for k in range(4):
                        a = AC.put(lambda e, k=k, sg=sg: e.activation(sg[:, k, :], bank[6][:, 128 * k:128 * k + 128],
                                                                      ACT.Sigmoid, bias=pcol("glu_b", 4 + k)), tk)
                    rel(free, 6, [a])
            yield
            for k in range(4):
                v = VE.put(lambda e, k=k, sg=sg, t=t: e.scalar_tensor_tensor(
                    out=ch[:, k, 30 + 128 * t:158 + 128 * t], in0=bank[5][:, 128 * k:128 * k + 128],
                    scalar=pcol("glu_b", k), in1=sg[:, k, :], op0=ALU.add, op1=ALU.mult), tk, a)
            rel(free, 5, [v])
        prev = [v] * 4
        for j in range(31):
            for k in range(4):
                wc = pcol("dw_w", 31 * k + j)
                if j == 0:
                    prev[k] = VE.put(lambda e, k=k, wc=wc: e.tensor_scalar(
                        ca[:, k, :], ch[:, k, 0:256], wc, pcol("dw_b", k), ALU.mult, ALU.add), prev[k], t_pad)
                else:
                    prev[k] = VE.put(lambda e, k=k, wc=wc, j=j: e.scalar_tensor_tensor(
                        out=ca[:, k, :], in0=ch[:, k, j:j + 256], scalar=wc, in1=ca[:, k, :], op0=ALU.mult,
                        op1=ALU.add), prev[k])
            if j % 3 == 2:
                yield
        for t in range(2):
            bk = 6
            w = yield from take(bk)
            w = prev + [w]
            for k in range(4):
                tk = tr(bank[bk][:, 128 * k:128 * k + 128], ca[:, k, 128 * t:128 * t + 128], w, sig=(k == 3))
                w = []
            yield
            bs = stat(6)
            mv = stat(2)
            v = VE.put(lambda e, bs=bs, bk=bk: e.bn_stats(bs, bank[bk]), tk)
            v = VE.put(lambda e, bs=bs, mv=mv: e.bn_aggr(mv, bs), v)
            r, tp = rsqrt(mv[:, 1:2], 1, 1, v)
            cn = ys[:, t, 512:1024]
            v = VE.put(lambda e, cn=cn, bk=bk, mv=mv, r=r: e.tensor_scalar(cn, bank[bk], mv[:, 0:1], r, ALU.subtract,
                                                                           ALU.mult), tp, v)
            rel(free, bk, [v])
            yield
            w = yield from take(bk)
            w = [v, w]
            for k in range(4):
                tk = tr(bank[bk][:, 128 * k:128 * k + 128], cn[:, 128 * k:128 * k + 128], w, sig=(k == 3))
                w = []
            yield
            sl = ch[:, :, 0:128]
            for k in range(4):
                a = AC.put(lambda e, k=k, bk=bk, sl=sl: e.activation(
                    sl[:, k, :], bank[bk][:, 128 * k:128 * k + 128], ACT.Silu, bias=pcol("ln_b", k),
                    scale=pcol("ln_g", k)), tk, c_t.get("sl"))
            rel(free, bk, [a])
            hi_ = Bhi[:, 4:8, 128 * t:128 * t + 128]
            lo_2 = Blo[:, 4:8, 128 * t:128 * t + 128]
            a = AC.put(lambda e, hi_=hi_, sl=sl: e.copy(hi_, sl), a)
            v = VE.put(lambda e, hi_=hi_, lo_2=lo_2, sl=sl: e.tensor_tensor(lo_2, sl, hi_.bitcast(F32), ALU.subtract),
                       a)
            c_t["sl"] = v
            Y_t[t, 1] = [a, v]
            yield

    Y_t = {}
    q2_t = {}
    V2_t = {}
    qs = {}
    u2f = [[], []]

    def evac_q(qk):
        def fn(t, bk, tk, n):
            o = ust[:, 0, t, :]
            v = AC.put(lambda e: e.mul(o, bank[bk], r4_[:, t:t + 1]), tk, t_r4, u_free[0], u2f[t])
            free[bk] = [v]
            pending.insert(0, rope_task(qk, t, o, v))
        return fn

    tmp_f = [[]]

    def rope_task(qk, t, o, t_in):
        o3 = o.rearrange("p (h d) -> p h d", h=8)
        w1 = PT2[:, 0, 0:512]
        w2 = PT2[:, 1, 0:512]
        w13 = w1.rearrange("p (h d) -> p h d", h=8)
        w23 = w2.rearrange("p (h d) -> p h d", h=8)
        s8 = stat(8)
        _, wt = yield from slot(tmp_f)
        v = VE.put(lambda e: e.tensor_tensor(w1, o, o, ALU.mult), t_in, wt, t_gfree)
        v = VE.put(lambda e: e.tensor_reduce(s8, w13, AX.X, ALU.add), v)
        r, tp = rsqrt(s8, 8, 64, v)
        yield
        v = VE.put(lambda e: e.tensor_tensor(o3, o3, r.unsqueeze(2).broadcast_to([128, 8, 64]), ALU.mult), tp)
        of = (qk * 2 + t) * 64
        cA = RT[:, of:of + 64].unsqueeze(1).broadcast_to([128, 8, 64])
        sA = RT2[:, of:of + 32].unsqueeze(1).broadcast_to([128, 8, 32])
        sB = RT2[:, of + 32:of + 64].unsqueeze(1).broadcast_to([128, 8, 32])
        va = VE.put(lambda e: e.tensor_tensor(w13, o3, cA, ALU.mult), v, t_rt)
        VE.put(lambda e: e.tensor_tensor(w23[:, :, 0:32], o3[:, :, 32:64], sA, ALU.mult), v)
        vb = VE.put(lambda e: e.tensor_tensor(w23[:, :, 32:64], o3[:, :, 0:32], sB, ALU.mult), v)
        v = VE.put(lambda e: e.tensor_tensor(w1, w1, w2, ALU.add), va, vb)
        u2f[t] = [v]
        yield
        w = yield from take(5)
        w = [v, w]
        for k in range(4):
            tk = tr(bank[5][:, 128 * k:128 * k + 128], w1[:, 128 * k:128 * k + 128], w, sig=(k == 3))
            w = []
        rel(tmp_f, 0, [tk])
        dst = qk2T[:, 4 * qk:4 * qk + 4, 128 * t:128 * t + 128]
        a = AC.put(lambda e: e.mul(dst, bank[5].rearrange("p (k q) -> p k q", k=4), 0.125 if qk == 0 else 1.0), tk,
                   t_gfree)
        rel(free, 5, [a])
        q2_t[qk, t] = a

    def evac_v2(t, bk, tk, n):
        v = AC.put(lambda e: e.mul(V2[:, t, :], bank[bk], r4_[:, t:t + 1]), tk, t_r4)
        free[bk] = [v]
        V2_t[t] = v
        if t == 1:
            pending.extend(att2_task(h, qb) for h in range(8) for qb in range(2))

    S2_free = [[], []]
    y2_t = {}

    def att2_task(h, qb):
        kn = qb + 1
        m = 128 * kn
        while len(q2_t) < 4:
            yield
        bk, wb = yield from take_one(3, 4)
        Z = bank[bk]
        p = 64 * (h % 2)
        tk = mm(Z[:, 0:m], qk2T[p:p + 64, h // 2, 128 * qb:128 * qb + 128], qk2T[p:p + 64, 4 + h // 2, 0:m],
                True, True, wb, [q2_t[a, b_] for a in range(2) for b_ in range(2)])
        yield
        si, ws = yield from slot(S2_free)
        P = S2[:, si, 0:m]
        t = VE.put(lambda e: e.tensor_tensor(P, Z[:, 0:m], maskF[:, 256 - m:256], ALU.add), tk, ws)
        rel(free, bk, [t])
        i = cnt["S"] % 8
        cnt["S"] += 1
        nm, l = stat_m[i][:, 0:1], stat_s[i][:, 0:1]
        t = VE.put(lambda e: e.tensor_reduce(nm, P, AX.X, ALU.max, negate=True), t)
        te = AC.put(lambda e: e.activation(P, P, ACT.Exp, bias=nm, accum_out=l), t)
        yield
        vs = [V2[:, kb, 64 * h:64 * h + 64] for kb in range(kn)]

        def write(o, rl, w):
            y2_t[h, qb] = VE.put(lambda e: e.tensor_scalar(ys[:, qb, 64 * h:64 * h + 64], o, rl, None, ALU.mult), w,
                                 PE_last(PE))
            return y2_t[h, qb]

        yield from softmax_tail(P, None, PT2, kn, vs, [V2_t[0], V2_t[1]], l, te, write, si, S2_free)

    PT_free[0] = []
    PT_free[1] = []
    for i, us in enumerate(u_p2):
        ev2 = [evac_u(0), evac_u(1), evac_q(0), evac_q(1), evac_v2][i]
        chunk(us, Ahi, Alo, H2_t, ev2, first_of_phase=(i == 0))
    bg_all()

    for t in range(2):
        Y_t[t, 0] = turn_split(ys[:, t, 0:512], [y2_t[h, t] for h in range(8)], Bhi, Blo, 0, t, 5 + t)
    x3_t = out_proj(u_wo2, Bhi, Blo, Y_t, lambda: None)
    H3_t = norm_turn(x3_t, Ahi, Alo, lambda k: pcol("g_n2", k, 4))
    (r5_, t_r5), ta5 = x_stats(x3_t, ys, PE_last(PE))
    x_w = [[ta5], [ta5]]

    out_t = {}
    res = residual(out_t)
    o_v = out_d.rearrange("(t p) d -> p t d", p=128)
    nout = [0]

    def final(t, n, tk):
        res(t, n, tk)
        dma(o_v[:, t, 512 * n:512 * n + 512], xr[:, t, 512 * n:512 * n + 512], d_out, out_t[t, n])
        nout[0] += 16

    hid2 = {}
    gl = ys
    gl_free = {0: PE_last(PE), 1: PE_last(PE)}
    for j in range(6):
        n_ = HC2[j] * 128
        sg_t = {}
        m_t = {}

        def ev_g(t, bk, tk, n):
            a = AC.put(lambda e: e.activation(gl[:, t, 0:n], bank[bk][:, 0:n], ACT.Silu, scale=r5_[:, t:t + 1]),
                       tk, t_r5, gl_free[t], ta5)
            free[bk] = [a]
            sg_t[t] = a

        def ev_u(t, bk, tk, n, j=j):
            o = ust[:, j % 2, t, 0:n]
            v = VE.put(lambda e: e.scalar_tensor_tensor(out=o, in0=bank[bk][:, 0:n], scalar=r5_[:, t:t + 1],
                                                        in1=gl[:, t, 0:n], op0=ALU.mult, op1=ALU.mult),
                       tk, sg_t[t], t_r5, u_free[j % 2])
            free[bk] = [v]
            gl_free[t] = v
            m_t[t] = v

        up_product(u_g2[j], Ahi, Alo, H3_t, j == 0, ev_g)
        up_product(u_u2[j], Ahi, Alo, H3_t, False, ev_u)
        if j:
            ffn_down(u_d2, j - 1, None, hid2[j - 1], False)
        hid2[j] = {}
        for t in range(2):
            free[5 + t] = free[5 + t] + h_free[j % 2]
            hid2[j][t] = turn_split(ust[:, j % 2, t, 0:n_], m_t[t], hhi[:, j % 2], hlo[:, j % 2], 0, t, 5 + t,
                                    nk=HC2[j])
        u_free[j % 2] = [PE_last(PE)]
    ffn_down(u_d2, 5, final, hid2[5], True)

    block = ctx.enter_context(nc.Block())

    @block.sync
    def _(e):
        SP.play(e)
        e.wait_ge(d_out, nout[0])

    @block.tensor
    def _(e):
        PE.play(e)

    @block.scalar
    def _(e):
        AC.play(e)

    @block.vector
    def _(e):
        VE.play(e)

    @block.gpsimd
    def _(e):
        GP.play(e)


def PE_last(q):
    return (q.sem, q.n)


def _constants():
    import numpy as np

    q = np.arange(128)
    ident = np.eye(128, dtype=np.float32)
    tri = np.where(q[None, :] <= q[:, None], 0.0, NEG).astype(np.float32)
    maskF = np.concatenate([np.zeros((128, 128), np.float32), tri], axis=1)
    DDs = []
    for window, dil in ((128, 1), (512, 4), (2048, 16), (10 ** 9, 1)):
        blocks = []
        for qo, ko in ((0, 0), (128, 0), (128, 128)):
            dist = (q[:, None] + qo) - (q[None, :] + ko)
            ok = (dist >= 0) & (dist % dil == 0) & (dist <= window)
            blocks.append(np.where(ok, dist, 1e30).astype(np.float32))
        DDs.append(np.concatenate(blocks, axis=1))
    kk, qq = q[:, None], q[None, :]
    strict = np.where(kk < qq, 0.0, NEG).astype(np.float32)
    MB = np.concatenate([strict, np.zeros((128, 128), np.float32), strict], axis=1)
    UO = np.concatenate([(kk <= qq).astype(np.float32), np.ones((128, 128), np.float32)], axis=1)
    LG = (kk >= qq).astype(np.float32)
    return np.ascontiguousarray(np.concatenate([ident, maskF] + DDs + [MB, UO, LG], axis=1), dtype=np.float32)


def _rope():
    import numpy as np

    pos = np.arange(256, dtype=np.float32)
    inv = np.power(np.float32(10000.0), -np.arange(0, 64, 2, dtype=np.float32) / np.float32(64)).astype(np.float32)
    ang = (pos[:, None] * inv[None, :]).astype(np.float32)
    cos, sin = np.cos(ang).astype(np.float32), np.sin(ang).astype(np.float32)
    c = np.concatenate([cos, cos], axis=1)
    s = np.concatenate([-sin, sin], axis=1)
    lay = lambda a: a.reshape(2, 128, 64).transpose(1, 0, 2).reshape(128, 128)
    return lay(c), lay(s)


def kernel(**inputs):
    import numpy as np
    import concourse.bacc as bacc
    from concourse.bass_utils import run_bass_kernel_spmd

    a = {k: np.asarray(v) for k, v in inputs.items()}
    col = lambda v, n: v.reshape(n, 128).T
    row = lambda v: np.broadcast_to(v.reshape(1, -1), (128, v.size))
    dw = a["dw_w_2"][0].reshape(31, 4, 128).transpose(2, 1, 0).reshape(128, 124)
    par = np.concatenate([
        col(a["mix_norm_g"], 8), col(a["mlp_norm_g"], 8), col(a["final_norm_g"], 8), col(a["norm1_g_2"], 8),
        col(a["norm2_g_2"], 8), col(a["glu_b_2"], 8), dw, col(a["dw_b_2"], 4), col(a["conv_ln_g_2"], 4),
        col(a["conv_ln_b_2"], 4), row(a["b_forget"]), row(a["lambda_q1"]), row(a["lambda_q2"]),
        row(a["lambda_k1"]), row(a["lambda_k2"]), row(a["diff_norm_g"])], axis=1)
    cosT, sinT = _rope()
    par2 = np.concatenate([row(a["final_norm_g"]), row(a["q_norm_g_2"]), row(a["k_norm_g_2"]), cosT, sinT], axis=1)
    arrays = {
        "x": a["x"][0], "w_in": a["w_in"][0], "w_br": a["w_branch"][0].reshape(1024, 1024), "w_out": a["w_out"][0],
        "w_up": a["w_up"][0], "w_dn": a["w_down"][0], "w_in2": a["w_in_2"][0], "w_out2": a["w_out_2"][0],
        "w_g2": a["w_gate_2"][0], "w_u2": a["w_up_2"][0], "w_d2": a["w_down_2"][0],
        "par": par, "par2": par2, "cst": _constants(),
    }
    nc = bacc.Bacc("TRN2", target_bir_lowering=False, num_devices=1)
    args, ins = [], {}
    for name, v in arrays.items():
        v = np.ascontiguousarray(v)
        ins["in_" + name] = v
        args.append(nc.dram_tensor("in_" + name, v.shape, mybir.dt.from_np(v.dtype), kind="ExternalInput").ap())
    args.append(nc.dram_tensor("out_0", (S, D), F32, kind="ExternalOutput").ap())
    program(nc, *args)
    r = run_bass_kernel_spmd(nc, [ins], core_ids=[0])
    return r.results[0]["out_0"].reshape(1, S, D)
```

```python
import concourse.bass as bass
from concourse import mybir
from contextlib import ExitStack

F32 = mybir.dt.float32
F32R = mybir.dt.float32r
ALU = mybir.AluOpType
ACT = mybir.ActivationFunctionType
AX = mybir.AxisListType

D = 1024
S = 256
EPS = 1e-6
DFF1 = 4096
DFF2 = 2816
NRAW = 4
NSPL = 3
LEAD = 2
NEG = -1e30

SLOPES = [2.0 ** (-8.0 * i / 16) for i in range(1, 17)]
SL_DIL = [SLOPES[0:4], SLOPES[8:12], SLOPES[12:16]]
SL_DIFF = SLOPES[4:8]

PAR = {}
CST = {}


def _layout():
    n = 0
    for name, w in (("g_mix", 8), ("g_mlp", 8), ("g_fin", 8), ("g_n1", 8), ("g_n2", 8), ("glu_b", 8),
                    ("dw_w", 124), ("dw_b", 4), ("ln_g", 4), ("ln_b", 4), ("b_f", 4), ("lam", 128),
                    ("g_diff", 64)):
        PAR[name] = (n, w)
        n += w
    PAR["_n"] = n
    n = 0
    for name, w in (("ident", 128), ("maskF", 256)):
        CST[name] = (n, w)
        n += w
    CST["_n0"] = n
    n = 0
    for name, w in (("DD", 1536), ("MB", 384), ("UO", 256), ("LG", 128)):
        CST[name] = (n, w)
        n += w
    CST["_n1"] = n
    return


_layout()


class Queue:

    def __init__(self, sem):
        self.sem = sem
        self.n = 0
        self.items = []

    def put(self, fn, *waits, sig=True):
        flat = []
        todo = list(waits)
        while todo:
            w = todo.pop(0)
            if isinstance(w, list):
                todo = w + todo
            elif w is not None:
                flat.append(w)
        if sig:
            self.n += 1
        self.items.append((fn, flat, sig))
        return (self.sem, self.n)

    def play(self, eng):
        seen = {}
        for fn, waits, sig in self.items:
            for sem, v in waits:
                if seen.get(sem, 0) < v:
                    eng.wait_ge(sem, v)
                    seen[sem] = v
            ins = fn(eng)
            if sig:
                ins.then_inc(self.sem, 1)


def program(nc, x_d, w_in, w_br, w_out, w_up, w_dn, w_in2, w_out2, w_g2, w_u2, w_d2, par_d, par2_d, cst_d, out_d):
    with ExitStack() as ctx:
        build(nc, ctx, x_d, w_in, w_br, w_out, w_up, w_dn, w_in2, w_out2, w_g2, w_u2, w_d2, par_d, par2_d,
              cst_d, out_d)


def build(nc, ctx, x_d, w_in, w_br, w_out, w_up, w_dn, w_in2, w_out2, w_g2, w_u2, w_d2, par_d, par2_d, cst_d, out_d):
    def sem(name):
        return ctx.enter_context(nc.semaphore(name))

    def sb(name, shape, dt=F32, c=ctx):
        return c.enter_context(nc.sbuf_tensor(name, shape, dt))

    NPAR = PAR["_n"]
    N0, N1 = CST["_n0"], CST["_n1"]
    raw = sb("raw", [128, NRAW, 2048])
    whi = sb("whi", [128, NSPL, 2048], F32R)
    wlo = sb("wlo", [128, NSPL, 2048], F32R)
    xr = sb("xr", [128, 2, D])
    Ahi = sb("Ahi", [128, 8, S], F32R)
    Alo = sb("Alo", [128, 8, S], F32R)
    ys = sb("ys", [128, 2, D])
    par = sb("par", [128, NPAR])
    cst = sb("cst", [128, N0])
    st = sb("st", [128, 384])
    with ExitStack() as r1:
        qkA = sb("qkA", [128, 16, S], c=r1)
    with ExitStack() as r2:
        Bhi = sb("Bhi", [128, 8, S], F32R, c=r2)
        Blo = sb("Blo", [128, 8, S], F32R, c=r2)
        gap = ExitStack()
        gates = sb("gates", [128, 2, 4096], c=gap)
        r1 = ExitStack()
        qkB = sb("qkB", [128, 8, S], c=r1)
        V = sb("V", [128, 2, 1536], c=r1)
        Sb = sb("Sb", [128, 2, 768], c=r1)
        PT = sb("PT", [128, 2, 768], c=r1)
        cs1 = sb("cs1", [128, N1], c=r1)
        nlf = sb("nlf", [128, 2, 128], c=r1)
        nsq = sb("nsq", [128, 256], c=r1)
        r1.close()
        r3 = ExitStack()
        hhi = sb("hhi", [128, 2, 4, S], F32R, c=r3)
        hlo = sb("hlo", [128, 2, 4, S], F32R, c=r3)
        ust = sb("ust", [128, 2, 2, 512], c=r3)
        V2 = sb("V2", [128, 2, 512], c=r3)
        tg = sb("tg", [128, 2, 512], c=r3)
        cv = sb("cv", [128, 6, S], c=r3)
        r3.close()
        gap.close()
        g2 = ExitStack()
        qk2T = sb("qk2T", [128, 8, S], c=g2)
        par2 = sb("par2", [128, 1024 + 128 + 256], c=g2)
        ch = sb("ch", [128, 4, 288], c=g2)
        ca = sb("ca", [128, 4, S], c=g2)
        PT2 = sb("PT2", [128, 2, 512], c=g2)
        S2 = sb("S2", [128, 3, 384], c=g2)
        g2.close()

    b = [ctx.enter_context(nc.psum_tensor(f"b{i}", [128, 512], F32)) for i in range(3)]
    SS = ctx.enter_context(nc.psum_tensor("SS", [128, 1024], F32))
    TT = ctx.enter_context(nc.psum_tensor("TT", [128, 1024], F32))
    OO = ctx.enter_context(nc.psum_tensor("OO", [128, 512], F32))
    bank = {0: b[0][:], 1: b[1][:], 2: b[2][:], 3: SS[:, 0:512], 4: SS[:, 512:1024],
            5: TT[:, 0:512], 6: TT[:, 512:1024], 7: OO[:]}
    free = {i: [] for i in range(8)}

    PE = Queue(sem("s_pe"))
    AC = Queue(sem("s_act"))
    VE = Queue(sem("s_dve"))
    GP = Queue(sem("s_pool"))
    SP = Queue(sem("s_sp"))
    d_raw = [sem(f"d_raw{i}") for i in range(NRAW)]
    d_x = sem("d_x")
    d_par = sem("d_par")
    d_cst = sem("d_cst")
    d_cs1 = sem("d_cs1")
    d_par2 = sem("d_par2")
    d_out = sem("d_out")

    def dma(dst, src, s, *waits):
        def fn(e):
            e.dma_start(dst, src).then_inc(s, 16)
        SP.put(fn, *waits, sig=False)

    def pcol(name, i=0, n=1):
        o, w = PAR[name]
        return par[:, o + i:o + i + n]

    ident = cst[:, 0:128]
    maskF = cst[:, 128:384]

    def c1(name, a=0, n=None):
        o, w = CST[name]
        return cs1[:, o + a:o + a + (w - a if n is None else n)]

    _st = [0]

    def stat(n=1):
        a = _st[0]
        _st[0] += n
        assert _st[0] <= 384
        return st[:, a:a + n]

    units = []

    def add_unit(src, k0, kn, c0, n):
        v = src[k0 * 128:(k0 + kn) * 128, c0:c0 + n].rearrange("(k p) n -> p k n", p=128)
        units.append((v, kn, n))
        return len(units) - 1

    CH1 = [(0, 512), (512, 512), (1024, 512), (1536, 512), (2048, 512), (2560, 512), (3072, 512),
           (3584, 260), (3844, 512), (4356, 256)] + [(4612 + 512 * i, 512) for i in range(8)]
    u_p1 = [[add_unit(w_in, 0, 4, c, n), add_unit(w_in, 4, 4, c, n)] for c, n in CH1]
    u_br = [[add_unit(w_br, 4 * p, 4, 512 * h, 512) for p in range(2)] for h in range(2)]
    u_wo = [[add_unit(w_out, 4 * k, 4, 512 * n, 512) for n in range(2)] for k in range(2)]
    u_up, u_dn = {}, {}

    def plan_down(tab, w, j, kn):
        if kn == 4:
            tab[j] = [add_unit(w, 4 * j, 4, 512 * n, 512) for n in range(2)]
        else:
            tab[j] = [add_unit(w, 4 * j, kn, 0, 1024)]

    for j in range(8):
        u_up[j] = [add_unit(w_up, 4 * k, 4, 512 * j, 512) for k in range(2)]
        if j:
            plan_down(u_dn, w_dn, j - 1, 4)
    plan_down(u_dn, w_dn, 7, 4)
    CH2 = [(2048, 512), (1536, 512), (0, 512), (512, 512), (1024, 512)]
    u_p2 = [[add_unit(w_in2, 4 * k, 4, c, n) for k in range(2)] for c, n in CH2]
    u_wo2 = [[add_unit(w_out2, 4 * k, 4, 512 * n, 512) for n in range(2)] for k in range(2)]
    u_g2, u_u2, u_d2 = {}, {}, {}
    HC2 = [4, 4, 4, 4, 4, 2]
    for j in range(6):
        n = HC2[j] * 128
        u_g2[j] = [add_unit(w_g2, 4 * k, 4, 512 * j, n) for k in range(2)]
        u_u2[j] = [add_unit(w_u2, 4 * k, 4, 512 * j, n) for k in range(2)]
        if j:
            plan_down(u_d2, w_d2, j - 1, HC2[j - 1])
    plan_down(u_d2, w_d2, 5, 2)

    nu = len(units)
    hi_t, lo_t, pe_t = [None] * nu, [None] * nu, [None] * nu
    nxt = {"dma": 0, "split": 0}

    def load(i):
        v, kn, n = units[i]
        s = i % NRAW
        w = [hi_t[i - NRAW], lo_t[i - NRAW]] if i >= NRAW else []
        dma(raw[:, s, 0:kn * n].rearrange("p (k n) -> p k n", k=kn), v, d_raw[s], w)

    def split_hi(i):
        v, kn, n = units[i]
        s, r = i % NSPL, i % NRAW
        m = kn * n
        landed = (d_raw[r], 16 * (i // NRAW + 1))
        old = pe_t[i - NSPL] if i >= NSPL else None
        hi_t[i] = AC.put(lambda e: e.copy(whi[:, s, 0:m], raw[:, r, 0:m]), landed, old)

    def split_lo(i):
        v, kn, n = units[i]
        s, r = i % NSPL, i % NRAW
        m = kn * n
        landed = (d_raw[r], 16 * (i // NRAW + 1))
        lo_t[i] = VE.put(lambda e: e.tensor_tensor(wlo[:, s, 0:m], raw[:, r, 0:m], whi[:, s, 0:m].bitcast(F32),
                                                   ALU.subtract), landed, hi_t[i])
        if nxt["dma"] < nu:
            load(nxt["dma"])
            nxt["dma"] += 1

    def prefetch(i):
        lows()
        while nxt["split"] < min(nu, i + LEAD):
            split_hi(nxt["split"])
            lo_due.append(nxt["split"])
            nxt["split"] += 1

    lo_due = []

    def lows():
        while lo_due:
            split_lo(lo_due.pop(0))

    def mm_unit(i, hi, lo, k0, t, out_of, first, last, waits, done, kr=None):
        lows()
        v, kn, n = units[i]
        s = i % NSPL
        H = whi[:, s, 0:kn * n].rearrange("p (k n) -> p k n", k=kn)
        L = wlo[:, s, 0:kn * n].rearrange("p (k n) -> p k n", k=kn)
        ws = [hi_t[i], lo_t[i]] + list(waits)
        krs = list(range(kn)) if kr is None else list(kr)
        tok = None
        for c0 in range(0, n, 512):
            c1_ = min(n, c0 + 512)
            for kc in krs:
                dst = out_of(kc, c0)
                xh = hi[:, k0 + kc, t * 128:(t + 1) * 128]
                xl = lo[:, k0 + kc, t * 128:(t + 1) * 128]
                f = first(kc)
                for q, (a, w) in enumerate(((xh, H), (xh, L), (xl, H))):
                    tok = PE.put(_mm(dst, a, w[:, kc, c0:c1_], f and q == 0, last(kc) and q == 2), ws,
                                 sig=(kc == krs[-1] and q == 2 and c1_ == n))
                    ws = []
        if done:
            pe_t[i] = tok
        return tok

    def _mm(dst, a, w, start, stop):
        return lambda e: e.matmul(dst, a, w, start=start, stop=stop)

    def mm(dst, lhsT, rhs, start, stop, *waits, sig=True):
        return PE.put(_mm(dst, lhsT, rhs, start, stop), *waits, sig=sig)

    def tr(dst, src, *waits, sig=True):
        return PE.put(lambda e: e.transpose(dst, src, ident), *waits, sig=sig)

    active, pending = [], []
    cnt = {"O": 0, "S": 0, "P": 0, "B": 0, "T": 0}
    tg_free = [None, None]
    tgbuf = [PT]

    freed = []

    def rel(tab, k, toks):
        freed.append((tab, k, toks))

    def bg(start=1):
        for g in list(active):
            if next(g, "end") == "end":
                active.remove(g)
        for _ in range(start):
            if pending:
                g = pending.pop(0)
                if next(g, "end") != "end":
                    active.append(g)
        while freed:
            tab, k, toks = freed.pop(0)
            tab[k] = toks

    def bg_all():
        late()
        while active or pending:
            bg()

    def take(*bks):
        while any(free[k] is None for k in bks):
            yield
        w = [free[k] for k in bks]
        for k in bks:
            free[k] = None
        return w

    def take_one(*bks):
        while all(free[k] is None for k in bks):
            yield
        k = next(k for k in bks if free[k] is not None)
        w = free[k]
        free[k] = None
        return k, w

    def slot(frees):
        while all(f is None for f in frees):
            yield
        i = next(i for i, f in enumerate(frees) if f is not None)
        w = frees[i]
        frees[i] = None
        return i, w

    dma(xr[:], x_d.rearrange("(t p) d -> p t d", p=128), d_x)
    dma(cst[:], cst_d[:, 0:N0], d_cst)
    dma(par[:], par_d, d_par)
    for i in range(NRAW):
        load(i)
        nxt["dma"] += 1
    dma(cs1[:], cst_d[:, N0:N0 + N1], d_cs1)
    T_X, T_PAR, T_CST, T_CS1 = (d_x, 16), (d_par, 16), (d_cst, 16), (d_cs1, 16)

    mhalf = stat(16)
    t_mh = GP.put(lambda e: e.memset(mhalf, -0.5))

    def rsqrt(src, n, count, t_src):
        v = stat(n)
        r = stat(n)
        a = VE.put(lambda e: e.tensor_scalar(v, src, 1.0 / count, EPS, ALU.mult, ALU.add), t_src)
        c = GP.put(lambda e: e.tensor_tensor(r, v, mhalf[:, 0:n], ALU.pow), a, t_mh)
        return r, c

    def sumsq(src, t_src, junk):
        o = stat(1)
        t = AC.put(lambda e: e.activation(junk, src, ACT.Square, accum_out=o), t_src)
        return o, t

    def turn_split(src, t_src, hi, lo, kc0, t, bk, gain=None, nk=4, post=None):
        w = [t_src, T_CST] + free[bk]
        for k in range(nk):
            tk = tr(bank[bk][:, 128 * k:128 * k + 128], src[:, 128 * k:128 * k + 128], w, sig=(k == nk - 1))
            w = []
        ph = hi[:, kc0:kc0 + nk, t * 128:(t + 1) * 128]
        pl = lo[:, kc0:kc0 + nk, t * 128:(t + 1) * 128]
        ps = bank[bk][:, 0:128 * nk].rearrange("p (k q) -> p k q", k=nk)
        if gain is None:
            a = AC.put(lambda e: e.copy(ph, ps), tk)
            v = VE.put(lambda e: e.tensor_tensor(pl, ps, ph.bitcast(F32), ALU.subtract), a)
        else:
            i = cnt["T"] % 2
            cnt["T"] += 1
            w = tgbuf[0][:, i, 0:128 * nk].rearrange("p (k q) -> p k q", k=nk)
            m = VE.put(lambda e: e.tensor_tensor(w, ps, gain(kc0).unsqueeze(2).broadcast_to([128, nk, 128]), ALU.mult),
                       tk, T_PAR, tg_free[i])
            a = AC.put(lambda e: e.copy(ph, w), m)
            v = VE.put(lambda e: e.tensor_tensor(pl, w, ph.bitcast(F32), ALU.subtract), a)
            tg_free[i] = v
            free[bk] = [m]
            return [a, v]
        free[bk] = [a, v]
        return [a, v]

    prefetch(0)
    A_t = {}
    for t in range(2):
        for h in range(2):
            A_t[t, h] = turn_split(xr[:, t, 512 * h:512 * h + 512], T_X, Ahi, Alo, 4 * h, t, 5 + h,
                                   gain=lambda k: pcol("g_mix", k, 4))
    ss1 = stat(2)
    tq = None
    for t in range(2):
        tq = AC.put(lambda e, t=t: e.activation(ys[:, t, :], xr[:, t, :], ACT.Square, accum_out=ss1[:, t:t + 1]), T_X)
    r1_, t_r1 = rsqrt(ss1, 2, D, tq)

    lamt = stat(2)
    lame = stat(2)
    lam = stat(1)
    nlam = stat(1)
    lo_, _ = PAR["lam"]
    lscr = stat(64)
    ta = VE.put(lambda e: e.tensor_tensor(lscr, par[:, lo_:lo_ + 64], par[:, lo_ + 64:lo_ + 128], ALU.mult), T_PAR)
    ta = VE.put(lambda e: e.tensor_reduce(lamt, lscr.rearrange("p (a b) -> p a b", a=2), AX.X, ALU.add), ta)
    ta = AC.put(lambda e: e.activation(lame, lamt, ACT.Exp), ta)
    ta = VE.put(lambda e: e.tensor_tensor(lam, lame[:, 0:1], lame[:, 1:2], ALU.subtract), ta)
    t_nlam = VE.put(lambda e: e.tensor_scalar(nlam, lam, -1.0, -0.2, ALU.mult, ALU.add), ta)

    rot = [0]
    later = []

    def late():
        while later:
            later.pop(0)()

    def chunk(us, hi, lo, src_t, evac, first_of_phase=False, start=1):
        n = units[us[0]][2]
        bks = []
        for t in range(2):
            bks.append(rot[0] % 2)
            rot[0] += 1
        order = [(0, 0), (1, 0), (0, 1), (1, 1)] if first_of_phase else [(0, 0), (0, 1), (1, 0), (1, 1)]
        for ui, t in order:
            bk = bks[t]
            w = list(src_t[t, ui])
            if ui == 0:
                w += free[bk]
                free[bk] = []
            tk = mm_unit(us[ui], hi, lo, 4 * ui, t, lambda kc, c0, bk=bk: bank[bk][:, 0:n],
                         lambda kc, ui=ui: ui == 0 and kc == 0, lambda kc, ui=ui: ui == 1 and kc == 3, w, t == 1)
            if t == 1:
                prefetch(us[ui] + 1)
            late()
            if ui == 1:
                later.append(lambda t=t, bk=bk, tk=tk: evac(t, bk, tk, n))
            bg(start)

    qk_t = {}
    V_t = {}
    PAIRS = {0: [(0, "qk", 0, 0.125), (256, "qk", 2, 1.0)],
             1: [(0, "v", 0, None), (256, "qk", 4, 0.125)],
             2: [(0, "qk", 6, 0.125), (256, "qk", 8, 0.125)],
             3: [(0, "qk", 10, 1.0), (256, "qk", 12, 1.0)],
             4: [(0, "qk", 14, 1.0), (256, "v", 256, None)],
             5: [(0, "v", 512, None), (256, "v", 768, None)],
             6: [(0, "qk", 16, 0.125), (256, "qk", 18, 1.0)],
             7: [(0, "v", 1024, None)],
             8: [(0, "qk", 20, 32 ** -0.5), (256, "qk", 22, 1.0)],
             9: [(0, "v", 1280, None)]}
    f_t = {}
    ff = stat(8)
    stage_free = {5: [], 7: [], 9: []}

    def qk_tile(i):
        return qkA[:, i, :] if i < 16 else qkB[:, i - 16, :]

    def turn_pairs(c, t_stage):
        sg = gates[:, :, 1024 + 512 * (c % 6):1536 + 512 * (c % 6)]
        done = []
        for col, kind, dst, sc in PAIRS[c]:
            if kind != "qk":
                continue
            bk = 5 + (dst // 2) % 2
            w = yield from take(bk)
            w = [t_stage[0], t_stage[1], w]
            for j in range(2):
                for t in range(2):
                    tk = tr(bank[bk][:, 256 * j + 128 * t:256 * j + 128 * t + 128],
                            sg[:, t, col + 128 * j:col + 128 * j + 128], w, sig=(j == 1 and t == 1))
                    w = []
            done.append(tk)
            yield
            q = qkA[:, dst:dst + 2, :] if dst < 16 else qkB[:, dst - 16:dst - 14, :]
            src = bank[bk].rearrange("p (j q) -> p j q", j=2)
            if (dst // 2) % 2 == 0:
                tv = VE.put(lambda e, q=q, src=src, sc=sc: e.tensor_scalar(q, src, sc, None, ALU.mult), tk)
            else:
                tv = AC.put(lambda e, q=q, src=src, sc=sc: e.mul(q, src, sc), tk)
            rel(free, bk, [tv])
            qk_t[dst] = qk_t[dst + 1] = tv
        stage_free[c] = [done[-1]]

    def evac1(c):
        def fn(t, bk, tk, n):
            ts = []
            for col, kind, dst, sc in PAIRS[c]:
                if kind == "v":
                    o = V[:, t, dst:dst + 256]
                    w = []
                else:
                    a = 1024 + 512 * (c % 6) + col
                    o = gates[:, t, a:a + 256]
                    w = stage_free[c - 6] if c >= 6 else []
                tv = AC.put(lambda e, o=o, col=col: e.mul(o, bank[bk][:, col:col + 256], r1_[:, t:t + 1]), tk, t_r1, w)
                if kind == "v":
                    V_t[dst, t] = tv
                else:
                    stg[c, t] = tv
                ts.append(tv)
            if c == 7:
                tv = VE.put(lambda e: e.scalar_tensor_tensor(
                    out=ff[:, 4 * t:4 * t + 4], in0=bank[bk][:, 256:260], scalar=r1_[:, t:t + 1],
                    in1=pcol("b_f", 0, 4), op0=ALU.mult, op1=ALU.add), tk, tv, t_r1, T_PAR)
                f_t[t] = tv
                ts.append(tv)
            free[bk] = ts
            if t == 1 and any(k == "qk" for _, k, _, _ in PAIRS[c]):
                active.insert(0, turn_pairs(c, [stg[c, 0], stg[c, 1]]))
            if t == 1:
                if c == 1:
                    pending.extend(sb_task(h) for h in range(4))
                if c == 5:
                    pending.extend(dil_task(h, qb) for h in range(4) for qb in range(2))
                if c == 7:
                    pending.append(forget_gates())
                    pending.extend(fox_task(h, qb) for h in range(4) for qb in range(2))
                if c == 9:
                    for h_ in range(4):
                        pending.extend(diff_task(h_, qb) for qb in range(2))
                        if h_ == 1:
                            pending.extend(turn_task(ys[:, t_, 0:512], [(a_, i_, t_) for a_ in (0, 1) for i_ in range(4)],
                                                     Bhi, Blo, 0, t_, B_t, [(2, 0, 0)]) for t_ in range(2))
                    for t_ in range(2):
                        pending.append(diff_norm(t_))
                        pending.append(turn_task(ys[:, t_, 512:1024], [(2, h_, t_) for h_ in range(4)] + [("d", t_)],
                                                 Bhi, Blo, 4, t_, B_t))
        return fn

    stg = {}
    Sb_free = [[], []]
    PT_free = [[tg_free[0]], [tg_free[1]]]
    ys_t = {}

    def sb_task(h):
        qt, kt, p = h // 2, 2 + h // 2, 64 * (h % 2)
        Q, K = qkA[p:p + 64, qt, :], qkA[p:p + 64, kt, :]
        while kt not in qk_t:
            yield
        bk, wb = yield from take_one(3, 4)
        Z = bank[bk]
        mm(Z[:, 0:256], K[:, 0:128], Q[:, 0:256], True, True, qk_t[qt], qk_t[kt], wb, sig=False)
        tz = mm(Z[:, 256:384], K[:, 128:256], Q[:, 128:256], True, True)
        yield
        si, ws = yield from slot(Sb_free)
        zm, L = Sb[:, si, 0:384], Sb[:, si, 384:768]
        t = VE.put(lambda e: e.tensor_tensor(zm, Z[:, 0:384], c1("MB"), ALU.add), tz, T_CS1, ws)
        rel(free, bk, [t])
        a = AC.put(lambda e: e.activation(L, zm, ACT.Abs), t)
        a = AC.put(lambda e: e.activation(L, L, ACT.Exp, scale=-1.0), a)
        a = AC.put(lambda e: e.activation(L, L, ACT.Ln, bias=1.0), a)
        yield
        t = VE.put(lambda e: e.scalar_tensor_tensor(out=L, in0=zm, scalar=0.0, in1=L, op0=ALU.max, op1=ALU.add), a)
        yield
        bk, wb = yield from take_one(5, 6)
        R = bank[bk]
        mm(R[:, 0:384], c1("LG"), L, True, False, t, wb, sig=False)
        tr_ = mm(R[:, 128:256], c1("UO", 128, 128), L[:, 256:384], False, True)
        yield
        t = VE.put(lambda e: e.tensor_tensor(zm, zm, R[:, 0:384], ALU.subtract), tr_)
        rel(free, bk, [t])
        a = AC.put(lambda e: e.activation(zm, zm, ACT.Exp), t)
        yield
        ob, wo = yield from take_one(2, 7)
        o0, o1 = bank[ob][:, 0:64], bank[ob][:, 64:128]
        v = V[:, :, 64 * h:64 * h + 64]
        t0 = mm(o0, zm[:, 0:128], v[:, 0, :], True, True, a, V_t[0, 0], V_t[0, 1], wo)
        mm(o1, zm[:, 128:256], v[:, 0, :], True, False, sig=False)
        t1 = mm(o1, zm[:, 256:384], v[:, 1, :], False, True)
        rel(Sb_free, si, [t1])
        yield
        for qb, o in ((0, o0), (1, o1)):
            ys_t[0, h, qb] = VE.put(
                lambda e, qb=qb, o=o: e.tensor_copy(ys[:, qb, 64 * h:64 * h + 64], o), t1, tq)
        rel(free, ob, [ys_t[0, h, 1]])

    def softmax_tail(P, segs, ptr, kn, vs, vw, l, t_exp, write, si, sfree):
        n = len(vs)
        if n > 4:
            wb = yield from take(5, 6)
            bt, T = 5, TT
        else:
            bt, wb = yield from take_one(5, 6)
            T = bank[bt]
        w = [t_exp, wb]
        for j in range(n):
            tk = tr(T[:, 128 * j:128 * j + 128], P[:, 128 * j:128 * j + 128], w, sig=(j == n - 1))
            w = []
        rel(sfree, si, [tk])
        yield
        m = 128 * n
        pi, wp = yield from slot(PT_free)
        te = AC.put(lambda e: e.copy(ptr[:, pi, 0:m], T[:, 0:m]), tk, wp)
        rel(free, bt, [te])
        if n > 4:
            rel(free, 6, [te])
        rl = stat_l[cnt["P"] % 8]
        cnt["P"] += 1
        trl = VE.put(lambda e: e.reciprocal(rl, l), t_exp)
        yield
        ob, wo = yield from take_one(2, 7)
        o = bank[ob][:, 0:64]
        w = [te, vw, wo]
        for j in range(n):
            tk = mm(o, ptr[:, pi, 128 * j:128 * j + 128], vs[j], j == 0, j == n - 1, w, sig=(j == n - 1))
            w = []
        rel(PT_free, pi, [tk])
        yield
        rel(free, ob, [write(o, rl, [tk, trl])])

    stat_l = [stat(1) for _ in range(8)]
    stat_m = [stat(2) for _ in range(8)]
    stat_s = [stat(2) for _ in range(8)]

    def dil_task(h, qb):
        kn = qb + 1
        m = 128 * kn
        off = 0 if qb == 0 else 128
        while 14 not in qk_t:
            yield
        w = yield from take(3, 4)
        w = [w] + [qk_t[i] for i in (4, 6, 8, 10, 12, 14)]
        p = 64 * (h % 2)
        for g in range(3):
            q, k = 4 + 2 * g + h // 2, 10 + 2 * g + h // 2
            tk = mm(SS[:, m * g:m * g + m], qkA[p:p + 64, q, 128 * qb:128 * qb + 128], qkA[p:p + 64, k, 0:m],
                    True, True, w, sig=(g == 2))
            w = []
        yield
        si, ws = yield from slot(Sb_free)
        P = Sb[:, si, 0:3 * m]
        for g in range(3):
            t = VE.put(lambda e, g=g: e.scalar_tensor_tensor(
                out=P[:, m * g:m * g + m], in0=c1("DD", 384 * g + off, m), scalar=-SL_DIL[g][h],
                in1=SS[:, m * g:m * g + m], op0=ALU.mult, op1=ALU.add), tk, T_CS1, ws)
        rel(free, 3, [t])
        rel(free, 4, [t])
        i = cnt["S"] % 8
        cnt["S"] += 1
        nm, l = stat_m[i][:, 0:1], stat_s[i][:, 0:1]
        t = VE.put(lambda e: e.tensor_reduce(nm, P, AX.X, ALU.max, negate=True), t)
        te = AC.put(lambda e: e.activation(P, P, ACT.Exp, bias=nm, accum_out=l), t)
        yield
        vs = [V[:, kb, 256 + 256 * g + 64 * h:320 + 256 * g + 64 * h] for g in range(3) for kb in range(kn)]
        vw = [V_t[256 * g, t_] for g in (1, 2, 3) for t_ in range(2)]

        def write(o, rl, w):
            ys_t[1, h, qb] = VE.put(lambda e: e.tensor_scalar(ys[:, qb, 256 + 64 * h:320 + 64 * h], o, rl, None,
                                                              ALU.mult), w)
            return ys_t[1, h, qb]

        yield from softmax_tail(P, None, PT, kn, vs, vw, l, te, write, si, Sb_free)

    cumq = stat(8)
    lf = stat(8)
    fox = {}

    def forget_gates():
        e1 = stat(8)
        a = AC.put(lambda e: e.activation(e1, ff, ACT.Abs), f_t[0], f_t[1])
        a = AC.put(lambda e: e.activation(e1, e1, ACT.Exp, scale=-1.0), a)
        a = AC.put(lambda e: e.activation(e1, e1, ACT.Ln, bias=1.0), a)
        yield
        t = VE.put(lambda e: e.scalar_tensor_tensor(out=lf, in0=ff, scalar=0.0, in1=e1, op0=ALU.min,
                                                    op1=ALU.subtract), a)
        fox["lf"] = t
        yield
        ob, wo = yield from take_one(2, 7)
        o0, o1 = bank[ob][:, 0:64], bank[ob][:, 64:128]
        mm(o0[:, 0:4], c1("UO", 0, 128), lf[:, 0:4], True, True, t, T_CS1, wo, sig=False)
        mm(o1[:, 0:4], c1("UO", 128, 128), lf[:, 0:4], True, False, sig=False)
        tk = mm(o1[:, 0:4], c1("UO", 0, 128), lf[:, 4:8], False, True)
        yield
        VE.put(lambda e: e.tensor_copy(cumq[:, 0:4], o0[:, 0:4]), tk)
        fox["cq"] = VE.put(lambda e: e.tensor_copy(cumq[:, 4:8], o1[:, 0:4]), tk)
        rel(free, ob, [fox["cq"]])

    nlf_free = [[]]

    def fox_task(h, qb):
        while "cq" not in fox or (qb == 1 and ("b", h, 1) not in fox):
            yield
        if qb == 0:
            _, wn = yield from slot(nlf_free)
            for t_ in range(2):
                src = lf[:, 4 * t_ + h:4 * t_ + h + 1]
                fox["b", h, t_] = VE.put(lambda e, src=src, t_=t_: e.tensor_scalar(
                    nlf[:, t_, :], c1("UO", 128, 128), src, -1.0, ALU.mult, ALU.mult), fox["lf"], wn, T_CS1)
            yield
        kn = qb + 1
        m = 128 * kn
        while 18 not in qk_t:
            yield
        bk, wb = yield from take_one(3, 4)
        Z = bank[bk]
        p = 64 * (h % 2)
        q, k = h // 2, 2 + h // 2
        mm(Z[:, 0:m], qkB[p:p + 64, q, 128 * qb:128 * qb + 128], qkB[p:p + 64, k, 0:m], True, False,
           wb, qk_t[16], qk_t[18], sig=False)
        tk = mm(Z[:, 0:m], nlf[:, 0, :], c1("UO", 0, m), False, qb == 0, fox["b", h, 0], fox["b", h, 1])
        if qb == 1:
            tk = mm(Z[:, 128:256], nlf[:, 1, :], c1("UO", 0, 128), False, True)
        fox["r", h, qb] = tk
        if ("r", h, 1 - qb) in fox:
            rel(nlf_free, 0, [fox["r", h, 0], fox["r", h, 1]])
        yield
        si, ws = yield from slot(Sb_free)
        P = Sb[:, si, 0:m]
        t = VE.put(lambda e: e.scalar_tensor_tensor(
            out=P, in0=Z[:, 0:m], scalar=cumq[:, 4 * qb + h:4 * qb + h + 1], in1=maskF[:, 256 - m:256],
            op0=ALU.add, op1=ALU.add), tk, ws, fox["cq"])
        rel(free, bk, [t])
        i = cnt["S"] % 8
        cnt["S"] += 1
        nm, l = stat_m[i][:, 0:1], stat_s[i][:, 0:1]
        t = VE.put(lambda e: e.tensor_reduce(nm, P, AX.X, ALU.max, negate=True), t)
        te = AC.put(lambda e: e.activation(P, P, ACT.Exp, bias=nm, accum_out=l), t)
        yield
        vs = [V[:, kb, 1024 + 64 * h:1088 + 64 * h] for kb in range(kn)]

        def write(o, rl, w):
            ys_t[2, h, qb] = VE.put(lambda e: e.tensor_scalar(ys[:, qb, 512 + 64 * h:576 + 64 * h], o, rl, None,
                                                              ALU.mult), w)
            return ys_t[2, h, qb]

        yield from softmax_tail(P, None, PT, kn, vs, [V_t[1024, 0], V_t[1024, 1]], l, te, write, si, Sb_free)

    lc = [stat(1) for _ in range(8)]

    def diff_task(h, qb):
        kn = qb + 1
        m = 128 * kn
        off = 0 if qb == 0 else 128
        while 22 not in qk_t:
            yield
        bk, wb = yield from take_one(3, 4)
        Z = bank[bk]
        w = [wb, qk_t[20], qk_t[22]]
        for c in range(2):
            p = 64 * (h % 2) + 32 * c
            tk = mm(Z[:, m * c:m * c + m], qkB[p:p + 32, 4 + h // 2, 128 * qb:128 * qb + 128],
                    qkB[p:p + 32, 6 + h // 2, 0:m], True, True, w)
            w = [tk]
        yield
        si, ws = yield from slot(Sb_free)
        P = Sb[:, si, 0:2 * m]
        for c in range(2):
            t = VE.put(lambda e, c=c: e.scalar_tensor_tensor(
                out=P[:, m * c:m * c + m], in0=c1("DD", 1152 + off, m), scalar=-SL_DIFF[h],
                in1=Z[:, m * c:m * c + m], op0=ALU.mult, op1=ALU.add), tk, T_CS1, ws)
        rel(free, bk, [t])
        i = cnt["S"] % 8
        cnt["S"] += 1
        nm, l = stat_m[i], stat_s[i]
        t = VE.put(lambda e: e.tensor_reduce(nm, P.rearrange("p (c k) -> p c k", c=2), AX.X, ALU.max, negate=True), t)
        for c in range(2):
            te = AC.put(lambda e, c=c: e.activation(P[:, m * c:m * c + m], P[:, m * c:m * c + m], ACT.Exp,
                                                    bias=nm[:, c:c + 1], accum_out=l[:, c:c + 1]), t)
        yield
        co = lc[i]
        t = VE.put(lambda e: e.reciprocal(co, l[:, 1:2]), te)
        t = VE.put(lambda e: e.scalar_tensor_tensor(out=co, in0=co, scalar=l[:, 0:1], in1=nlam, op0=ALU.mult,
                                                    op1=ALU.mult), t, t_nlam)
        t = VE.put(lambda e: e.scalar_tensor_tensor(out=P[:, 0:m], in0=P[:, m:2 * m], scalar=co, in1=P[:, 0:m],
                                                    op0=ALU.mult, op1=ALU.add), t)
        yield
        vs = [V[:, kb, 1280 + 64 * h:1344 + 64 * h] for kb in range(kn)]

        def write(o, rl, w):
            ys_t[3, h, qb] = VE.put(lambda e: e.tensor_scalar(ys[:, qb, 768 + 64 * h:832 + 64 * h], o, rl, None,
                                                              ALU.mult), w)
            return ys_t[3, h, qb]

        yield from softmax_tail(P, None, PT, kn, vs, [V_t[1280, 0], V_t[1280, 1]], l[:, 0:1], t, write, si, Sb_free)

    nsq_free = []

    def diff_norm(qb):
        while any((3, h, qb) not in ys_t for h in range(4)):
            yield
        yd = ys[:, qb, 768:1024]
        y3 = yd.rearrange("p (h d) -> p h d", h=4)
        sq = nsq[:]
        rs4 = stat(4)
        t = VE.put(lambda e: e.tensor_tensor(sq, yd, yd, ALU.mult), [ys_t[3, h, qb] for h in range(4)], nsq_free)
        t = VE.put(lambda e: e.tensor_reduce(rs4, sq.rearrange("p (h d) -> p h d", h=4), AX.X, ALU.add), t)
        nsq_free[:] = [t]
        r, tp = rsqrt(rs4, 4, 64, t)
        yield
        t = VE.put(lambda e: e.tensor_tensor(y3, y3, r.unsqueeze(2).broadcast_to([128, 4, 64]), ALU.mult), tp)
        t = VE.put(lambda e: e.scalar_tensor_tensor(
            out=y3, in0=y3, scalar=0.8, in1=pcol("g_diff", 0, 64).unsqueeze(1).broadcast_to([128, 4, 64]),
            op0=ALU.mult, op1=ALU.mult), t)
        ys_t["d", qb] = t

    def turn_task(src, keys, hi, lo, kc0, t, out, prior=()):
        while any(k not in ys_t for k in keys):
            yield
        bk, wb = yield from take_one(5, 6)
        w = [[ys_t[k] for k in keys], wb, [ys_t[k] for k in prior]]
        for k in range(4):
            tk = tr(bank[bk][:, 128 * k:128 * k + 128], src[:, 128 * k:128 * k + 128], w, sig=(k == 3))
            w = []
        yield
        ph = hi[:, kc0:kc0 + 4, t * 128:(t + 1) * 128]
        pl = lo[:, kc0:kc0 + 4, t * 128:(t + 1) * 128]
        ps = bank[bk].rearrange("p (k q) -> p k q", k=4)
        a = AC.put(lambda e: e.copy(ph, ps), tk)
        v = VE.put(lambda e: e.tensor_tensor(pl, ps, ph.bitcast(F32), ALU.subtract), a)
        rel(free, bk, [a, v])
        out[t, kc0 // 4] = [a, v]

    B_t = {}

    prefetch(u_p1[0][0])
    g_t = {}

    def evac_gate(c):
        def fn(t, bk, tk, n):
            o = gates[:, t, 512 * c:512 * c + 512]
            w = [[stage_free[k] for k in range(10)], None]
            free[bk] = [AC.put(lambda e: e.mul(o, bank[bk], r1_[:, t:t + 1]), tk, t_r1, w[0], w[1])]
            g_t[c, t] = free[bk][0]
        return fn

    for c in range(18):
        chunk(u_p1[c], Ahi, Alo, A_t, evac1(c) if c < 10 else evac_gate(c - 10), first_of_phase=(c == 0))
    tgbuf[0] = tg

    mix_t = {}
    M_t = {}
    W_acc = {(0, 0): 3, (1, 0): 4, (0, 1): 7, (1, 1): 0}

    def gated(u, n, hf, t, sg, tsg, bk, tk):
        mx = ys[:, t, 512 * hf:512 * hf + 512]
        if n == 0:
            v = VE.put(lambda e: e.tensor_tensor(mx, sg[:, t, :], bank[bk], ALU.mult), tk, tsg, B_t[t, hf])
            free[bk] = [v]
        else:
            v = VE.put(lambda e: e.tensor_tensor(sg[:, t, :], sg[:, t, :], bank[bk], ALU.mult), tk, tsg)
            free[bk] = [v]
            v = VE.put(lambda e: e.tensor_tensor(mx, mx, sg[:, t, :], ALU.add), v, mix_t[t, hf])
        mix_t[t, hf] = v

    for hf in range(2):
        for n in range(4):
            if hf == 0 and n == 2:
                bg_all()
            sg = gates[:, :, 1024 * n + 512 * hf:1024 * n + 512 * hf + 512]
            tsg = AC.put(lambda e, sg=sg: e.activation(sg, sg, ACT.Sigmoid), g_t[2 * n + hf, 0], g_t[2 * n + hf, 1])
            u = u_br[hf][n // 2]
            kr = range(2 * (n % 2), 2 * (n % 2) + 2)
            for t in range(2):
                bk = rot[0] % 2
                rot[0] += 1
                while (t, n // 2) not in B_t:
                    bg()
                tk = mm_unit(u, Bhi, Blo, 4 * (n // 2), t, lambda kc, c0, bk=bk: bank[bk],
                             lambda kc, kr=kr: kc == kr[0], lambda kc, kr=kr: kc == kr[-1],
                             B_t[t, n // 2] + free[bk], t == 1 and n % 2 == 1, kr=kr)
                late()
                later.append(lambda u=u, n=n, hf=hf, t=t, sg=sg, tsg=tsg, bk=bk, tk=tk: gated(
                    u, n, hf, t, sg, tsg, bk, tk))
                free[bk] = []
                if active or pending:
                    bg()
            if n % 2 == 1:
                prefetch(u + 1)
            if hf == 1 and n in (0, 1):
                t = n
                M_t[t, 0] = turn_split(ys[:, t, 0:512], mix_t[t, 0], Ahi, Alo, 0, t, 5 + t)
    late()
    t_gfree = (VE.sem, VE.n)

    def out_proj(us, hi, lo, src_t, mid, ts, turn):
        for n in range(2):
            for t in range(2):
                bk = W_acc[t, n]
                while (t, 0) not in src_t or free[bk] is None:
                    bg()
                mm_unit(us[0][n], hi, lo, 0, t, lambda kc, c0, bk=bk: bank[bk],
                        lambda kc: kc == 0, lambda kc: False, src_t[t, 0] + free[bk], t == 1)
                free[bk] = []
                late()
                if active or pending:
                    bg()
                if n == 1 and t == 0:
                    mid()
            prefetch(us[0][n] + 1)
        for t in range(2):
            for n in range(2):
                bk = W_acc[t, n]
                while (t, 1) not in src_t:
                    bg()
                tk = mm_unit(us[1][n], hi, lo, 4, t, lambda kc, c0, bk=bk: bank[bk],
                             lambda kc: False, lambda kc: kc == 3, src_t[t, 1], t == 1)
                if t == 1:
                    prefetch(us[1][n] + 1)
                xs = xr[:, t, 512 * n:512 * n + 512]
                v = VE.put(lambda e, xs=xs, bk=bk: e.tensor_tensor(xs, xs, bank[bk], ALU.add), tk, x_w[t])
                free[bk] = [v]
                ts[t, n] = v
                late()
                if active or pending:
                    bg()
                later.append(turn(t, n))

    x_w = [[tq], [tq]]

    def mid1():
        for t in range(2):
            M_t[t, 1] = turn_split(ys[:, t, 512:1024], mix_t[t, 1], Ahi, Alo, 4, t, 5 + t)

    def norm_turn(ts, hi, lo, gain, H, extra=None):
        def turn(t, n):
            def fn():
                H[t, n] = turn_split(xr[:, t, 512 * n:512 * n + 512], [ts[t, n], extra], hi, lo, 4 * n, t, 5 + n, gain=gain)
            return fn
        return turn

    x1_t, H_t = {}, {}
    out_proj(u_wo, Ahi, Alo, M_t, mid1, x1_t, norm_turn(x1_t, Bhi, Blo, lambda k: pcol("g_mlp", k, 4), H_t))

    def x_stats(ts, junk, jw):
        o = stat(2)
        for t in range(2):
            a = AC.put(lambda e, t=t: e.activation(junk[:, t, :], xr[:, t, :], ACT.Square, accum_out=o[:, t:t + 1]),
                       ts[t, 0], ts[t, 1], jw)
        return rsqrt(o, 2, D, a), a


    h_free = [[], []]
    u_free = [[], []]

    def ffn_down(us, j, nj, hid_t, last, turn=None):
        kn = nj_of(us, j)
        hi, lo = hhi[:, j % 2], hlo[:, j % 2]
        if len(us[j]) == 2:
            seq = [(n, t) for t in range(2) for n in range(2)] if last else [(n, t) for n in range(2) for t in range(2)]
            for n, t in seq:
                bk = W_acc[t, n]
                w = hid_t[t] + (free[bk] if j == 0 else [])
                tk = mm_unit(us[j][n], hi, lo, 0, t, lambda kc, c0, bk=bk: bank[bk],
                             lambda kc: j == 0 and kc == 0, lambda kc: last and kc == 3, w, t == 1)
                if j == 0:
                    free[bk] = []
                if t == 1:
                    prefetch(us[j][n] + 1)
                if last:
                    nj(t, n, tk)
                late()
                if last and turn:
                    later.append(turn(t, n))
        else:
            for t in range(2):
                tk = mm_unit(us[j][0], hi, lo, 0, t, lambda kc, c0, t=t: bank[W_acc[t, c0 // 512]],
                             lambda kc: False, lambda kc: last and kc == kn - 1, hid_t[t], t == 1)
                for n in range(2):
                    nj(t, n, tk)
            prefetch(us[j][0] + 1)
        h_free[j % 2] = [tk]

    def nj_of(us, j):
        return units[us[j][0]][1]

    def residual(ts):
        def fn(t, n, tk):
            bk = W_acc[t, n]
            xs = xr[:, t, 512 * n:512 * n + 512]
            v = VE.put(lambda e: e.tensor_tensor(xs, xs, bank[bk], ALU.add), tk, x_w[t])
            free[bk] = [v]
            ts[t, n] = v
        return fn

    def up_product(us, hi, lo, src_t, order_first, evac):
        n = units[us[0]][2]
        order = [(0, 0), (1, 0), (0, 1), (1, 1)] if order_first else [(0, 0), (0, 1), (1, 0), (1, 1)]
        for ui, t in order:
            bk = 1 + t
            w = list(src_t[t, ui])
            if ui == 0:
                w += free[bk]
                free[bk] = []
            tk = mm_unit(us[ui], hi, lo, 4 * ui, t, lambda kc, c0, bk=bk: bank[bk][:, 0:n],
                         lambda kc, ui=ui: ui == 0 and kc == 0, lambda kc, ui=ui: ui == 1 and kc == 3, w, t == 1)
            if t == 1:
                prefetch(us[ui] + 1)
            late()
            if ui == 1:
                later.append(lambda t=t, bk=bk, tk=tk: evac(t, bk, tk, n))

    ST = {}

    def stats1():
        (ST["r2"], ST["t_r2"]), ta = x_stats(x1_t, ys, PE_last(PE))
        x_w[0], x_w[1] = [ta], [ta]

    later.append(stats1)
    x2_t, H2_t = {}, {}
    gg = stat(8)
    t_gg = VE.put(lambda e: e.tensor_tensor(gg, pcol("g_fin", 0, 8), pcol("g_n1", 0, 8), ALU.mult), T_PAR)
    hid_t = {}
    for j in range(8):
        up_t = {}

        def ev(t, bk, tk, n, j=j):
            o = ust[:, j % 2, t, :]
            r = ST["r2"]
            a = AC.put(lambda e: e.activation(o, bank[bk], ACT.Relu, scale=r[:, t:t + 1]), tk, ST["t_r2"],
                       u_free[j % 2])
            free[bk] = [a]
            up_t[t] = AC.put(lambda e: e.activation(o, o, ACT.Square), a)

        up_product(u_up[j], Bhi, Blo, H_t, j == 0, ev)
        if j:
            ffn_down(u_dn, j - 1, None, hid_t[j - 1], False)
        late()
        hid_t[j] = {}
        for t in range(2):
            free[5 + t] = free[5 + t] + h_free[j % 2]
            hid_t[j][t] = turn_split(ust[:, j % 2, t, :], up_t[t], hhi[:, j % 2], hlo[:, j % 2], 0, t, 5 + t)
        u_free[j % 2] = [PE_last(PE)]
    ffn_down(u_dn, 7, residual(x2_t), hid_t[7], True,
             norm_turn(x2_t, Ahi, Alo, lambda k: gg[:, k:k + 4], H2_t, t_gg))

    dma(par2[:], par2_d, d_par2, t_gfree)
    T_P2 = (d_par2, 16)
    r4_ = stat(2)
    ss4 = stat(2)

    def stats2():
        t_turned = PE_last(PE)
        (r3, t_r3), ta3 = x_stats(x2_t, ys, PE_last(PE))
        for t in range(2):
            v = VE.put(lambda e, t=t: e.scalar_tensor_tensor(
                out=xr[:, t, :], in0=xr[:, t, :], scalar=r3[:, t:t + 1], in1=par2[:, 0:1024], op0=ALU.mult,
                op1=ALU.mult), t_r3, T_P2, ta3, t_turned)
            a = AC.put(lambda e, t=t: e.activation(ys[:, t, :], xr[:, t, :], ACT.Square, accum_out=ss4[:, t:t + 1]), v)
        r4a, t_r4a = rsqrt(ss4, 2, D, a)
        ST["t_r4"] = VE.put(lambda e: e.tensor_tensor(r4_, r3, r4a, ALU.mult), t_r4a)
        x_w[0], x_w[1] = [a], [a]

    later.append(stats2)

    RT = ust[:, 1, 0, :]
    RT2 = ust[:, 1, 1, :]
    for qk in range(2):
        g = par2[:, 1024 + 64 * qk:1088 + 64 * qk]
        for t in range(2):
            o = (qk * 2 + t) * 64
            VE.put(lambda e, o=o, g=g, t=t: e.tensor_tensor(RT[:, o:o + 64], par2[:, 1152 + 64 * t:1216 + 64 * t], g,
                                                            ALU.mult), T_P2, u_free[1])
            VE.put(lambda e, o=o, g=g, t=t: e.tensor_tensor(
                RT2[:, o:o + 32], par2[:, 1280 + 64 * t:1312 + 64 * t], g[:, 32:64], ALU.mult))
            t_rt = VE.put(lambda e, o=o, g=g, t=t: e.tensor_tensor(
                RT2[:, o + 32:o + 64], par2[:, 1312 + 64 * t:1344 + 64 * t], g[:, 0:32], ALU.mult))

    t_pad = GP.put(lambda e: e.memset(ch[:, :, 0:30], 0.0), t_gfree)
    glu_t = {}
    c_t = {}

    def evac_u(c):
        def fn(t, bk, tk, n):
            o = (ys[:, t, 0:512], ys[:, t, 512:1024])[c]
            v = AC.put(lambda e: e.mul(o, bank[bk], r4_[:, t:t + 1]), tk, ST["t_r4"])
            free[bk] = [v]
            glu_t[c, t] = v
            pending.append(sig_task(t) if c == 1 else glu_task(t))
            if c == 0 and t == 1:
                pending.append(conv_task())
        return fn

    cols = {}

    def turn_u(c, t, bk, w):
        for k in range(4):
            tk = tr(bank[bk][:, 128 * k:128 * k + 128], ys[:, t, 512 * c + 128 * k:512 * c + 128 * k + 128], w,
                    sig=(k == 3))
            w = []
        cols[c, t] = tk
        return tk

    def sig_task(t):
        bk, w = yield from take_one(5, 6)
        tk = turn_u(1, t, bk, [glu_t[1, t], w])
        yield
        sg = ca[:, :, 128 * t:128 * t + 128]
        for k in range(4):
            a = AC.put(lambda e, k=k: e.activation(sg[:, k, :], bank[bk][:, 128 * k:128 * k + 128],
                                                   ACT.Sigmoid, bias=pcol("glu_b", 4 + k)), tk)
        rel(free, bk, [a])
        sg_tok[t] = a

    sg_tok = {}
    gl_tok = {}

    def glu_task(t):
        bk, w = yield from take_one(5, 6)
        tk = turn_u(0, t, bk, [glu_t[0, t], w])
        yield
        while t not in sg_tok:
            yield
        for k in range(4):
            v = VE.put(lambda e, k=k: e.scalar_tensor_tensor(
                out=ch[:, k, 30 + 128 * t:158 + 128 * t], in0=bank[bk][:, 128 * k:128 * k + 128],
                scalar=pcol("glu_b", k), in1=ca[:, k, 128 * t:128 * t + 128], op0=ALU.add, op1=ALU.mult),
                tk, sg_tok[t])
        rel(free, bk, [v])
        gl_tok[t] = v

    def conv_task():
        while len(gl_tok) < 2:
            yield
        prev = [[gl_tok[0], gl_tok[1], t_pad]] * 4
        cv_free = [None] * 6
        i = 0
        for j in range(31):
            for k in range(4):
                wc = pcol("dw_w", 31 * k + j)
                src = ch[:, k, j:j + 256]
                if k < 2:
                    if j == 0:
                        prev[k] = VE.put(lambda e, k=k, wc=wc, src=src: e.tensor_scalar(
                            ca[:, k, :], src, wc, pcol("dw_b", k), ALU.mult, ALU.add), prev[k])
                    else:
                        prev[k] = VE.put(lambda e, k=k, wc=wc, src=src: e.scalar_tensor_tensor(
                            out=ca[:, k, :], in0=src, scalar=wc, in1=ca[:, k, :], op0=ALU.mult, op1=ALU.add), prev[k])
                elif j == 0:
                    prev[k] = AC.put(lambda e, k=k, wc=wc, src=src: e.activation(
                        ca[:, k, :], src, ACT.Identity, bias=pcol("dw_b", k), scale=wc), prev[k])
                    t_in = prev[k]
                else:
                    a = AC.put(lambda e, i=i, wc=wc, src=src: e.mul(cv[:, i, :], src, wc), cv_free[i], t_in)
                    prev[k] = GP.put(lambda e, i=i, k=k: e.tensor_tensor(ca[:, k, :], ca[:, k, :], cv[:, i, :],
                                                                         ALU.add), a, prev[k])
                    cv_free[i] = prev[k]
                    i = (i + 1) % 6
            if j % 2 == 1:
                yield
        for t in range(2):
            active.append(ln_task(t, list(prev)))

    def ln_task(t, prev):
        bk, w = yield from take_one(5, 6)
        w = [prev, w]
        for k in range(4):
            tk = tr(bank[bk][:, 128 * k:128 * k + 128], ca[:, k, 128 * t:128 * t + 128], w, sig=(k == 3))
            w = []
        yield
        bs = stat(6)
        mv = stat(2)
        v = VE.put(lambda e: e.bn_stats(bs, bank[bk]), tk)
        v = VE.put(lambda e: e.bn_aggr(mv, bs), v)
        r, tp = rsqrt(mv[:, 1:2], 1, 1, v)
        cn = ys[:, t, 512:1024]
        v = VE.put(lambda e: e.tensor_scalar(cn, bank[bk], mv[:, 0:1], r, ALU.subtract, ALU.mult), tp, v)
        for k in range(4):
            tk = tr(bank[bk][:, 128 * k:128 * k + 128], cn[:, 128 * k:128 * k + 128], v, sig=(k == 3))
        yield
        sl = ch[:, :, 128 * t:128 * t + 128]
        for k in range(4):
            a = AC.put(lambda e, k=k: e.activation(sl[:, k, :], bank[bk][:, 128 * k:128 * k + 128], ACT.Silu,
                                                   bias=pcol("ln_b", k), scale=pcol("ln_g", k)), tk)
        rel(free, bk, [a])
        hi_ = Bhi[:, 4:8, 128 * t:128 * t + 128]
        lo_2 = Blo[:, 4:8, 128 * t:128 * t + 128]
        a = AC.put(lambda e: e.copy(hi_, sl), a)
        v = VE.put(lambda e: e.tensor_tensor(lo_2, sl, hi_.bitcast(F32), ALU.subtract), a)
        Y_t[t, 1] = [a, v]

    Y_t = {}
    q2_t = {}
    V2_t = {}
    qs = {}
    u2f = [[], []]

    def evac_q(qk):
        def fn(t, bk, tk, n):
            o = ust[:, 0, t, :]
            v = AC.put(lambda e: e.mul(o, bank[bk], r4_[:, t:t + 1]), tk, ST["t_r4"], u_free[0], u2f[t])
            free[bk] = [v]
            pending.insert(0, rope_task(qk, t, o, v))
            if qk == 1 and t == 1:
                pending.extend(att2_task(h) for h in range(8))
                pending.extend(turn_task(ys[:, t_, 0:512], [(4, h) for h in range(8)], Bhi, Blo, 0, t_, Y_t)
                               for t_ in range(2))
        return fn

    tmp_f = [[]]

    def rope_task(qk, t, o, t_in):
        o3 = o.rearrange("p (h d) -> p h d", h=8)
        w1 = PT2[:, 0, 0:512]
        w2 = PT2[:, 1, 0:512]
        w13 = w1.rearrange("p (h d) -> p h d", h=8)
        w23 = w2.rearrange("p (h d) -> p h d", h=8)
        s8 = stat(8)
        _, wt = yield from slot(tmp_f)
        v = AC.put(lambda e: e.activation(w1, o, ACT.Square), t_in, wt, t_gfree)
        v = VE.put(lambda e: e.tensor_reduce(s8, w13, AX.X, ALU.add), v)
        r, tp = rsqrt(s8, 8, 64, v)
        yield
        v = VE.put(lambda e: e.tensor_tensor(o3, o3, r.unsqueeze(2).broadcast_to([128, 8, 64]), ALU.mult), tp)
        of = (qk * 2 + t) * 64
        cA = RT[:, of:of + 64].unsqueeze(1).broadcast_to([128, 8, 64])
        sA = RT2[:, of:of + 32].unsqueeze(1).broadcast_to([128, 8, 32])
        sB = RT2[:, of + 32:of + 64].unsqueeze(1).broadcast_to([128, 8, 32])
        va = VE.put(lambda e: e.tensor_tensor(w13, o3, cA, ALU.mult), v, t_rt)
        VE.put(lambda e: e.tensor_tensor(w23[:, :, 0:32], o3[:, :, 32:64], sA, ALU.mult), v)
        vb = VE.put(lambda e: e.tensor_tensor(w23[:, :, 32:64], o3[:, :, 0:32], sB, ALU.mult), v)
        v = GP.put(lambda e: e.tensor_tensor(w1, w1, w2, ALU.add), va, vb)
        u2f[t] = [v]
        yield
        w = yield from take(5)
        w = [v, w]
        for k in range(4):
            tk = tr(bank[5][:, 128 * k:128 * k + 128], w1[:, 128 * k:128 * k + 128], w, sig=(k == 3))
            w = []
        rel(tmp_f, 0, [tk])
        dst = qk2T[:, 4 * qk:4 * qk + 4, 128 * t:128 * t + 128]
        a = AC.put(lambda e: e.mul(dst, bank[5].rearrange("p (k q) -> p k q", k=4), 0.125 if qk == 0 else 1.0), tk,
                   t_gfree)
        rel(free, 5, [a])
        q2_t[qk, t] = a

    def evac_v2(t, bk, tk, n):
        v = AC.put(lambda e: e.mul(V2[:, t, :], bank[bk], r4_[:, t:t + 1]), tk, ST["t_r4"])
        free[bk] = [v]
        V2_t[t] = v

    S2_free = [[], [], []]

    def att2_task(h):
        while len(q2_t) < 4:
            yield
        bk, wb = yield from take_one(3, 4)
        Z = bank[bk]
        p = 64 * (h % 2)
        q, k = qk2T[p:p + 64, h // 2, :], qk2T[p:p + 64, 4 + h // 2, :]
        mm(Z[:, 0:128], q[:, 0:128], k[:, 0:128], True, True, wb, [q2_t[a, b_] for a in range(2) for b_ in range(2)],
           sig=False)
        tk = mm(Z[:, 128:384], q[:, 128:256], k, True, True)
        yield
        si, ws = yield from slot(S2_free)
        P = S2[:, si, :]
        Zd = Z.rearrange("p (a b) -> p a b", a=2)[:, :, 0:128]
        t = VE.put(lambda e: e.tensor_tensor(Zd, Zd, maskF[:, 128:256].unsqueeze(1).broadcast_to([128, 2, 128]),
                                             ALU.add), tk)
        i = cnt["S"] % 8
        cnt["S"] += 1
        nm, l = stat_m[i], stat_s[i]
        VE.put(lambda e: e.tensor_reduce(nm[:, 0:1], Z[:, 0:128], AX.X, ALU.max, negate=True), t)
        t = VE.put(lambda e: e.tensor_reduce(nm[:, 1:2], Z[:, 128:384], AX.X, ALU.max, negate=True), t)
        AC.put(lambda e: e.activation(P[:, 0:128], Z[:, 0:128], ACT.Exp, bias=nm[:, 0:1], accum_out=l[:, 0:1]), t, ws)
        te = AC.put(lambda e: e.activation(P[:, 128:384], Z[:, 128:384], ACT.Exp, bias=nm[:, 1:2],
                                           accum_out=l[:, 1:2]))
        rel(free, bk, [te])
        yield
        bk, wb = yield from take_one(5, 6)
        w = [te, wb]
        for j in range(3):
            tk = tr(bank[bk][:, 128 * j:128 * j + 128], P[:, 128 * j:128 * j + 128], w, sig=(j == 2))
            w = []
        rel(S2_free, si, [tk])
        trl = VE.put(lambda e: e.reciprocal(l, l), te)
        yield
        pi, wp = yield from slot(PT_free)
        ta = AC.put(lambda e: e.copy(PT2[:, pi, 0:384], bank[bk][:, 0:384]), tk, wp)
        rel(free, bk, [ta])
        yield
        while len(V2_t) < 2:
            yield
        ob, wo = yield from take_one(2, 7)
        mm(bank[ob][:, 0:64], PT2[:, pi, 0:128], V2[:, 0, 64 * h:64 * h + 64], True, True, ta, wo, V2_t[0], V2_t[1],
           sig=False)
        mm(bank[ob][:, 64:128], PT2[:, pi, 128:256], V2[:, 0, 64 * h:64 * h + 64], True, False, sig=False)
        tk = mm(bank[ob][:, 64:128], PT2[:, pi, 256:384], V2[:, 1, 64 * h:64 * h + 64], False, True)
        rel(PT_free, pi, [tk])
        yield
        o = bank[ob][:, 0:128].rearrange("p (a d) -> p a d", a=2)
        ys_t[4, h] = VE.put(lambda e: e.tensor_tensor(ys[:, :, 64 * h:64 * h + 64], o,
                                                      l.unsqueeze(2).broadcast_to([128, 2, 64]), ALU.mult),
                            tk, trl, cols[0, 0], cols[0, 1])
        rel(free, ob, [ys_t[4, h]])

    PT_free[0] = []
    PT_free[1] = []
    for i, us in enumerate(u_p2):
        ev2 = [evac_u(1), evac_u(0), evac_q(0), evac_q(1), evac_v2][i]
        chunk(us, Ahi, Alo, H2_t, ev2, first_of_phase=(i == 0), start=2)
    late()

    x3_t, H3_t = {}, {}
    out_proj(u_wo2, Bhi, Blo, Y_t, lambda: None, x3_t, norm_turn(x3_t, Ahi, Alo, lambda k: pcol("g_n2", k, 4), H3_t))

    def stats3():
        (ST["r5"], ST["t_r5"]), ta = x_stats(x3_t, ys, PE_last(PE))
        ST["ta5"] = ta
        x_w[0], x_w[1] = [ta], [ta]

    later.append(stats3)

    out_t = {}
    res = residual(out_t)
    o_v = out_d.rearrange("(t p) d -> p t d", p=128)
    nout = [0]

    def final(t, n, tk):
        res(t, n, tk)
        dma(o_v[:, t, 512 * n:512 * n + 512], xr[:, t, 512 * n:512 * n + 512], d_out, out_t[t, n])
        nout[0] += 16

    hid2 = {}
    gl = ys
    gl_free = {0: PE_last(PE), 1: PE_last(PE)}
    for j in range(6):
        n_ = HC2[j] * 128
        sg_t = {}
        m_t = {}

        def ev_g(t, bk, tk, n):
            r = ST["r5"]
            a = AC.put(lambda e: e.activation(gl[:, t, 0:n], bank[bk][:, 0:n], ACT.Silu, scale=r[:, t:t + 1]),
                       tk, ST["t_r5"], gl_free[t], ST["ta5"])
            free[bk] = [a]
            sg_t[t] = a

        def ev_u(t, bk, tk, n, j=j):
            o = ust[:, j % 2, t, 0:n]
            r = ST["r5"]
            v = VE.put(lambda e: e.scalar_tensor_tensor(out=o, in0=bank[bk][:, 0:n], scalar=r[:, t:t + 1],
                                                        in1=gl[:, t, 0:n], op0=ALU.mult, op1=ALU.mult),
                       tk, sg_t[t], ST["t_r5"], u_free[j % 2])
            free[bk] = [v]
            gl_free[t] = v
            m_t[t] = v

        up_product(u_g2[j], Ahi, Alo, H3_t, j == 0, ev_g)
        up_product(u_u2[j], Ahi, Alo, H3_t, False, ev_u)
        if j:
            ffn_down(u_d2, j - 1, None, hid2[j - 1], False)
        late()
        hid2[j] = {}
        for t in range(2):
            free[5 + t] = free[5 + t] + h_free[j % 2]
            hid2[j][t] = turn_split(ust[:, j % 2, t, 0:n_], m_t[t], hhi[:, j % 2], hlo[:, j % 2], 0, t, 5 + t,
                                    nk=HC2[j])
        u_free[j % 2] = [PE_last(PE)]
    ffn_down(u_d2, 5, final, hid2[5], True)

    block = ctx.enter_context(nc.Block())

    @block.sync
    def _(e):
        SP.play(e)
        e.wait_ge(d_out, nout[0])

    @block.tensor
    def _(e):
        PE.play(e)

    @block.scalar
    def _(e):
        AC.play(e)

    @block.vector
    def _(e):
        VE.play(e)

    @block.gpsimd
    def _(e):
        GP.play(e)


def PE_last(q):
    return (q.sem, q.n)


def _constants():
    import numpy as np

    q = np.arange(128)
    ident = np.eye(128, dtype=np.float32)
    tri = np.where(q[None, :] <= q[:, None], 0.0, NEG).astype(np.float32)
    maskF = np.concatenate([np.zeros((128, 128), np.float32), tri], axis=1)
    DDs = []
    for window, dil in ((128, 1), (512, 4), (2048, 16), (10 ** 9, 1)):
        blocks = []
        for qo, ko in ((0, 0), (128, 0), (128, 128)):
            dist = (q[:, None] + qo) - (q[None, :] + ko)
            ok = (dist >= 0) & (dist % dil == 0) & (dist <= window)
            blocks.append(np.where(ok, dist, 1e30).astype(np.float32))
        DDs.append(np.concatenate(blocks, axis=1))
    kk, qq = q[:, None], q[None, :]
    strict = np.where(kk < qq, 0.0, NEG).astype(np.float32)
    MB = np.concatenate([strict, np.zeros((128, 128), np.float32), strict], axis=1)
    UO = np.concatenate([(kk <= qq).astype(np.float32), np.ones((128, 128), np.float32)], axis=1)
    LG = (kk >= qq).astype(np.float32)
    return np.ascontiguousarray(np.concatenate([ident, maskF] + DDs + [MB, UO, LG], axis=1), dtype=np.float32)


def _rope():
    import numpy as np

    pos = np.arange(256, dtype=np.float32)
    inv = np.power(np.float32(10000.0), -np.arange(0, 64, 2, dtype=np.float32) / np.float32(64)).astype(np.float32)
    ang = (pos[:, None] * inv[None, :]).astype(np.float32)
    cos, sin = np.cos(ang).astype(np.float32), np.sin(ang).astype(np.float32)
    c = np.concatenate([cos, cos], axis=1)
    s = np.concatenate([-sin, sin], axis=1)
    lay = lambda a: a.reshape(2, 128, 64).transpose(1, 0, 2).reshape(128, 128)
    return lay(c), lay(s)


def kernel(**inputs):
    import numpy as np
    import concourse.bacc as bacc
    from concourse.bass_utils import run_bass_kernel_spmd

    a = {k: np.asarray(v) for k, v in inputs.items()}
    col = lambda v, n: v.reshape(n, 128).T
    row = lambda v: np.broadcast_to(v.reshape(1, -1), (128, v.size))
    dw = a["dw_w_2"][0].reshape(31, 4, 128).transpose(2, 1, 0).reshape(128, 124)
    par = np.concatenate([
        col(a["mix_norm_g"], 8), col(a["mlp_norm_g"], 8), col(a["final_norm_g"], 8), col(a["norm1_g_2"], 8),
        col(a["norm2_g_2"], 8), col(a["glu_b_2"], 8), dw, col(a["dw_b_2"], 4), col(a["conv_ln_g_2"], 4),
        col(a["conv_ln_b_2"], 4), row(a["b_forget"]), row(a["lambda_q1"]), row(a["lambda_q2"]),
        row(a["lambda_k1"]), row(a["lambda_k2"]), row(a["diff_norm_g"])], axis=1)
    cosT, sinT = _rope()
    par2 = np.concatenate([row(a["final_norm_g"]), row(a["q_norm_g_2"]), row(a["k_norm_g_2"]), cosT, sinT], axis=1)
    arrays = {
        "x": a["x"][0], "w_in": a["w_in"][0], "w_br": a["w_branch"][0].reshape(1024, 1024), "w_out": a["w_out"][0],
        "w_up": a["w_up"][0], "w_dn": a["w_down"][0], "w_in2": a["w_in_2"][0], "w_out2": a["w_out_2"][0],
        "w_g2": a["w_gate_2"][0], "w_u2": a["w_up_2"][0], "w_d2": a["w_down_2"][0],
        "par": par, "par2": par2, "cst": _constants(),
    }
    nc = bacc.Bacc("TRN2", target_bir_lowering=False, num_devices=1)
    args, ins = [], {}
    for name, v in arrays.items():
        v = np.ascontiguousarray(v)
        ins["in_" + name] = v
        args.append(nc.dram_tensor("in_" + name, v.shape, mybir.dt.from_np(v.dtype), kind="ExternalInput").ap())
    args.append(nc.dram_tensor("out_0", (S, D), F32, kind="ExternalOutput").ap())
    program(nc, *args)
    r = run_bass_kernel_spmd(nc, [ins], core_ids=[0])
    return r.results[0]["out_0"].reshape(1, S, D)
```

```python
import concourse.bass as bass
from concourse import mybir
from contextlib import ExitStack

F32 = mybir.dt.float32
F32R = mybir.dt.float32r
ALU = mybir.AluOpType
ACT = mybir.ActivationFunctionType
AX = mybir.AxisListType

D = 1024
S = 256
EPS = 1e-6
DFF1 = 4096
DFF2 = 2816
NRAW = 4
NSPL = 3
LEAD = 2
NEG = -1e30

SLOPES = [2.0 ** (-8.0 * i / 16) for i in range(1, 17)]
SL_DIL = [SLOPES[0:4], SLOPES[8:12], SLOPES[12:16]]
SL_DIFF = SLOPES[4:8]

PAR = {}
CST = {}


def _layout():
    n = 0
    for name, w in (("g_mix", 8), ("g_mlp", 8), ("g_fin", 8), ("g_n1", 8), ("g_n2", 8), ("glu_b", 8),
                    ("dw_w", 124), ("dw_b", 4), ("ln_g", 4), ("ln_b", 4), ("b_f", 4), ("lam", 128),
                    ("g_diff", 64)):
        PAR[name] = (n, w)
        n += w
    PAR["_n"] = n
    n = 0
    for name, w in (("ident", 128), ("maskF", 256)):
        CST[name] = (n, w)
        n += w
    CST["_n0"] = n
    n = 0
    for name, w in (("DD", 1536), ("MB", 384), ("UO", 256), ("LG", 128)):
        CST[name] = (n, w)
        n += w
    CST["_n1"] = n
    return


_layout()


class Queue:

    def __init__(self, sem):
        self.sem = sem
        self.n = 0
        self.items = []

    def put(self, fn, *waits, sig=True):
        flat = []
        todo = list(waits)
        while todo:
            w = todo.pop(0)
            if isinstance(w, list):
                todo = w + todo
            elif w is not None:
                flat.append(w)
        if sig:
            self.n += 1
        self.items.append((fn, flat, sig))
        return (self.sem, self.n)

    def play(self, eng):
        seen = {}
        for fn, waits, sig in self.items:
            for sem, v in waits:
                if seen.get(sem, 0) < v:
                    eng.wait_ge(sem, v)
                    seen[sem] = v
            ins = fn(eng)
            if sig:
                ins.then_inc(self.sem, 1)


def program(nc, x_d, w_in, w_br, w_out, w_up, w_dn, w_in2, w_out2, w_g2, w_u2, w_d2, par_d, par2_d, cst_d, out_d):
    with ExitStack() as ctx:
        build(nc, ctx, x_d, w_in, w_br, w_out, w_up, w_dn, w_in2, w_out2, w_g2, w_u2, w_d2, par_d, par2_d,
              cst_d, out_d)


def build(nc, ctx, x_d, w_in, w_br, w_out, w_up, w_dn, w_in2, w_out2, w_g2, w_u2, w_d2, par_d, par2_d, cst_d, out_d):
    def sem(name):
        return ctx.enter_context(nc.semaphore(name))

    def sb(name, shape, dt=F32, c=ctx):
        return c.enter_context(nc.sbuf_tensor(name, shape, dt))

    NPAR = PAR["_n"]
    N0, N1 = CST["_n0"], CST["_n1"]
    raw = sb("raw", [128, NRAW, 2048])
    whi = sb("whi", [128, NSPL, 2048], F32R)
    wlo = sb("wlo", [128, NSPL, 2048], F32R)
    xr = sb("xr", [128, 2, D])
    Ahi = sb("Ahi", [128, 8, S], F32R)
    Alo = sb("Alo", [128, 8, S], F32R)
    ys = sb("ys", [128, 2, D])
    par = sb("par", [128, NPAR])
    cst = sb("cst", [128, N0])
    st = sb("st", [128, 384])
    with ExitStack() as r1:
        qkA = sb("qkA", [128, 16, S], c=r1)
    with ExitStack() as r2:
        Bhi = sb("Bhi", [128, 8, S], F32R, c=r2)
        Blo = sb("Blo", [128, 8, S], F32R, c=r2)
        gap = ExitStack()
        gates = sb("gates", [128, 2, 4096], c=gap)
        r1 = ExitStack()
        qkB = sb("qkB", [128, 8, S], c=r1)
        V = sb("V", [128, 2, 1536], c=r1)
        Sb = sb("Sb", [128, 2, 768], c=r1)
        PT = sb("PT", [128, 2, 768], c=r1)
        cs1 = sb("cs1", [128, N1], c=r1)
        nlf = sb("nlf", [128, 2, 128], c=r1)
        nsq = sb("nsq", [128, 256], c=r1)
        r1.close()
        r3 = ExitStack()
        hhi = sb("hhi", [128, 2, 4, S], F32R, c=r3)
        hlo = sb("hlo", [128, 2, 4, S], F32R, c=r3)
        ust = sb("ust", [128, 2, 2, 512], c=r3)
        V2 = sb("V2", [128, 2, 512], c=r3)
        tg = sb("tg", [128, 2, 512], c=r3)
        cv = sb("cv", [128, 6, S], c=r3)
        dg = sb("dg", [128, 6, 128], c=r3)
        rope = sb("rope", [128, 2, 256], c=r3)
        r3.close()
        gap.close()
        g2 = ExitStack()
        qk2T = sb("qk2T", [128, 8, S], c=g2)
        par2 = sb("par2", [128, 1024 + 128 + 256], c=g2)
        ch = sb("ch", [128, 4, 288], c=g2)
        ca = sb("ca", [128, 4, S], c=g2)
        PT2 = sb("PT2", [128, 2, 512], c=g2)
        S2 = sb("S2", [128, 3, 384], c=g2)
        g2.close()

    b = [ctx.enter_context(nc.psum_tensor(f"b{i}", [128, 512], F32)) for i in range(3)]
    SS = ctx.enter_context(nc.psum_tensor("SS", [128, 1024], F32))
    TT = ctx.enter_context(nc.psum_tensor("TT", [128, 1024], F32))
    OO = ctx.enter_context(nc.psum_tensor("OO", [128, 512], F32))
    bank = {0: b[0][:], 1: b[1][:], 2: b[2][:], 3: SS[:, 0:512], 4: SS[:, 512:1024],
            5: TT[:, 0:512], 6: TT[:, 512:1024], 7: OO[:]}
    free = {i: [] for i in range(8)}

    PE = Queue(sem("s_pe"))
    AC = Queue(sem("s_act"))
    VE = Queue(sem("s_dve"))
    GP = Queue(sem("s_pool"))
    SP = Queue(sem("s_sp"))
    d_raw = [sem(f"d_raw{i}") for i in range(NRAW)]
    d_x = sem("d_x")
    d_x1 = sem("d_x1")
    d_par = sem("d_par")
    d_cst = sem("d_cst")
    d_cs1 = sem("d_cs1")
    d_par2 = sem("d_par2")
    d_out = sem("d_out")

    def dma(dst, src, s, *waits):
        def fn(e):
            e.dma_start(dst, src).then_inc(s, 16)
        SP.put(fn, *waits, sig=False)

    def pcol(name, i=0, n=1):
        o, w = PAR[name]
        return par[:, o + i:o + i + n]

    ident = cst[:, 0:128]
    maskF = cst[:, 128:384]

    def c1(name, a=0, n=None):
        o, w = CST[name]
        return cs1[:, o + a:o + a + (w - a if n is None else n)]

    _st = [0]

    def stat(n=1):
        a = _st[0]
        _st[0] += n
        assert _st[0] <= 384
        return st[:, a:a + n]

    units = []

    def add_unit(src, k0, kn, c0, n):
        v = src[k0 * 128:(k0 + kn) * 128, c0:c0 + n].rearrange("(k p) n -> p k n", p=128)
        units.append((v, kn, n))
        return len(units) - 1

    CH1 = [(0, 512), (512, 512), (1024, 512), (1536, 512), (2048, 512), (2560, 512), (3072, 512),
           (3584, 260), (3844, 512), (4356, 256)] + [(4612 + 512 * i, 512) for i in range(8)]
    u_p1 = [[add_unit(w_in, 0, 4, c, n), add_unit(w_in, 4, 4, c, n)] for c, n in CH1]
    u_br = [[add_unit(w_br, 4 * p, 4, 512 * h, 512) for p in range(2)] for h in range(2)]
    u_wo = [[add_unit(w_out, 4 * k, 4, 512 * n, 512) for n in range(2)] for k in range(2)]
    u_up, u_dn = {}, {}

    def plan_down(tab, w, j, kn):
        if kn == 4:
            tab[j] = [add_unit(w, 4 * j, 4, 512 * n, 512) for n in range(2)]
        else:
            tab[j] = [add_unit(w, 4 * j, kn, 0, 1024)]

    for j in range(8):
        u_up[j] = [add_unit(w_up, 4 * k, 4, 512 * j, 512) for k in range(2)]
        if j:
            plan_down(u_dn, w_dn, j - 1, 4)
    plan_down(u_dn, w_dn, 7, 4)
    CH2 = [(2048, 512), (0, 512), (512, 512), (1536, 512), (1024, 512)]
    u_p2 = [[add_unit(w_in2, 4 * k, 4, c, n) for k in range(2)] for c, n in CH2]
    u_wo2 = [[add_unit(w_out2, 4 * k, 4, 512 * n, 512) for n in range(2)] for k in range(2)]
    u_g2, u_u2, u_d2 = {}, {}, {}
    HC2 = [4, 4, 4, 4, 4, 2]
    for j in range(6):
        n = HC2[j] * 128
        u_g2[j] = [add_unit(w_g2, 4 * k, 4, 512 * j, n) for k in range(2)]
        u_u2[j] = [add_unit(w_u2, 4 * k, 4, 512 * j, n) for k in range(2)]
        if j:
            plan_down(u_d2, w_d2, j - 1, HC2[j - 1])
    plan_down(u_d2, w_d2, 5, 2)

    nu = len(units)
    hi_t, lo_t, pe_t = [None] * nu, [None] * nu, [None] * nu
    nxt = {"dma": 0, "split": 0}
    NPC = 2
    hi_k, lo_k = {}, {}

    def load(i):
        v, kn, n = units[i]
        s = i % NRAW
        w = [hi_t[i - NRAW], lo_t[i - NRAW]] if i >= NRAW else []
        dma(raw[:, s, 0:kn * n].rearrange("p (k n) -> p k n", k=kn), v, d_raw[s], w)

    def split_hi(i):
        v, kn, n = units[i]
        s, r = i % NSPL, i % NRAW
        m = kn * n
        landed = (d_raw[r], 16 * (i // NRAW + 1))
        old = pe_t[i - NSPL] if i >= NSPL else None
        if i < NPC:
            hi_k[i] = []
            for k in range(kn):
                hi_t[i] = AC.put(lambda e, k=k: e.copy(whi[:, s, k * n:k * n + n], raw[:, r, k * n:k * n + n]), landed)
                hi_k[i].append(hi_t[i])
            return
        hi_t[i] = AC.put(lambda e: e.copy(whi[:, s, 0:m], raw[:, r, 0:m]), landed, old)

    def split_lo(i):
        v, kn, n = units[i]
        s, r = i % NSPL, i % NRAW
        m = kn * n
        landed = (d_raw[r], 16 * (i // NRAW + 1))
        if i < NPC:
            lo_k[i] = []
            for k in range(kn):
                lo_t[i] = VE.put(lambda e, k=k: e.tensor_tensor(
                    wlo[:, s, k * n:k * n + n], raw[:, r, k * n:k * n + n], whi[:, s, k * n:k * n + n].bitcast(F32),
                    ALU.subtract), landed, hi_k[i][k])
                lo_k[i].append(lo_t[i])
        else:
            lo_t[i] = VE.put(lambda e: e.tensor_tensor(wlo[:, s, 0:m], raw[:, r, 0:m], whi[:, s, 0:m].bitcast(F32),
                                                       ALU.subtract), landed, hi_t[i])
        if nxt["dma"] < nu:
            load(nxt["dma"])
            nxt["dma"] += 1

    def prefetch(i):
        lows()
        while nxt["split"] < min(nu, i + LEAD):
            split_hi(nxt["split"])
            lo_due.append(nxt["split"])
            nxt["split"] += 1

    lo_due = []

    def lows():
        while lo_due:
            split_lo(lo_due.pop(0))

    def mm_unit(i, hi, lo, k0, t, out_of, first, last, waits, done, kr=None):
        lows()
        v, kn, n = units[i]
        s = i % NSPL
        H = whi[:, s, 0:kn * n].rearrange("p (k n) -> p k n", k=kn)
        L = wlo[:, s, 0:kn * n].rearrange("p (k n) -> p k n", k=kn)
        ws = ([] if i < NPC else [hi_t[i], lo_t[i]]) + list(waits)
        krs = list(range(kn)) if kr is None else list(kr)
        tok = None
        for c0 in range(0, n, 512):
            c1_ = min(n, c0 + 512)
            for kc in krs:
                dst = out_of(kc, c0)
                if i < NPC:
                    ws = ws + [hi_k[i][kc], lo_k[i][kc]]
                xh = hi[:, k0 + kc, t * 128:(t + 1) * 128]
                xl = lo[:, k0 + kc, t * 128:(t + 1) * 128]
                f = first(kc)
                for q, (a, w) in enumerate(((xh, H), (xh, L), (xl, H))):
                    tok = PE.put(_mm(dst, a, w[:, kc, c0:c1_], f and q == 0, last(kc) and q == 2), ws,
                                 sig=(kc == krs[-1] and q == 2 and c1_ == n))
                    ws = []
        if done:
            pe_t[i] = tok
        return tok

    def _mm(dst, a, w, start, stop):
        return lambda e: e.matmul(dst, a, w, start=start, stop=stop)

    def mm(dst, lhsT, rhs, start, stop, *waits, sig=True):
        return PE.put(_mm(dst, lhsT, rhs, start, stop), *waits, sig=sig)

    def tr(dst, src, *waits, sig=True):
        return PE.put(lambda e: e.transpose(dst, src, ident), *waits, sig=sig)

    active, pending = [], []
    cnt = {"O": 0, "S": 0, "P": 0, "B": 0, "T": 0}
    tg_free = [None, None]
    tgbuf = [PT]

    freed = []

    def rel(tab, k, toks):
        freed.append((tab, k, toks))

    def bg(start=1):
        for g in list(active):
            if next(g, "end") == "end":
                active.remove(g)
        for _ in range(start):
            if pending:
                g = pending.pop(0)
                if next(g, "end") != "end":
                    active.append(g)
        while freed:
            tab, k, toks = freed.pop(0)
            tab[k] = toks

    def bg_all():
        late()
        while active or pending:
            bg()

    def take(*bks):
        while any(free[k] is None for k in bks):
            yield
        w = [free[k] for k in bks]
        for k in bks:
            free[k] = None
        return w

    def take_one(*bks):
        while all(free[k] is None for k in bks):
            yield
        k = next(k for k in bks if free[k] is not None)
        w = free[k]
        free[k] = None
        return k, w

    def slot(frees):
        while all(f is None for f in frees):
            yield
        i = next(i for i, f in enumerate(frees) if f is not None)
        w = frees[i]
        frees[i] = None
        return i, w

    x_v = x_d.rearrange("(t p) d -> p t d", p=128)
    dma(xr[:, 0, :], x_v[:, 0, :], d_x)
    dma(cst[:, 0:128], cst_d[:, 0:128], d_cst)
    dma(par[:], par_d, d_par)
    dma(xr[:, 1, :], x_v[:, 1, :], d_x1)
    for i in range(NRAW):
        load(i)
        nxt["dma"] += 1
    dma(cst[:, 128:N0], cst_d[:, 128:N0], d_cs1)
    dma(cs1[:], cst_d[:, N0:N0 + N1], d_cs1)
    T_X, T_PAR, T_CST, T_CS1 = [(d_x, 16), (d_x1, 16)], (d_par, 16), (d_cst, 16), (d_cs1, 32)

    mhalf = stat(16)
    t_mh = GP.put(lambda e: e.memset(mhalf, -0.5))

    def rsqrt(src, n, count, t_src):
        v = stat(n)
        r = stat(n)
        a = VE.put(lambda e: e.tensor_scalar(v, src, 1.0 / count, EPS, ALU.mult, ALU.add), t_src)
        c = GP.put(lambda e: e.tensor_tensor(r, v, mhalf[:, 0:n], ALU.pow), a, t_mh)
        return r, c

    def sumsq(src, t_src, junk):
        o = stat(1)
        t = AC.put(lambda e: e.activation(junk, src, ACT.Square, accum_out=o), t_src)
        return o, t

    def turn_split(src, t_src, hi, lo, kc0, t, bk, gain=None, nk=4, post=None):
        tk = turn_pe(src, t_src, bk, nk)
        return turn_end(tk, hi, lo, kc0, t, bk, gain, nk)

    def turn_pe(src, t_src, bk, nk=4):
        w = [t_src, T_CST] + free[bk]
        for k in range(nk):
            tk = tr(bank[bk][:, 128 * k:128 * k + 128], src[:, 128 * k:128 * k + 128], w, sig=(k == nk - 1))
            w = []
        return tk

    def turn_end(tk, hi, lo, kc0, t, bk, gain, nk=4):
        ph = hi[:, kc0:kc0 + nk, t * 128:(t + 1) * 128]
        pl = lo[:, kc0:kc0 + nk, t * 128:(t + 1) * 128]
        ps = bank[bk][:, 0:128 * nk].rearrange("p (k q) -> p k q", k=nk)
        if gain is None:
            a = AC.put(lambda e: e.copy(ph, ps), tk)
            v = VE.put(lambda e: e.tensor_tensor(pl, ps, ph.bitcast(F32), ALU.subtract), a)
        else:
            i = cnt["T"] % 2
            cnt["T"] += 1
            w = tgbuf[0][:, i, 0:128 * nk].rearrange("p (k q) -> p k q", k=nk)
            m = VE.put(lambda e: e.tensor_tensor(w, ps, gain(kc0).unsqueeze(2).broadcast_to([128, nk, 128]), ALU.mult),
                       tk, T_PAR, tg_free[i])
            a = AC.put(lambda e: e.copy(ph, w), m)
            v = VE.put(lambda e: e.tensor_tensor(pl, w, ph.bitcast(F32), ALU.subtract), a)
            tg_free[i] = v
            free[bk] = [m]
            return [a, v]
        free[bk] = [a, v]
        return [a, v]

    A_t = {}
    xg = {}
    for t in range(2):
        for h in range(2):
            bk = 3 + h if t else 5 + h
            w = [T_X[t], T_CST]
            for k in range(4):
                o = 512 * h + 128 * k
                tk = tr(bank[bk][:, 128 * k:128 * k + 128], xr[:, t, o:o + 128], w, sig=(k == 3))
                w = []
            g = ys[:, t, 512 * h:512 * h + 512].rearrange("p (k q) -> p k q", k=4)
            ps = bank[bk].rearrange("p (k q) -> p k q", k=4)
            m = VE.put(lambda e, g=g, ps=ps, h=h: e.tensor_tensor(
                g, ps, pcol("g_mix", 4 * h, 4).unsqueeze(2).broadcast_to([128, 4, 128]), ALU.mult), tk, T_PAR)
            free[bk] = [m]
            xg[t, h] = (g, m)
        for h in range(2):
            g, m = xg[t, h]
            ph = Ahi[:, 4 * h:4 * h + 4, 128 * t:128 * t + 128]
            pl = Alo[:, 4 * h:4 * h + 4, 128 * t:128 * t + 128]
            a = AC.put(lambda e, g=g, ph=ph: e.copy(ph, g), m)
            v = VE.put(lambda e, g=g, ph=ph, pl=pl: e.tensor_tensor(pl, g, ph.bitcast(F32), ALU.subtract), a)
            A_t[t, h] = [a, v]
    prefetch(0)
    lows()
    ss1 = stat(2)
    tq = None
    for t in range(2):
        tq = AC.put(lambda e, t=t: e.activation(gates[:, t, 0:1024], xr[:, t, :], ACT.Square,
                                                accum_out=ss1[:, t:t + 1]), T_X)
    r1_, t_r1 = rsqrt(ss1, 2, D, tq)

    lamt = stat(2)
    lame = stat(2)
    lam = stat(1)
    nlam = stat(1)
    lo_, _ = PAR["lam"]
    lscr = stat(64)
    ta = VE.put(lambda e: e.tensor_tensor(lscr, par[:, lo_:lo_ + 64], par[:, lo_ + 64:lo_ + 128], ALU.mult), T_PAR)
    ta = VE.put(lambda e: e.tensor_reduce(lamt, lscr.rearrange("p (a b) -> p a b", a=2), AX.X, ALU.add), ta)
    ta = AC.put(lambda e: e.activation(lame, lamt, ACT.Exp), ta)
    ta = VE.put(lambda e: e.tensor_tensor(lam, lame[:, 0:1], lame[:, 1:2], ALU.subtract), ta)
    t_nlam = VE.put(lambda e: e.tensor_scalar(nlam, lam, -1.0, -0.2, ALU.mult, ALU.add), ta)

    rot = [0]
    later = []

    after = []

    def late(hold=False):
        while later:
            later.pop(0)()
        while after and not hold:
            after.pop(0)()

    def chunk(us, hi, lo, src_t, evac, first_of_phase=False, start=1):
        n = units[us[0]][2]
        bks = []
        for t in range(2):
            bks.append(rot[0] % 2)
            rot[0] += 1
        order = [(0, 0), (1, 0), (0, 1), (1, 1)] if first_of_phase else [(0, 0), (0, 1), (1, 0), (1, 1)]
        for ui, t in order:
            bk = bks[t]
            w = list(src_t[t, ui])
            if ui == 0:
                w += free[bk]
                free[bk] = []
            tk = mm_unit(us[ui], hi, lo, 4 * ui, t, lambda kc, c0, bk=bk: bank[bk][:, 0:n],
                         lambda kc, ui=ui: ui == 0 and kc == 0, lambda kc, ui=ui: ui == 1 and kc == 3, w, t == 1)
            if t == 1:
                prefetch(us[ui] + 1)
            late()
            if ui == 1:
                later.append(lambda t=t, bk=bk, tk=tk: evac(t, bk, tk, n))
            bg(start)

    qk_t = {}
    V_t = {}
    PAIRS = {0: [(0, "qk", 0, 0.125), (256, "qk", 2, 1.0)],
             1: [(0, "v", 0, None), (256, "qk", 4, 0.125)],
             2: [(0, "qk", 6, 0.125), (256, "qk", 8, 0.125)],
             3: [(0, "qk", 10, 1.0), (256, "qk", 12, 1.0)],
             4: [(0, "qk", 14, 1.0), (256, "v", 256, None)],
             5: [(0, "v", 512, None), (256, "v", 768, None)],
             6: [(0, "qk", 16, 0.125), (256, "qk", 18, 1.0)],
             7: [(0, "v", 1024, None)],
             8: [(0, "qk", 20, 32 ** -0.5), (256, "qk", 22, 1.0)],
             9: [(0, "v", 1280, None)]}
    f_t = {}
    ff = stat(8)
    stage_free = {5: [], 7: [], 9: []}

    def qk_tile(i):
        return qkA[:, i, :] if i < 16 else qkB[:, i - 16, :]

    def turn_pairs(c, t_stage):
        sg = gates[:, :, 1024 + 512 * (c % 6):1536 + 512 * (c % 6)]
        done = []
        for col, kind, dst, sc in PAIRS[c]:
            if kind != "qk":
                continue
            bk = 5 + (dst // 2) % 2
            w = yield from take(bk)
            w = [t_stage[0], t_stage[1], w]
            for j in range(2):
                for t in range(2):
                    tk = tr(bank[bk][:, 256 * j + 128 * t:256 * j + 128 * t + 128],
                            sg[:, t, col + 128 * j:col + 128 * j + 128], w, sig=(j == 1 and t == 1))
                    w = []
            done.append(tk)
            yield
            q = qkA[:, dst:dst + 2, :] if dst < 16 else qkB[:, dst - 16:dst - 14, :]
            src = bank[bk].rearrange("p (j q) -> p j q", j=2)
            if (dst // 2) % 2 == 0:
                tv = VE.put(lambda e, q=q, src=src, sc=sc: e.tensor_scalar(q, src, sc, None, ALU.mult), tk)
            else:
                tv = AC.put(lambda e, q=q, src=src, sc=sc: e.mul(q, src, sc), tk)
            rel(free, bk, [tv])
            qk_t[dst] = qk_t[dst + 1] = tv
        stage_free[c] = [done[-1]]

    def evac1(c):
        def fn(t, bk, tk, n):
            ts = []
            for col, kind, dst, sc in PAIRS[c]:
                if kind == "v":
                    o = V[:, t, dst:dst + 256]
                    w = []
                else:
                    a = 1024 + 512 * (c % 6) + col
                    o = gates[:, t, a:a + 256]
                    w = stage_free[c - 6] if c >= 6 else []
                tv = AC.put(lambda e, o=o, col=col: e.mul(o, bank[bk][:, col:col + 256], r1_[:, t:t + 1]), tk, t_r1, w)
                if kind == "v":
                    V_t[dst, t] = tv
                else:
                    stg[c, t] = tv
                ts.append(tv)
            if c == 7:
                tv = VE.put(lambda e: e.scalar_tensor_tensor(
                    out=ff[:, 4 * t:4 * t + 4], in0=bank[bk][:, 256:260], scalar=r1_[:, t:t + 1],
                    in1=pcol("b_f", 0, 4), op0=ALU.mult, op1=ALU.add), tk, tv, t_r1, T_PAR)
                f_t[t] = tv
                ts.append(tv)
            free[bk] = ts
            if t == 1 and any(k == "qk" for _, k, _, _ in PAIRS[c]):
                active.insert(0, turn_pairs(c, [stg[c, 0], stg[c, 1]]))
            if t == 1:
                if c == 1:
                    pending.extend(sb_task(h) for h in range(4))
                if c == 5:
                    pending.extend(dil_task(h, qb) for h in range(4) for qb in range(2))
                if c == 7:
                    pending.append(forget_gates())
                    pending.extend(fox_task(h, qb) for h in range(4) for qb in range(2))
                if c == 9:
                    for h_ in range(4):
                        pending.extend(diff_task(h_, qb) for qb in range(2))
                        if h_ == 1:
                            pending.extend(turn_task(ys[:, t_, 0:512], [(a_, i_, t_) for a_ in (0, 1) for i_ in range(4)],
                                                     Bhi, Blo, 0, t_, B_t, [(2, 0, 0)]) for t_ in range(2))
                    for t_ in range(2):
                        pending.append(diff_norm(t_))
                        pending.append(turn_task(ys[:, t_, 512:1024], [(2, h_, t_) for h_ in range(4)] + [("d", t_)],
                                                 Bhi, Blo, 4, t_, B_t))
        return fn

    stg = {}
    Sb_free = [[], []]
    PT_free = [[tg_free[0]], [tg_free[1]]]
    ys_t = {}

    def sb_task(h):
        qt, kt, p = h // 2, 2 + h // 2, 64 * (h % 2)
        Q, K = qkA[p:p + 64, qt, :], qkA[p:p + 64, kt, :]
        while kt not in qk_t:
            yield
        bk, wb = yield from take_one(3, 4)
        Z = bank[bk]
        mm(Z[:, 0:256], K[:, 0:128], Q[:, 0:256], True, True, qk_t[qt], qk_t[kt], wb, sig=False)
        tz = mm(Z[:, 256:384], K[:, 128:256], Q[:, 128:256], True, True)
        yield
        si, ws = yield from slot(Sb_free)
        zm, L = Sb[:, si, 0:384], Sb[:, si, 384:768]
        t = VE.put(lambda e: e.tensor_tensor(zm, Z[:, 0:384], c1("MB"), ALU.add), tz, T_CS1, ws)
        rel(free, bk, [t])
        a = AC.put(lambda e: e.activation(L, zm, ACT.Abs), t)
        a = AC.put(lambda e: e.activation(L, L, ACT.Exp, scale=-1.0), a)
        a = AC.put(lambda e: e.activation(L, L, ACT.Ln, bias=1.0), a)
        yield
        t = VE.put(lambda e: e.scalar_tensor_tensor(out=L, in0=zm, scalar=0.0, in1=L, op0=ALU.max, op1=ALU.add), a)
        yield
        bk, wb = yield from take_one(5, 6)
        R = bank[bk]
        mm(R[:, 0:384], c1("LG"), L, True, False, t, wb, sig=False)
        tr_ = mm(R[:, 128:256], c1("UO", 128, 128), L[:, 256:384], False, True)
        yield
        t = VE.put(lambda e: e.tensor_tensor(zm, zm, R[:, 0:384], ALU.subtract), tr_)
        rel(free, bk, [t])
        a = AC.put(lambda e: e.activation(zm, zm, ACT.Exp), t)
        yield
        ob, wo = yield from take_one(2, 7)
        o0, o1 = bank[ob][:, 0:64], bank[ob][:, 64:128]
        v = V[:, :, 64 * h:64 * h + 64]
        t0 = mm(o0, zm[:, 0:128], v[:, 0, :], True, True, a, V_t[0, 0], V_t[0, 1], wo)
        mm(o1, zm[:, 128:256], v[:, 0, :], True, False, sig=False)
        t1 = mm(o1, zm[:, 256:384], v[:, 1, :], False, True)
        rel(Sb_free, si, [t1])
        yield
        for qb, o in ((0, o0), (1, o1)):
            ys_t[0, h, qb] = VE.put(
                lambda e, qb=qb, o=o: e.tensor_copy(ys[:, qb, 64 * h:64 * h + 64], o), t1, [A_t[k] for k in A_t])
        rel(free, ob, [ys_t[0, h, 1]])

    def softmax_tail(P, segs, ptr, kn, vs, vw, l, t_exp, write, si, sfree):
        n = len(vs)
        if n > 4:
            wb = yield from take(5, 6)
            bt, T = 5, TT
        else:
            bt, wb = yield from take_one(5, 6)
            T = bank[bt]
        w = [t_exp, wb]
        for j in range(n):
            tk = tr(T[:, 128 * j:128 * j + 128], P[:, 128 * j:128 * j + 128], w, sig=(j == n - 1))
            w = []
        rel(sfree, si, [tk])
        yield
        m = 128 * n
        pi, wp = yield from slot(PT_free)
        te = AC.put(lambda e: e.copy(ptr[:, pi, 0:m], T[:, 0:m]), tk, wp)
        rel(free, bt, [te])
        if n > 4:
            rel(free, 6, [te])
        rl = stat_l[cnt["P"] % 8]
        cnt["P"] += 1
        trl = VE.put(lambda e: e.reciprocal(rl, l), t_exp)
        yield
        ob, wo = yield from take_one(2, 7)
        o = bank[ob][:, 0:64]
        w = [te, vw, wo]
        for j in range(n):
            tk = mm(o, ptr[:, pi, 128 * j:128 * j + 128], vs[j], j == 0, j == n - 1, w, sig=(j == n - 1))
            w = []
        rel(PT_free, pi, [tk])
        yield
        rel(free, ob, [write(o, rl, [tk, trl])])

    stat_l = [stat(1) for _ in range(8)]
    stat_m = [stat(2) for _ in range(8)]
    stat_s = [stat(2) for _ in range(8)]

    def dil_task(h, qb):
        kn = qb + 1
        m = 128 * kn
        off = 0 if qb == 0 else 128
        while 14 not in qk_t:
            yield
        w = yield from take(3, 4)
        w = [w] + [qk_t[i] for i in (4, 6, 8, 10, 12, 14)]
        p = 64 * (h % 2)
        for g in range(3):
            q, k = 4 + 2 * g + h // 2, 10 + 2 * g + h // 2
            tk = mm(SS[:, m * g:m * g + m], qkA[p:p + 64, q, 128 * qb:128 * qb + 128], qkA[p:p + 64, k, 0:m],
                    True, True, w, sig=(g == 2))
            w = []
        yield
        si, ws = yield from slot(Sb_free)
        P = Sb[:, si, 0:3 * m]
        for g in range(3):
            t = VE.put(lambda e, g=g: e.scalar_tensor_tensor(
                out=P[:, m * g:m * g + m], in0=c1("DD", 384 * g + off, m), scalar=-SL_DIL[g][h],
                in1=SS[:, m * g:m * g + m], op0=ALU.mult, op1=ALU.add), tk, T_CS1, ws)
        rel(free, 3, [t])
        rel(free, 4, [t])
        i = cnt["S"] % 8
        cnt["S"] += 1
        nm, l = stat_m[i][:, 0:1], stat_s[i][:, 0:1]
        t = VE.put(lambda e: e.tensor_reduce(nm, P, AX.X, ALU.max, negate=True), t)
        te = AC.put(lambda e: e.activation(P, P, ACT.Exp, bias=nm, accum_out=l), t)
        yield
        vs = [V[:, kb, 256 + 256 * g + 64 * h:320 + 256 * g + 64 * h] for g in range(3) for kb in range(kn)]
        vw = [V_t[256 * g, t_] for g in (1, 2, 3) for t_ in range(2)]

        def write(o, rl, w):
            ys_t[1, h, qb] = VE.put(lambda e: e.tensor_scalar(ys[:, qb, 256 + 64 * h:320 + 64 * h], o, rl, None,
                                                              ALU.mult), w)
            return ys_t[1, h, qb]

        yield from softmax_tail(P, None, PT, kn, vs, vw, l, te, write, si, Sb_free)

    cumq = stat(8)
    lf = stat(8)
    fox = {}

    def forget_gates():
        e1 = stat(8)
        a = AC.put(lambda e: e.activation(e1, ff, ACT.Abs), f_t[0], f_t[1])
        a = AC.put(lambda e: e.activation(e1, e1, ACT.Exp, scale=-1.0), a)
        a = AC.put(lambda e: e.activation(e1, e1, ACT.Ln, bias=1.0), a)
        yield
        t = VE.put(lambda e: e.scalar_tensor_tensor(out=lf, in0=ff, scalar=0.0, in1=e1, op0=ALU.min,
                                                    op1=ALU.subtract), a)
        fox["lf"] = t
        yield
        ob, wo = yield from take_one(2, 7)
        o0, o1 = bank[ob][:, 0:64], bank[ob][:, 64:128]
        mm(o0[:, 0:4], c1("UO", 0, 128), lf[:, 0:4], True, True, t, T_CS1, wo, sig=False)
        mm(o1[:, 0:4], c1("UO", 128, 128), lf[:, 0:4], True, False, sig=False)
        tk = mm(o1[:, 0:4], c1("UO", 0, 128), lf[:, 4:8], False, True)
        yield
        VE.put(lambda e: e.tensor_copy(cumq[:, 0:4], o0[:, 0:4]), tk)
        fox["cq"] = VE.put(lambda e: e.tensor_copy(cumq[:, 4:8], o1[:, 0:4]), tk)
        rel(free, ob, [fox["cq"]])

    nlf_free = [[]]

    def fox_task(h, qb):
        while "cq" not in fox or (qb == 1 and ("b", h, 1) not in fox):
            yield
        if qb == 0:
            _, wn = yield from slot(nlf_free)
            for t_ in range(2):
                src = lf[:, 4 * t_ + h:4 * t_ + h + 1]
                fox["b", h, t_] = VE.put(lambda e, src=src, t_=t_: e.tensor_scalar(
                    nlf[:, t_, :], c1("UO", 128, 128), src, -1.0, ALU.mult, ALU.mult), fox["lf"], wn, T_CS1)
            yield
        kn = qb + 1
        m = 128 * kn
        while 18 not in qk_t:
            yield
        bk, wb = yield from take_one(3, 4)
        Z = bank[bk]
        p = 64 * (h % 2)
        q, k = h // 2, 2 + h // 2
        mm(Z[:, 0:m], qkB[p:p + 64, q, 128 * qb:128 * qb + 128], qkB[p:p + 64, k, 0:m], True, False,
           wb, qk_t[16], qk_t[18], sig=False)
        tk = mm(Z[:, 0:m], nlf[:, 0, :], c1("UO", 0, m), False, qb == 0, fox["b", h, 0], fox["b", h, 1])
        if qb == 1:
            tk = mm(Z[:, 128:256], nlf[:, 1, :], c1("UO", 0, 128), False, True)
        fox["r", h, qb] = tk
        if ("r", h, 1 - qb) in fox:
            rel(nlf_free, 0, [fox["r", h, 0], fox["r", h, 1]])
        yield
        si, ws = yield from slot(Sb_free)
        P = Sb[:, si, 0:m]
        t = VE.put(lambda e: e.scalar_tensor_tensor(
            out=P, in0=Z[:, 0:m], scalar=cumq[:, 4 * qb + h:4 * qb + h + 1], in1=maskF[:, 256 - m:256],
            op0=ALU.add, op1=ALU.add), tk, ws, fox["cq"])
        rel(free, bk, [t])
        i = cnt["S"] % 8
        cnt["S"] += 1
        nm, l = stat_m[i][:, 0:1], stat_s[i][:, 0:1]
        t = VE.put(lambda e: e.tensor_reduce(nm, P, AX.X, ALU.max, negate=True), t)
        te = AC.put(lambda e: e.activation(P, P, ACT.Exp, bias=nm, accum_out=l), t)
        yield
        vs = [V[:, kb, 1024 + 64 * h:1088 + 64 * h] for kb in range(kn)]

        def write(o, rl, w):
            ys_t[2, h, qb] = VE.put(lambda e: e.tensor_scalar(ys[:, qb, 512 + 64 * h:576 + 64 * h], o, rl, None,
                                                              ALU.mult), w)
            return ys_t[2, h, qb]

        yield from softmax_tail(P, None, PT, kn, vs, [V_t[1024, 0], V_t[1024, 1]], l, te, write, si, Sb_free)

    lc = [stat(1) for _ in range(8)]

    def diff_task(h, qb):
        kn = qb + 1
        m = 128 * kn
        off = 0 if qb == 0 else 128
        while 22 not in qk_t:
            yield
        bk, wb = yield from take_one(3, 4)
        Z = bank[bk]
        w = [wb, qk_t[20], qk_t[22]]
        for c in range(2):
            p = 64 * (h % 2) + 32 * c
            tk = mm(Z[:, m * c:m * c + m], qkB[p:p + 32, 4 + h // 2, 128 * qb:128 * qb + 128],
                    qkB[p:p + 32, 6 + h // 2, 0:m], True, True, w)
            w = [tk]
        yield
        si, ws = yield from slot(Sb_free)
        P = Sb[:, si, 0:2 * m]
        for c in range(2):
            t = VE.put(lambda e, c=c: e.scalar_tensor_tensor(
                out=P[:, m * c:m * c + m], in0=c1("DD", 1152 + off, m), scalar=-SL_DIFF[h],
                in1=Z[:, m * c:m * c + m], op0=ALU.mult, op1=ALU.add), tk, T_CS1, ws)
        rel(free, bk, [t])
        i = cnt["S"] % 8
        cnt["S"] += 1
        nm, l = stat_m[i], stat_s[i]
        t = VE.put(lambda e: e.tensor_reduce(nm, P.rearrange("p (c k) -> p c k", c=2), AX.X, ALU.max, negate=True), t)
        for c in range(2):
            te = AC.put(lambda e, c=c: e.activation(P[:, m * c:m * c + m], P[:, m * c:m * c + m], ACT.Exp,
                                                    bias=nm[:, c:c + 1], accum_out=l[:, c:c + 1]), t)
        yield
        co = lc[i]
        t = VE.put(lambda e: e.reciprocal(co, l[:, 1:2]), te)
        t = VE.put(lambda e: e.scalar_tensor_tensor(out=co, in0=co, scalar=l[:, 0:1], in1=nlam, op0=ALU.mult,
                                                    op1=ALU.mult), t, t_nlam)
        t = VE.put(lambda e: e.scalar_tensor_tensor(out=P[:, 0:m], in0=P[:, m:2 * m], scalar=co, in1=P[:, 0:m],
                                                    op0=ALU.mult, op1=ALU.add), t)
        yield
        vs = [V[:, kb, 1280 + 64 * h:1344 + 64 * h] for kb in range(kn)]

        def write(o, rl, w):
            ys_t[3, h, qb] = VE.put(lambda e: e.tensor_scalar(ys[:, qb, 768 + 64 * h:832 + 64 * h], o, rl, None,
                                                              ALU.mult), w)
            return ys_t[3, h, qb]

        yield from softmax_tail(P, None, PT, kn, vs, [V_t[1280, 0], V_t[1280, 1]], l[:, 0:1], t, write, si, Sb_free)

    nsq_free = []

    def diff_norm(qb):
        while any((3, h, qb) not in ys_t for h in range(4)):
            yield
        yd = ys[:, qb, 768:1024]
        y3 = yd.rearrange("p (h d) -> p h d", h=4)
        sq = nsq[:]
        rs4 = stat(4)
        t = VE.put(lambda e: e.tensor_tensor(sq, yd, yd, ALU.mult), [ys_t[3, h, qb] for h in range(4)], nsq_free)
        t = VE.put(lambda e: e.tensor_reduce(rs4, sq.rearrange("p (h d) -> p h d", h=4), AX.X, ALU.add), t)
        nsq_free[:] = [t]
        r, tp = rsqrt(rs4, 4, 64, t)
        yield
        t = VE.put(lambda e: e.tensor_tensor(y3, y3, r.unsqueeze(2).broadcast_to([128, 4, 64]), ALU.mult), tp)
        t = VE.put(lambda e: e.scalar_tensor_tensor(
            out=y3, in0=y3, scalar=0.8, in1=pcol("g_diff", 0, 64).unsqueeze(1).broadcast_to([128, 4, 64]),
            op0=ALU.mult, op1=ALU.mult), t)
        ys_t["d", qb] = t

    def turn_task(src, keys, hi, lo, kc0, t, out, prior=()):
        while any(k not in ys_t for k in keys):
            yield
        bk, wb = yield from take_one(5, 6)
        w = [[ys_t[k] for k in keys], wb, [ys_t[k] for k in prior]]
        for k in range(4):
            tk = tr(bank[bk][:, 128 * k:128 * k + 128], src[:, 128 * k:128 * k + 128], w, sig=(k == 3))
            w = []
        yield
        ph = hi[:, kc0:kc0 + 4, t * 128:(t + 1) * 128]
        pl = lo[:, kc0:kc0 + 4, t * 128:(t + 1) * 128]
        ps = bank[bk].rearrange("p (k q) -> p k q", k=4)
        a = AC.put(lambda e: e.copy(ph, ps), tk)
        v = VE.put(lambda e: e.tensor_tensor(pl, ps, ph.bitcast(F32), ALU.subtract), a)
        rel(free, bk, [a, v])
        out[t, kc0 // 4] = [a, v]

    B_t = {}

    prefetch(u_p1[0][0])
    g_t = {}

    def evac_gate(c):
        def fn(t, bk, tk, n):
            o = gates[:, t, 512 * c:512 * c + 512]
            w = [[stage_free[k] for k in range(10)], None]
            free[bk] = [AC.put(lambda e: e.mul(o, bank[bk], r1_[:, t:t + 1]), tk, t_r1, w[0], w[1])]
            g_t[c, t] = free[bk][0]
        return fn

    for c in range(18):
        chunk(u_p1[c], Ahi, Alo, A_t, evac1(c) if c < 10 else evac_gate(c - 10), first_of_phase=(c == 0))
    tgbuf[0] = tg

    mix_t = {}
    sig_t = {}
    M_t = {}
    W_acc = {(0, 0): 3, (1, 0): 4, (0, 1): 7, (1, 1): 0}

    def gated(u, n, hf, t, sg, tsg, bk, tk):
        mx = ys[:, t, 512 * hf:512 * hf + 512]
        if n == 0:
            v = VE.put(lambda e: e.tensor_tensor(mx, sg[:, t, :], bank[bk], ALU.mult), tk, tsg, B_t[t, hf])
            free[bk] = [v]
        else:
            v = VE.put(lambda e: e.tensor_tensor(sg[:, t, :], sg[:, t, :], bank[bk], ALU.mult), tk, tsg)
            free[bk] = [v]
            v = (VE if n == 3 else GP).put(lambda e: e.tensor_tensor(mx, mx, sg[:, t, :], ALU.add), v, mix_t[t, hf])
        mix_t[t, hf] = v

    for hf in range(2):
        for n in range(4):
            if hf == 0 and n == 2:
                bg_all()
            sg = gates[:, :, 1024 * n + 512 * hf:1024 * n + 512 * hf + 512]
            for m in range(4 * hf + n, min(8, 4 * hf + n + 2)):
                if m not in sig_t:
                    o = 1024 * (m % 4) + 512 * (m // 4)
                    sig_t[m] = AC.put(lambda e, o=o: e.activation(gates[:, :, o:o + 512], gates[:, :, o:o + 512],
                                                                  ACT.Sigmoid),
                                      g_t[2 * (m % 4) + m // 4, 0], g_t[2 * (m % 4) + m // 4, 1])
            tsg = sig_t[4 * hf + n]
            u = u_br[hf][n // 2]
            kr = range(2 * (n % 2), 2 * (n % 2) + 2)
            for t in range(2):
                bk = rot[0] % (2 if hf == 0 and n < 2 else 3)
                rot[0] += 1
                while (t, n // 2) not in B_t:
                    bg()
                tk = mm_unit(u, Bhi, Blo, 4 * (n // 2), t, lambda kc, c0, bk=bk: bank[bk],
                             lambda kc, kr=kr: kc == kr[0], lambda kc, kr=kr: kc == kr[-1],
                             B_t[t, n // 2] + free[bk], t == 1 and n % 2 == 1, kr=kr)
                late()
                later.append(lambda u=u, n=n, hf=hf, t=t, sg=sg, tsg=tsg, bk=bk, tk=tk: gated(
                    u, n, hf, t, sg, tsg, bk, tk))
                free[bk] = []
                if active or pending:
                    bg()
            if n % 2 == 1:
                prefetch(u + 1)
            if hf == 1 and n in (0, 1):
                t = n
                M_t[t, 0] = turn_split(ys[:, t, 0:512], mix_t[t, 0], Ahi, Alo, 0, t, 5 + t)
    late()
    t_gfree = [(VE.sem, VE.n), (GP.sem, GP.n)]

    def out_proj(us, hi, lo, src_t, mid, ts, turn):
        for n in range(2):
            for t in range(2):
                bk = W_acc[t, n]
                lows()
                while (t, 0) not in src_t or free[bk] is None:
                    bg()
                mm_unit(us[0][n], hi, lo, 0, t, lambda kc, c0, bk=bk: bank[bk],
                        lambda kc: kc == 0, lambda kc: False, src_t[t, 0] + free[bk], t == 1)
                free[bk] = []
                late()
                if active or pending:
                    bg()
                if n == 1 and t == 0:
                    mid()
            prefetch(us[0][n] + 1)
        for t in range(2):
            for n in range(2):
                bk = W_acc[t, n]
                while (t, 1) not in src_t:
                    bg()
                if not ys_free:
                    ys_free[:] = [PE_last(PE)]
                tk = mm_unit(us[1][n], hi, lo, 4, t, lambda kc, c0, bk=bk: bank[bk],
                             lambda kc: False, lambda kc: kc == 3, src_t[t, 1], t == 1)
                if t == 1:
                    prefetch(us[1][n] + 1)
                late(True)
                xs = xr[:, t, 512 * n:512 * n + 512]
                v = VE.put(lambda e, xs=xs, bk=bk: e.tensor_tensor(xs, xs, bank[bk], ALU.add), tk, x_w[t])
                free[bk] = [v]
                ts[t, n] = v
                late()
                if active or pending:
                    bg()
                later.append(turn(t, n))

    x_w = [[tq], [tq]]

    def mid1():
        for t in range(2):
            M_t[t, 1] = turn_split(ys[:, t, 512:1024], mix_t[t, 1], Ahi, Alo, 4, t, 5 + t)
        ys_free[:] = [PE_last(PE)]

    def norm_turn(ts, hi, lo, gain, H, o, extra=None):
        def turn(t, n):
            def fn():
                tk = turn_pe(xr[:, t, 512 * n:512 * n + 512], [ts[t, n], extra], 5 + n)
                after.append(lambda: end(tk))
                sq_t[id(o), t, n] = AC.put(lambda e: e.activation(
                    ys[:, t, 512 * n:512 * n + 512], xr[:, t, 512 * n:512 * n + 512], ACT.Square,
                    accum_out=o[:, 2 * t + n:2 * t + n + 1]), ts[t, n], ys_free)

            def end(tk):
                H[t, n] = turn_end(tk, hi, lo, 4 * n, t, 5 + n, gain)
            return fn
        return turn

    sq_t = {}
    ys_free = []
    o2, o3, o4, o5 = stat(4), stat(4), stat(4), stat(4)

    def x_stats(o):
        w = [sq_t[id(o), t, n] for t in range(2) for n in range(2)]
        sm = stat(2)
        v = VE.put(lambda e: e.tensor_tensor(sm, o.rearrange("p (t n) -> p t n", n=2)[:, :, 0],
                                             o.rearrange("p (t n) -> p t n", n=2)[:, :, 1], ALU.add), w)
        return rsqrt(sm, 2, D, v), w

    x1_t, H_t = {}, {}
    ys_free[:] = [mix_t[t, h] for t in range(2) for h in range(2)]
    out_proj(u_wo, Ahi, Alo, M_t, mid1, x1_t, norm_turn(x1_t, Bhi, Blo, lambda k: pcol("g_mlp", k, 4), H_t, o2))

    dma(par2[:], par2_d, d_par2, t_gfree)
    T_P2 = (d_par2, 16)

    RT = rope[:, 0, :]
    RT2 = rope[:, 1, :]

    diag = []
    diag += [V2[:, i // 4, 128 * (i % 4):128 * (i % 4) + 128] for i in range(8)]
    diag += [dg[:, i, :] for i in range(6)]
    diag_t = []
    diag_u = {}

    def diagonals(a, b_):
        for i in range(a, b_):
            diag_t[:] = [VE.put(lambda e, i=i: e.tensor_scalar(diag[i], ident, pcol("dw_w", 93 + i), None, ALU.mult),
                                t_gfree, T_PAR)]

    def rope_tables():
        t_rt = None
        for qk in range(2):
            g = par2[:, 1024 + 64 * qk:1088 + 64 * qk]
            for t in range(2):
                o = (qk * 2 + t) * 64
                VE.put(lambda e, o=o, g=g, t=t: e.tensor_tensor(RT[:, o:o + 64], par2[:, 1152 + 64 * t:1216 + 64 * t], g,
                                                                ALU.mult), T_P2)
                VE.put(lambda e, o=o, g=g, t=t: e.tensor_tensor(
                    RT2[:, o:o + 32], par2[:, 1280 + 64 * t:1312 + 64 * t], g[:, 32:64], ALU.mult))
                t_rt = VE.put(lambda e, o=o, g=g, t=t: e.tensor_tensor(
                    RT2[:, o + 32:o + 64], par2[:, 1312 + 64 * t:1344 + 64 * t], g[:, 0:32], ALU.mult))
        return t_rt

    h_free = [[], []]
    u_free = [[], []]

    def ffn_down(us, j, nj, hid_t, last, turn=None):
        kn = nj_of(us, j)
        hi, lo = hhi[:, j % 2], hlo[:, j % 2]
        if len(us[j]) == 2:
            seq = [(n, t) for t in range(2) for n in range(2)] if last else [(n, t) for n in range(2) for t in range(2)]
            for n, t in seq:
                bk = W_acc[t, n]
                w = hid_t[t] + (free[bk] if j == 0 else [])
                tk = mm_unit(us[j][n], hi, lo, 0, t, lambda kc, c0, bk=bk: bank[bk],
                             lambda kc: j == 0 and kc == 0, lambda kc: last and kc == 3, w, t == 1)
                if j == 0:
                    free[bk] = []
                if t == 1:
                    prefetch(us[j][n] + 1)
                if last:
                    late(True)
                    nj(t, n, tk)
                late()
                if last and turn:
                    later.append(turn(t, n))
        else:
            for t in range(2):
                tk = mm_unit(us[j][0], hi, lo, 0, t, lambda kc, c0, t=t: bank[W_acc[t, c0 // 512]],
                             lambda kc: False, lambda kc: last and kc == kn - 1, hid_t[t], t == 1)
                for n in range(2):
                    nj(t, n, tk)
            prefetch(us[j][0] + 1)
        h_free[j % 2] = [tk]

    def nj_of(us, j):
        return units[us[j][0]][1]

    def residual(ts):
        def fn(t, n, tk):
            bk = W_acc[t, n]
            xs = xr[:, t, 512 * n:512 * n + 512]
            v = VE.put(lambda e: e.tensor_tensor(xs, xs, bank[bk], ALU.add), tk, x_w[t])
            free[bk] = [v]
            ts[t, n] = v
        return fn

    def up_product(us, hi, lo, src_t, order_first, evac):
        n = units[us[0]][2]
        order = [(0, 0), (1, 0), (0, 1), (1, 1)] if order_first else [(0, 0), (0, 1), (1, 0), (1, 1)]
        for ui, t in order:
            bk = 1 + t
            w = list(src_t[t, ui])
            if ui == 0:
                w += free[bk]
                free[bk] = []
            tk = mm_unit(us[ui], hi, lo, 4 * ui, t, lambda kc, c0, bk=bk: bank[bk][:, 0:n],
                         lambda kc, ui=ui: ui == 0 and kc == 0, lambda kc, ui=ui: ui == 1 and kc == 3, w, t == 1)
            if t == 1:
                prefetch(us[ui] + 1)
            late()
            if ui == 1:
                later.append(lambda t=t, bk=bk, tk=tk: evac(t, bk, tk, n))

    ST = {}

    gg = stat(8)
    t_gg = VE.put(lambda e: e.tensor_tensor(gg, pcol("g_fin", 0, 8), pcol("g_n1", 0, 8), ALU.mult), T_PAR)

    def turn2(t, n):
        xs = xr[:, t, 512 * n:512 * n + 512]
        ju = ys[:, t, 512 * n:512 * n + 512]
        a = AC.put(lambda e: e.activation(ju, xs, ACT.Square, accum_out=o3[:, 2 * t + n:2 * t + n + 1]), x2_t[t, n],
                   ys_free)
        sq_t[id(o3), t, n] = a
        tk = turn_pe(xs, [x2_t[t, n], t_gg], 5 + n)
        v = GP.put(lambda e: e.tensor_tensor(xs, xs, par2[:, 512 * n:512 * n + 512], ALU.mult), a, tk, T_P2)

        def end():
            H2_t[t, n] = turn_end(tk, Ahi, Alo, 4 * n, t, 5 + n, lambda k: gg[:, k:k + 4])
            sq_t[4, t, n] = AC.put(lambda e: e.activation(ju, xs, ACT.Square,
                                                          accum_out=o4[:, 2 * t + n:2 * t + n + 1]), v)

        after.append(end)

    def stats1():
        (ST["r2"], ST["t_r2"]), ta = x_stats(o2)
        x_w[0], x_w[1] = ta, ta

    later.append(lambda: after.append(stats1))
    x2_t, H2_t = {}, {}
    hid_t = {}
    for j in range(8):
        up_t = {}

        def ev(t, bk, tk, n, j=j):
            o = ust[:, j % 2, t, :]
            r = ST["r2"]
            a = AC.put(lambda e: e.activation(o, bank[bk], ACT.Relu, scale=r[:, t:t + 1]), tk, ST["t_r2"],
                       u_free[j % 2])
            free[bk] = [a]
            up_t[t] = AC.put(lambda e: e.activation(o, o, ACT.Square), a)

        up_product(u_up[j], Bhi, Blo, H_t, j == 0, ev)
        if j == 2:
            t_rt = rope_tables()
        if 3 <= j < 7:
            diagonals(8 * (j - 3), min(8 * (j - 3) + 8, len(diag)))
        if j:
            ffn_down(u_dn, j - 1, None, hid_t[j - 1], False)
        late()
        hid_t[j] = {}
        for t in range(2):
            free[5 + t] = free[5 + t] + h_free[j % 2]
            hid_t[j][t] = turn_split(ust[:, j % 2, t, :], up_t[t], hhi[:, j % 2], hlo[:, j % 2], 0, t, 5 + t)
        u_free[j % 2] = [PE_last(PE)]
    ffn_down(u_dn, 7, residual(x2_t), hid_t[7], True,
             lambda t, n: lambda: turn2(t, n))

    r4_ = stat(2)

    def stats2():
        (r3, t_r3), w = x_stats(o3)
        ms, r3s = stat(2), stat(2)
        o4v = o4.rearrange("p (t n) -> p t n", n=2)
        w4 = [sq_t[4, t, n] for t in range(2) for n in range(2)]
        v = VE.put(lambda e: e.tensor_tensor(ms, o4v[:, :, 0], o4v[:, :, 1], ALU.add), w4)
        v2 = VE.put(lambda e: e.tensor_tensor(r3s, r3, r3, ALU.mult), t_r3)
        v = VE.put(lambda e: e.tensor_tensor(ms, ms, r3s, ALU.mult), v, v2)
        r4a, t_r4a = rsqrt(ms, 2, D, v)
        ST["t_r4"] = VE.put(lambda e: e.tensor_tensor(r4_, r3, r4a, ALU.mult), t_r4a)
        for t in range(2):
            x_w[t] = [VE.put(lambda e, t=t: e.tensor_scalar(xr[:, t, :], xr[:, t, :], r3[:, t:t + 1], None, ALU.mult),
                             t_r3, w4)]

    later.append(lambda: after.append(stats2))

    t_pad = GP.put(lambda e: e.memset(ch[:, :, 0:30], 0.0), t_gfree)
    glu_t = {}
    c_t = {}

    def evac_u(c):
        def fn(t, bk, tk, n):
            o = (ys[:, t, 0:512], ys[:, t, 512:1024])[c]
            v = AC.put(lambda e: e.mul(o, bank[bk], r4_[:, t:t + 1]), tk, ST["t_r4"])
            free[bk] = [v]
            glu_t[c, t] = v
            active.insert(0, sig_task(t) if c == 1 else glu_task(t))
            if c == 0 and t == 1:
                active.insert(0, conv_task())
        return fn

    cols = {}

    def turn_u(c, t, bk, w):
        for k in range(4):
            tk = tr(bank[bk][:, 128 * k:128 * k + 128], ys[:, t, 512 * c + 128 * k:512 * c + 128 * k + 128], w,
                    sig=(k == 3))
            w = []
        cols[c, t] = tk
        return tk

    def sig_task(t):
        bk, w = yield from take_one(5, 6)
        tk = turn_u(1, t, bk, [glu_t[1, t], w])
        yield
        sg = ca[:, :, 128 * t:128 * t + 128]
        for k in range(4):
            a = AC.put(lambda e, k=k: e.activation(sg[:, k, :], bank[bk][:, 128 * k:128 * k + 128],
                                                   ACT.Sigmoid, bias=pcol("glu_b", 4 + k)), tk)
        rel(free, bk, [a])
        sg_tok[t] = a

    sg_tok = {}
    gl_tok = {}

    def glu_task(t):
        bk, w = yield from take_one(5, 6)
        tk = turn_u(0, t, bk, [glu_t[0, t], w])
        yield
        while t not in sg_tok:
            yield
        for k in range(4):
            v = VE.put(lambda e, k=k: e.scalar_tensor_tensor(
                out=ch[:, k, 30 + 128 * t:158 + 128 * t], in0=bank[bk][:, 128 * k:128 * k + 128],
                scalar=pcol("glu_b", k), in1=ca[:, k, 128 * t:128 * t + 128], op0=ALU.add, op1=ALU.mult),
                tk, sg_tok[t])
        rel(free, bk, [v])
        gl_tok[t] = v

    def conv_task():
        while len(gl_tok) < 2:
            yield
        t_gl = [gl_tok[0], gl_tok[1], t_pad]
        prev = [t_gl] * 4
        cv_free = [None] * 5
        dg_free = [None] * 6
        part = cv[:, 5, :]
        t_part = None
        apart = [j for j in range(31) if j % 3 == 2 or j >= 27]
        on_pe = [(3, j) for j in range(31)] + [(2, j) for j in apart]
        wb = yield from take(7)
        i = 0
        jt = 0
        for j in range(31):
            src = [ch[:, k, j:j + 256] for k in range(3)]
            wc = [pcol("dw_w", 31 * k + j) for k in range(3)]
            if j == 0:
                prev[0] = VE.put(lambda e, w=wc[0], x=src[0]: e.tensor_scalar(ca[:, 0, :], x, w, pcol("dw_b", 0),
                                                                              ALU.mult, ALU.add), t_gl)
            else:
                prev[0] = VE.put(lambda e, w=wc[0], x=src[0]: e.scalar_tensor_tensor(
                    out=ca[:, 0, :], in0=x, scalar=w, in1=ca[:, 0, :], op0=ALU.mult, op1=ALU.add), prev[0])
            if j == 2:
                t_part = VE.put(lambda e, w=wc[1], x=src[1]: e.tensor_scalar(part, x, w, None, ALU.mult), t_gl)
            elif j in apart:
                t_part = VE.put(lambda e, w=wc[1], x=src[1]: e.scalar_tensor_tensor(
                    out=part, in0=x, scalar=w, in1=part, op0=ALU.mult, op1=ALU.add), t_part)
            for k in (1, 2):
                if j == 0:
                    prev[k] = AC.put(lambda e, k=k, w=wc[k], x=src[k]: e.activation(
                        ca[:, k, :], x, ACT.Identity, bias=pcol("dw_b", k), scale=w), t_gl)
                elif j not in apart:
                    a = AC.put(lambda e, i=i, w=wc[k], x=src[k]: e.mul(cv[:, i, :], x, w), cv_free[i], t_gl)
                    prev[k] = GP.put(lambda e, i=i, k=k: e.tensor_tensor(ca[:, k, :], ca[:, k, :], cv[:, i, :],
                                                                         ALU.add), a, prev[k])
                    cv_free[i] = prev[k]
                    i = (i + 1) % 5
            for k, jj in on_pe[jt:jt + 2]:
                if jt < len(diag):
                    tap, v = diag[jt], t_gl
                else:
                    q = (jt - len(diag)) % 6
                    tap = dg[:, q, :]
                    v = VE.put(lambda e, tap=tap, w=pcol("dw_w", 31 * k + jj): e.tensor_scalar(
                        tap, ident, w, None, ALU.mult), dg_free[q], t_gl)
                o = bank[7][:, 0:256] if k == 3 else bank[7][:, 256:512]
                tk = mm(o, tap, ch[:, k, jj:jj + 256], (k, jj) in ((3, 0), (2, 2)), jj == 30, v,
                        wb, diag_t)
                if jt < len(diag):
                    if jt < 8:
                        diag_u[1] = tk
                    if jt >= len(diag) - 6:
                        dg_free[jt - len(diag) + 6] = tk
                else:
                    dg_free[q] = tk
                jt += 1
                if jt == len(on_pe):
                    prev[3] = AC.put(lambda e: e.activation(ca[:, 3, :], bank[7][:, 0:256], ACT.Identity,
                                                            bias=pcol("dw_b", 3)), tk)
                    t_sum2 = AC.put(lambda e: e.copy(ch[:, 3, 0:256], bank[7][:, 256:512]), tk)
                    rel(free, 7, [prev[3], t_sum2])
            if j % 2 == 1:
                yield
        prev[1] = VE.put(lambda e: e.tensor_tensor(ca[:, 1, :], ca[:, 1, :], part, ALU.add), prev[1], t_part)
        prev[2] = VE.put(lambda e: e.tensor_tensor(ca[:, 2, :], ca[:, 2, :], ch[:, 3, 0:256], ALU.add), prev[2], t_sum2)
        for t in range(2):
            active.append(ln_task(t, list(prev)))

    def ln_task(t, prev):
        bk, w = yield from take_one(1, 0)
        w = [prev, w]
        for k in range(4):
            tk = tr(bank[bk][:, 128 * k:128 * k + 128], ca[:, k, 128 * t:128 * t + 128], w, sig=(k == 3))
            w = []
        yield
        bs = stat(6)
        mv = stat(2)
        v = VE.put(lambda e: e.bn_stats(bs, bank[bk]), tk)
        v = VE.put(lambda e: e.bn_aggr(mv, bs), v)
        r, tp = rsqrt(mv[:, 1:2], 1, 1, v)
        yield
        cn = ys[:, t, 512:1024]
        v = VE.put(lambda e: e.tensor_scalar(cn, bank[bk], mv[:, 0:1], r, ALU.subtract, ALU.mult), tp, v)
        for k in range(4):
            tk = tr(bank[bk][:, 128 * k:128 * k + 128], cn[:, 128 * k:128 * k + 128], v, sig=(k == 3))
        yield
        while (0, 0) not in Y_t or (1, 0) not in Y_t:
            yield
        sl = ch[:, :, 128 * t:128 * t + 128]
        for k in range(4):
            a = AC.put(lambda e, k=k: e.activation(sl[:, k, :], bank[bk][:, 128 * k:128 * k + 128], ACT.Silu,
                                                   bias=pcol("ln_b", k), scale=pcol("ln_g", k)), tk)
        rel(free, bk, [a])
        hi_ = Bhi[:, 4:8, 128 * t:128 * t + 128]
        lo_2 = Blo[:, 4:8, 128 * t:128 * t + 128]
        a = AC.put(lambda e: e.copy(hi_, sl), a)
        v = VE.put(lambda e: e.tensor_tensor(lo_2, sl, hi_.bitcast(F32), ALU.subtract), a)
        Y_t[t, 1] = [a, v]

    Y_t = {}
    q2_t = {}
    V2_t = {}
    qs = {}
    u2f = [[], []]

    def evac_q(qk):
        def fn(t, bk, tk, n):
            o = ust[:, 0, t, :]
            v = AC.put(lambda e: e.mul(o, bank[bk], r4_[:, t:t + 1]), tk, ST["t_r4"], u_free[0], u2f[t])
            free[bk] = [v]
            pending.insert(0, rope_task(qk, t, o, v))
            if qk == 1 and t == 1:
                pending.extend(att2_task(h) for h in range(8))
                for t_ in range(2):
                    active.append(turn_task(ys[:, t_, 0:512], [(4, h) for h in range(8)], Bhi, Blo, 0, t_, Y_t))
        return fn

    tmp_f = [[], []]

    def rope_task(qk, t, o, t_in):
        o3 = o.rearrange("p (h d) -> p h d", h=8)
        ti, wt = yield from slot(tmp_f)
        rt = (PT2, S2)[ti].rearrange("p a b -> p (a b)")
        w1, w2 = rt[:, 0:512], rt[:, 512:1024]
        w13 = w1.rearrange("p (h d) -> p h d", h=8)
        w23 = w2.rearrange("p (h d) -> p h d", h=8)
        s8 = stat(8)
        v = AC.put(lambda e: e.activation(w1, o, ACT.Square), t_in, wt, t_gfree)
        v = VE.put(lambda e: e.tensor_reduce(s8, w13, AX.X, ALU.add), v)
        r, tp = rsqrt(s8, 8, 64, v)
        yield
        yield
        v = VE.put(lambda e: e.tensor_tensor(o3, o3, r.unsqueeze(2).broadcast_to([128, 8, 64]), ALU.mult), tp)
        of = (qk * 2 + t) * 64
        cA = RT[:, of:of + 64].unsqueeze(1).broadcast_to([128, 8, 64])
        sA = RT2[:, of:of + 32].unsqueeze(1).broadcast_to([128, 8, 32])
        sB = RT2[:, of + 32:of + 64].unsqueeze(1).broadcast_to([128, 8, 32])
        va = VE.put(lambda e: e.tensor_tensor(w13, o3, cA, ALU.mult), v, t_rt)
        VE.put(lambda e: e.tensor_tensor(w23[:, :, 0:32], o3[:, :, 32:64], sA, ALU.mult), v)
        vb = VE.put(lambda e: e.tensor_tensor(w23[:, :, 32:64], o3[:, :, 0:32], sB, ALU.mult), v)
        v = GP.put(lambda e: e.tensor_tensor(w1, w1, w2, ALU.add), va, vb)
        u2f[t] = [v]
        yield
        yield
        w = yield from take(5)
        w = [v, w]
        for k in range(4):
            tk = tr(bank[5][:, 128 * k:128 * k + 128], w1[:, 128 * k:128 * k + 128], w, sig=(k == 3))
            w = []
        rel(tmp_f, ti, [tk])
        dst = qk2T[:, 4 * qk:4 * qk + 4, 128 * t:128 * t + 128]
        a = AC.put(lambda e: e.mul(dst, bank[5].rearrange("p (k q) -> p k q", k=4), 0.125 if qk == 0 else 1.0), tk,
                   t_gfree)
        rel(free, 5, [a])
        q2_t[qk, t] = a

    def evac_v2(t, bk, tk, n):
        v = AC.put(lambda e: e.mul(V2[:, t, :], bank[bk], r4_[:, t:t + 1]), tk, ST["t_r4"], diag_u[1])
        free[bk] = [v]
        V2_t[t] = v

    S2_free = [[], [], []]

    def att2_task(h):
        while len(q2_t) < 4:
            yield
        bk, wb = yield from take_one(3, 4)
        Z = bank[bk]
        p = 64 * (h % 2)
        q, k = qk2T[p:p + 64, h // 2, :], qk2T[p:p + 64, 4 + h // 2, :]
        mm(Z[:, 0:128], q[:, 0:128], k[:, 0:128], True, True, wb, [q2_t[a, b_] for a in range(2) for b_ in range(2)],
           sig=False)
        tk = mm(Z[:, 128:384], q[:, 128:256], k, True, True)
        yield
        si, ws = yield from slot(S2_free)
        P = S2[:, si, :]
        Zd = Z.rearrange("p (a b) -> p a b", a=2)[:, :, 0:128]
        t = VE.put(lambda e: e.tensor_tensor(Zd, Zd, maskF[:, 128:256].unsqueeze(1).broadcast_to([128, 2, 128]),
                                             ALU.add), tk)
        i = cnt["S"] % 8
        cnt["S"] += 1
        nm, l = stat_m[i], stat_s[i]
        VE.put(lambda e: e.tensor_reduce(nm[:, 0:1], Z[:, 0:128], AX.X, ALU.max, negate=True), t)
        t = VE.put(lambda e: e.tensor_reduce(nm[:, 1:2], Z[:, 128:384], AX.X, ALU.max, negate=True), t)
        AC.put(lambda e: e.activation(P[:, 0:128], Z[:, 0:128], ACT.Exp, bias=nm[:, 0:1], accum_out=l[:, 0:1]), t, ws)
        te = AC.put(lambda e: e.activation(P[:, 128:384], Z[:, 128:384], ACT.Exp, bias=nm[:, 1:2],
                                           accum_out=l[:, 1:2]))
        rel(free, bk, [te])
        yield
        bk, wb = yield from take_one(5, 6)
        w = [te, wb]
        for j in range(3):
            tk = tr(bank[bk][:, 128 * j:128 * j + 128], P[:, 128 * j:128 * j + 128], w, sig=(j == 2))
            w = []
        rel(S2_free, si, [tk])
        trl = VE.put(lambda e: e.reciprocal(l, l), te)
        yield
        pi, wp = yield from slot(PT_free)
        ta = AC.put(lambda e: e.copy(PT2[:, pi, 0:384], bank[bk][:, 0:384]), tk, wp)
        rel(free, bk, [ta])
        yield
        while len(V2_t) < 2:
            yield
        ob, wo = yield from take_one(2, 7)
        mm(bank[ob][:, 0:64], PT2[:, pi, 0:128], V2[:, 0, 64 * h:64 * h + 64], True, True, ta, wo, V2_t[0], V2_t[1],
           sig=False)
        mm(bank[ob][:, 64:128], PT2[:, pi, 128:256], V2[:, 0, 64 * h:64 * h + 64], True, False, sig=False)
        tk = mm(bank[ob][:, 64:128], PT2[:, pi, 256:384], V2[:, 1, 64 * h:64 * h + 64], False, True)
        rel(PT_free, pi, [tk])
        yield
        o = bank[ob][:, 0:128].rearrange("p (a d) -> p a d", a=2)
        ys_t[4, h] = VE.put(lambda e: e.tensor_tensor(ys[:, :, 64 * h:64 * h + 64], o,
                                                      l.unsqueeze(2).broadcast_to([128, 2, 64]), ALU.mult),
                            tk, trl, cols[0, 0], cols[0, 1])
        rel(free, ob, [ys_t[4, h]])

    PT_free[0] = []
    PT_free[1] = []
    for i, us in enumerate(u_p2):
        ev2 = [evac_u(1), evac_q(0), evac_q(1), evac_u(0), evac_v2][i]
        chunk(us, Ahi, Alo, H2_t, ev2, first_of_phase=(i == 0), start=2)
    late()

    x3_t, H3_t = {}, {}
    ys_free[:] = []
    out_proj(u_wo2, Bhi, Blo, Y_t, lambda: None, x3_t, norm_turn(x3_t, Ahi, Alo, lambda k: pcol("g_n2", k, 4), H3_t, o5))

    def stats3():
        (ST["r5"], ST["t_r5"]), ta = x_stats(o5)
        ST["ta5"] = ta
        x_w[0], x_w[1] = ta, ta

    later.append(lambda: after.append(stats3))

    out_t = {}
    res = residual(out_t)
    o_v = out_d.rearrange("(t p) d -> p t d", p=128)
    nout = [0]

    def final(t, n, tk):
        res(t, n, tk)
        dma(o_v[:, t, 512 * n:512 * n + 512], xr[:, t, 512 * n:512 * n + 512], d_out, out_t[t, n])
        nout[0] += 16

    hid2 = {}
    gl = ys
    gl_free = {0: PE_last(PE), 1: PE_last(PE)}
    for j in range(6):
        n_ = HC2[j] * 128
        sg_t = {}
        m_t = {}

        def ev_g(t, bk, tk, n):
            r = ST["r5"]
            a = AC.put(lambda e: e.activation(gl[:, t, 0:n], bank[bk][:, 0:n], ACT.Silu, scale=r[:, t:t + 1]),
                       tk, ST["t_r5"], gl_free[t], ST["ta5"])
            free[bk] = [a]
            sg_t[t] = a

        def ev_u(t, bk, tk, n, j=j):
            o = ust[:, j % 2, t, 0:n]
            r = ST["r5"]
            v = VE.put(lambda e: e.scalar_tensor_tensor(out=o, in0=bank[bk][:, 0:n], scalar=r[:, t:t + 1],
                                                        in1=gl[:, t, 0:n], op0=ALU.mult, op1=ALU.mult),
                       tk, sg_t[t], ST["t_r5"], u_free[j % 2])
            free[bk] = [v]
            gl_free[t] = v
            m_t[t] = v

        up_product(u_g2[j], Ahi, Alo, H3_t, j == 0, ev_g)
        up_product(u_u2[j], Ahi, Alo, H3_t, False, ev_u)
        if j:
            ffn_down(u_d2, j - 1, None, hid2[j - 1], False)
        late()
        hid2[j] = {}
        for t in range(2):
            free[5 + t] = free[5 + t] + h_free[j % 2]
            hid2[j][t] = turn_split(ust[:, j % 2, t, 0:n_], m_t[t], hhi[:, j % 2], hlo[:, j % 2], 0, t, 5 + t,
                                    nk=HC2[j])
        u_free[j % 2] = [PE_last(PE)]
    ffn_down(u_d2, 5, final, hid2[5], True)

    block = ctx.enter_context(nc.Block())

    @block.sync
    def _(e):
        SP.play(e)
        e.wait_ge(d_out, nout[0])

    @block.tensor
    def _(e):
        PE.play(e)

    @block.scalar
    def _(e):
        AC.play(e)

    @block.vector
    def _(e):
        VE.play(e)

    @block.gpsimd
    def _(e):
        GP.play(e)


def PE_last(q):
    return (q.sem, q.n)


def _constants():
    import numpy as np

    q = np.arange(128)
    ident = np.eye(128, dtype=np.float32)
    tri = np.where(q[None, :] <= q[:, None], 0.0, NEG).astype(np.float32)
    maskF = np.concatenate([np.zeros((128, 128), np.float32), tri], axis=1)
    DDs = []
    for window, dil in ((128, 1), (512, 4), (2048, 16), (10 ** 9, 1)):
        blocks = []
        for qo, ko in ((0, 0), (128, 0), (128, 128)):
            dist = (q[:, None] + qo) - (q[None, :] + ko)
            ok = (dist >= 0) & (dist % dil == 0) & (dist <= window)
            blocks.append(np.where(ok, dist, 1e30).astype(np.float32))
        DDs.append(np.concatenate(blocks, axis=1))
    kk, qq = q[:, None], q[None, :]
    strict = np.where(kk < qq, 0.0, NEG).astype(np.float32)
    MB = np.concatenate([strict, np.zeros((128, 128), np.float32), strict], axis=1)
    UO = np.concatenate([(kk <= qq).astype(np.float32), np.ones((128, 128), np.float32)], axis=1)
    LG = (kk >= qq).astype(np.float32)
    return np.ascontiguousarray(np.concatenate([ident, maskF] + DDs + [MB, UO, LG], axis=1), dtype=np.float32)


def _rope():
    import numpy as np

    pos = np.arange(256, dtype=np.float32)
    inv = np.power(np.float32(10000.0), -np.arange(0, 64, 2, dtype=np.float32) / np.float32(64)).astype(np.float32)
    ang = (pos[:, None] * inv[None, :]).astype(np.float32)
    cos, sin = np.cos(ang).astype(np.float32), np.sin(ang).astype(np.float32)
    c = np.concatenate([cos, cos], axis=1)
    s = np.concatenate([-sin, sin], axis=1)
    lay = lambda a: a.reshape(2, 128, 64).transpose(1, 0, 2).reshape(128, 128)
    return lay(c), lay(s)


def kernel(**inputs):
    import numpy as np
    import concourse.bacc as bacc
    from concourse.bass_utils import run_bass_kernel_spmd

    a = {k: np.asarray(v) for k, v in inputs.items()}
    col = lambda v, n: v.reshape(n, 128).T
    row = lambda v: np.broadcast_to(v.reshape(1, -1), (128, v.size))
    dw = a["dw_w_2"][0].reshape(31, 4, 128).transpose(2, 1, 0).reshape(128, 124)
    par = np.concatenate([
        col(a["mix_norm_g"], 8), col(a["mlp_norm_g"], 8), col(a["final_norm_g"], 8), col(a["norm1_g_2"], 8),
        col(a["norm2_g_2"], 8), col(a["glu_b_2"], 8), dw, col(a["dw_b_2"], 4), col(a["conv_ln_g_2"], 4),
        col(a["conv_ln_b_2"], 4), row(a["b_forget"]), row(a["lambda_q1"]), row(a["lambda_q2"]),
        row(a["lambda_k1"]), row(a["lambda_k2"]), row(a["diff_norm_g"])], axis=1)
    cosT, sinT = _rope()
    par2 = np.concatenate([row(a["final_norm_g"]), row(a["q_norm_g_2"]), row(a["k_norm_g_2"]), cosT, sinT], axis=1)
    arrays = {
        "x": a["x"][0], "w_in": a["w_in"][0], "w_br": a["w_branch"][0].reshape(1024, 1024), "w_out": a["w_out"][0],
        "w_up": a["w_up"][0], "w_dn": a["w_down"][0], "w_in2": a["w_in_2"][0], "w_out2": a["w_out_2"][0],
        "w_g2": a["w_gate_2"][0], "w_u2": a["w_up_2"][0], "w_d2": a["w_down_2"][0],
        "par": par, "par2": par2, "cst": _constants(),
    }
    nc = bacc.Bacc("TRN2", target_bir_lowering=False, num_devices=1)
    args, ins = [], {}
    for name, v in arrays.items():
        v = np.ascontiguousarray(v)
        ins["in_" + name] = v
        args.append(nc.dram_tensor("in_" + name, v.shape, mybir.dt.from_np(v.dtype), kind="ExternalInput").ap())
    args.append(nc.dram_tensor("out_0", (S, D), F32, kind="ExternalOutput").ap())
    program(nc, *args)
    r = run_bass_kernel_spmd(nc, [ins], core_ids=[0])
    return r.results[0]["out_0"].reshape(1, S, D)
```
